# Optimizing a Trainium2 kernel written in Bass

```python
import jax, jax.numpy as jnp
from jax import lax
import numpy as np

D_MODEL = 1024
BATCH = 1
SEQ = 512
DEPTH = 1

GRID_W = 64
CTX_LEN = 256
D_MIX = D_MODEL
SSD_WIDTH = D_MIX // 2
SSD_HEADDIM = 64
SSD_HEADS = SSD_WIDTH // SSD_HEADDIM
SSD_GROUPS = 2
HEADS_PER_GROUP = SSD_HEADS // SSD_GROUPS
SSD_STATE = 128
SSD_CONV = 3
SSD_CHUNK = 128
XBC_WIDTH = SSD_WIDTH + 2 * SSD_GROUPS * SSD_STATE
FNET_WIDTH = D_MIX // 4
FNET_GROUPS = 4
FNET_GDIM = FNET_WIDTH // FNET_GROUPS
POOL_WINDOWS = (2, 4, 8, 16)
POOL_WIDTH = D_MIX // 4
POOL_GDIM = POOL_WIDTH // len(POOL_WINDOWS)
D_FF = 256 * ((8 * D_MODEL // 3 + 255) // 256)
FFN_CONV = 3
OFF_Z = 0
OFF_XBC = OFF_Z + SSD_WIDTH
OFF_DT = OFF_XBC + XBC_WIDTH
OFF_FNET = OFF_DT + 2 * SSD_HEADS
OFF_POOL = OFF_FNET + FNET_WIDTH
N_IN = OFF_POOL + POOL_WIDTH
ALPHA = (2.0 * DEPTH) ** 0.25
BETA = (8.0 * DEPTH) ** -0.25
EPS = 1e-6


def layer_norm(x):
    xf = x.astype(jnp.float32)
    mu = jnp.mean(xf, -1, keepdims=True)
    var = jnp.mean(jnp.square(xf - mu), -1, keepdims=True)
    return ((xf - mu) * lax.rsqrt(var + EPS)).astype(x.dtype)

def ada(cvec, w, b):
    m = jax.nn.silu(cvec) @ w + b
    return [mi[:, None, :] for mi in jnp.split(m, 6, axis=-1)]

def modulate(x, shift, scale):
    return layer_norm(x) * (1 + scale) + shift

def post_norm(x, y, gate, g, b):
    return layer_norm(ALPHA * x + gate * y) * g + b

def dwconv1d(x, w, b):
    k = w.shape[0]
    left = (k - 1) // 2
    y = lax.conv_general_dilated(x, w[:, None, :], window_strides=(1,), padding=[(left, k - 1 - left)],
                                 dimension_numbers=("NWC", "WIO", "NWC"), feature_group_count=x.shape[-1])
    return y + b

def dwconv2d_grid(x, w, b):
    bsz, L, C = x.shape
    rows = L // GRID_W
    xg = x.reshape(bsz, rows, GRID_W, C)
    y = lax.conv_general_dilated(xg, w[:, :, None, :], window_strides=(1, 1), padding=[(1, 1), (1, 1)],
                                 dimension_numbers=("NHWC", "HWIO", "NHWC"), feature_group_count=C)
    return y.reshape(bsz, L, C) + b

def segsum(a):
    T = a.shape[-1]
    cs = jnp.cumsum(a, axis=-1)
    seg = cs[..., :, None] - cs[..., None, :]
    mask = jnp.tril(jnp.ones((T, T), dtype=bool))
    return jnp.where(mask, seg, -jnp.inf)

def ssd_chunked(X, dA, B, C, init_state):
    b, L, h, p = X.shape
    n = B.shape[-1]
    nc = L // SSD_CHUNK
    X = X.astype(jnp.float32).reshape(b, nc, SSD_CHUNK, h, p)
    B = B.astype(jnp.float32).reshape(b, nc, SSD_CHUNK, h, n)
    C = C.astype(jnp.float32).reshape(b, nc, SSD_CHUNK, h, n)
    A = dA.astype(jnp.float32).reshape(b, nc, SSD_CHUNK, h).transpose(0, 3, 1, 2)
    A_cs = jnp.cumsum(A, axis=-1)
    Lmat = jnp.exp(segsum(A))
    y_diag = jnp.einsum("bclhn,bcshn,bhcls,bcshp->bclhp", C, B, Lmat, X)
    decay_states = jnp.exp(A_cs[..., -1:] - A_cs)
    states = jnp.einsum("bclhn,bhcl,bclhp->bchpn", B, decay_states, X)
    states = jnp.concatenate([init_state[:, None].astype(jnp.float32), states], axis=1)
    chunk_decay = jnp.exp(segsum(jnp.pad(A_cs[..., -1], ((0, 0), (0, 0), (1, 0)))))
    new_states = jnp.einsum("bhzc,bchpn->bzhpn", chunk_decay, states)
    states, final_state = new_states[:, :-1], new_states[:, -1]
    y_off = jnp.einsum("bclhn,bchpn,bhcl->bclhp", C, states, jnp.exp(A_cs))
    return (y_diag + y_off).reshape(b, L, h, p), final_state

def ssd_final_state(X, dA, B):
    cs = jnp.cumsum(dA, axis=1)
    return jnp.einsum("blh,blhn,blhp->bhpn", jnp.exp(cs[:, -1:] - cs), B.astype(jnp.float32), X)

def rev(a):
    return jnp.flip(a, axis=1)

def ssd_prep(u, conv_w, conv_b, dt_bias, a_log):
    bsz, L, _ = u.shape
    xbc = jax.nn.silu(dwconv1d(u[..., OFF_XBC:OFF_DT], conv_w, conv_b))
    xs = xbc[..., :SSD_WIDTH].reshape(bsz, L, SSD_HEADS, SSD_HEADDIM)
    gn = SSD_GROUPS * SSD_STATE
    bm = xbc[..., SSD_WIDTH:SSD_WIDTH + gn].reshape(bsz, L, SSD_GROUPS, SSD_STATE)
    cm = xbc[..., SSD_WIDTH + gn:].reshape(bsz, L, SSD_GROUPS, SSD_STATE)
    bm = jnp.repeat(bm, HEADS_PER_GROUP, axis=2)
    cm = jnp.repeat(cm, HEADS_PER_GROUP, axis=2)
    dt_raw = u[..., OFF_DT:OFF_FNET].reshape(bsz, L, 2, SSD_HEADS)
    dt = jax.nn.softplus((dt_raw + dt_bias).astype(jnp.float32))
    dA = dt * (-jnp.exp(a_log.astype(jnp.float32)))
    return xs, bm, cm, dt, dA

def ssd_bidir(xs, bm, cm, dt, dA, init_f, init_b):
    x32 = xs.astype(jnp.float32)
    y_f, s_f = ssd_chunked(x32 * dt[:, :, 0, :, None], dA[:, :, 0], bm, cm, init_f)
    y_b, s_b = ssd_chunked(rev(x32 * dt[:, :, 1, :, None]), rev(dA[:, :, 1]), rev(bm), rev(cm), init_b)
    return y_f + rev(y_b), s_f, s_b

def ssd_gate_norm(y, xs, z, d_skip, norm_w):
    bsz, L = z.shape[:2]
    y = (y + xs.astype(jnp.float32) * d_skip.astype(jnp.float32)[:, None]).reshape(bsz, L, SSD_WIDTH)
    y = (y * jax.nn.silu(z.astype(jnp.float32))).reshape(bsz, L, SSD_GROUPS, SSD_WIDTH // SSD_GROUPS)
    y = (y * lax.rsqrt(jnp.mean(y * y, -1, keepdims=True) + EPS)).reshape(bsz, L, SSD_WIDTH)
    return (y * norm_w).astype(z.dtype)

def fourier_mix(f, w):
    bsz, L, _ = f.shape
    fg = f.astype(jnp.float32).reshape(bsz, L, FNET_GROUPS, FNET_GDIM)
    spec = jnp.fft.fft2(fg, axes=(1, 3), norm="ortho").real
    y = jnp.einsum("blgc,gcd->blgd", spec.astype(f.dtype), w)
    return y.reshape(bsz, L, FNET_WIDTH)

def pool_mix(p, w, scale):
    bsz, L, _ = p.shape
    pf = p.astype(jnp.float32)
    cs = jnp.pad(jnp.cumsum(pf, axis=1), ((0, 0), (1, 0), (0, 0)))
    pos = jnp.arange(L)
    outs = []
    for gi, win in enumerate(POOL_WINDOWS):
        left = win // 2
        right = win - 1 - left
        hi = jnp.minimum(pos + right + 1, L)
        lo = jnp.maximum(pos - left, 0)
        sl = slice(gi * POOL_GDIM, (gi + 1) * POOL_GDIM)
        csg = cs[..., sl]
        mean = (csg[:, hi] - csg[:, lo]) / (hi - lo).astype(jnp.float32)[None, :, None]
        outs.append(mean - pf[..., sl])
    pooled = jnp.stack(outs, axis=2).astype(p.dtype)
    y = jnp.einsum("blgc,gcd->blgd", pooled, w).reshape(bsz, L, POOL_WIDTH)
    return y * scale

def token_mixer(u, init_f, init_b, conv_w, conv_b, dt_bias, a_log, d_skip, norm_w, fnet_w, pool_w, pool_scale, w_out):
    xs, bm, cm, dt, dA = ssd_prep(u, conv_w, conv_b, dt_bias, a_log)
    y, s_f, s_b = ssd_bidir(xs, bm, cm, dt, dA, init_f, init_b)
    y_ssd = ssd_gate_norm(y, xs, u[..., OFF_Z:OFF_XBC], d_skip, norm_w)
    y_fnet = fourier_mix(u[..., OFF_FNET:OFF_POOL], fnet_w)
    y_pool = pool_mix(u[..., OFF_POOL:N_IN], pool_w, pool_scale)
    return jnp.concatenate([y_ssd, y_fnet, y_pool], axis=-1) @ w_out, s_f, s_b

def ctx_scan_states(u, conv_w, conv_b, dt_bias, a_log):
    xs, bm, _, dt, dA = ssd_prep(u, conv_w, conv_b, dt_bias, a_log)
    x32 = xs.astype(jnp.float32)
    s_f = ssd_final_state(x32 * dt[:, :, 0, :, None], dA[:, :, 0], bm)
    s_b = ssd_final_state(rev(x32 * dt[:, :, 1, :, None]), rev(dA[:, :, 1]), rev(bm))
    return s_f, s_b

def conv_ffn(h, w_up, conv_w, conv_b, w_down, grid):
    a = h @ w_up
    a = dwconv2d_grid(a, conv_w, conv_b) if grid else dwconv1d(a, conv_w[1], conv_b)
    val, gate = jnp.split(a, 2, axis=-1)
    return (jax.nn.gelu(gate) * val) @ w_down

def first_inputs(seed: int = 0) -> dict:
    key = jax.random.key(seed)
    ks = jax.random.split(key, 25)
    f32 = jnp.float32

    def nrm(k, shape, s):
        return s * jax.random.normal(k, shape, f32)

    dt0 = jnp.exp(jax.random.uniform(ks[9], (DEPTH, 2, SSD_HEADS), f32, np.log(1e-3), np.log(1e-1)))
    return {
        "x": nrm(ks[0], (BATCH, SEQ, D_MODEL), 1.0),
        "c": nrm(ks[1], (BATCH, D_MODEL), 1.0),
        "ctx": nrm(ks[2], (BATCH, CTX_LEN, D_MODEL), 1.0),
        "c_ctx": nrm(ks[3], (D_MODEL,), 1.0),
        "w_ada": nrm(ks[4], (DEPTH, D_MODEL, 6 * D_MODEL), 0.5 * D_MODEL ** -0.5),
        "b_ada": nrm(ks[5], (DEPTH, 6 * D_MODEL), 0.02),
        "w_in": nrm(ks[6], (DEPTH, D_MODEL, N_IN), D_MODEL ** -0.5),
        "ssd_conv_w": nrm(ks[7], (DEPTH, SSD_CONV, XBC_WIDTH), SSD_CONV ** -0.5),
        "ssd_conv_b": nrm(ks[8], (DEPTH, XBC_WIDTH), 0.02),
        "ssd_dt_bias": dt0 + jnp.log(-jnp.expm1(-dt0)),
        "ssd_a_log": jnp.log(jax.random.uniform(ks[10], (DEPTH, 2, SSD_HEADS), f32, 1.0, 16.0)),
        "ssd_d": 1.0 + nrm(ks[11], (DEPTH, SSD_HEADS), 0.1),
        "ssd_norm_w": 1.0 + nrm(ks[12], (DEPTH, SSD_WIDTH), 0.1),
        "fnet_w": nrm(ks[13], (DEPTH, FNET_GROUPS, FNET_GDIM, FNET_GDIM), FNET_GDIM ** -0.5),
        "pool_w": nrm(ks[14], (DEPTH, len(POOL_WINDOWS), POOL_GDIM, POOL_GDIM), POOL_GDIM ** -0.5),
        "pool_scale": 1.0 + nrm(ks[15], (DEPTH, POOL_WIDTH), 0.1),
        "w_out": nrm(ks[16], (DEPTH, D_MIX, D_MODEL), BETA * D_MIX ** -0.5),
        "ln1_g": 1.0 + nrm(ks[17], (DEPTH, D_MODEL), 0.1),
        "ln1_b": nrm(ks[18], (DEPTH, D_MODEL), 0.02),
        "ffn_w_up": nrm(ks[19], (DEPTH, D_MODEL, 2 * D_FF), D_MODEL ** -0.5),
        "ffn_conv_w": nrm(ks[20], (DEPTH, FFN_CONV, FFN_CONV, 2 * D_FF), 1.0 / FFN_CONV),
        "ffn_conv_b": nrm(ks[21], (DEPTH, 2 * D_FF), 0.02),
        "ffn_w_down": nrm(ks[22], (DEPTH, D_FF, D_MODEL), BETA * D_FF ** -0.5),
        "ln2_g": 1.0 + nrm(ks[23], (DEPTH, D_MODEL), 0.1),
        "ln2_b": nrm(ks[24], (DEPTH, D_MODEL), 0.02),
    }

def first_block(x, c, ctx, c_ctx, w_ada, b_ada, w_in, ssd_conv_w, ssd_conv_b, ssd_dt_bias, ssd_a_log, ssd_d,
              ssd_norm_w, fnet_w, pool_w, pool_scale, w_out, ln1_g, ln1_b, ffn_w_up, ffn_conv_w, ffn_conv_b,
              ffn_w_down, ln2_g, ln2_b):
    bsz = x.shape[0]
    zero_state = jnp.zeros((bsz, SSD_HEADS, SSD_HEADDIM, SSD_STATE), jnp.float32)
    for l in range(DEPTH):
        last = l == DEPTH - 1
        sh1, sc1, g1, sh2, sc2, g2 = ada(c, w_ada[l], b_ada[l])
        csh1, csc1, cg1, csh2, csc2, cg2 = ada(c_ctx[None, :], w_ada[l], b_ada[l])
        mixer_p = (ssd_conv_w[l], ssd_conv_b[l], ssd_dt_bias[l], ssd_a_log[l], ssd_d[l], ssd_norm_w[l],
                   fnet_w[l], pool_w[l], pool_scale[l], w_out[l])
        u_ctx = modulate(ctx, csh1, csc1) @ w_in[l]
        u_lat = modulate(x, sh1, sc1) @ w_in[l]
        if last:
            s_f, s_b = ctx_scan_states(u_ctx, ssd_conv_w[l], ssd_conv_b[l], ssd_dt_bias[l], ssd_a_log[l])
        else:
            mix_ctx, s_f, s_b = token_mixer(u_ctx, zero_state, zero_state, *mixer_p)
        mix_lat, _, _ = token_mixer(u_lat, s_f, s_b, *mixer_p)
        x = post_norm(x, mix_lat, g1, ln1_g[l], ln1_b[l])
        ffn_lat = conv_ffn(modulate(x, sh2, sc2), ffn_w_up[l], ffn_conv_w[l], ffn_conv_b[l], ffn_w_down[l], True)
        x = post_norm(x, ffn_lat, g2, ln2_g[l], ln2_b[l])
        if not last:
            ctx = post_norm(ctx, mix_ctx, cg1, ln1_g[l], ln1_b[l])
            ffn_ctx = conv_ffn(modulate(ctx, csh2, csc2), ffn_w_up[l], ffn_conv_w[l], ffn_conv_b[l], ffn_w_down[l], False)
            ctx = post_norm(ctx, ffn_ctx, cg2, ln2_g[l], ln2_b[l])
    return x


DEPTH_2 = 2

PLE_DIM = 256
ATT_HEADS = 8
ATT_KV_HEADS = 2
HEAD_DIM = 64
Q_RANK = 256
IDX_HEADS = 8
IDX_DIM = 64
TOPK_MAX = 256
Q_BLOCK = 128
ML_HEADS = 4
ML_DIM = 128
CONV_W = 4
CHUNK = 64
D_FF_2 = 4 * D_MODEL
ROPE_THETA = 500000.0
ROT_DIM = HEAD_DIM // 4

ATT_W = ATT_HEADS * HEAD_DIM
KV_W = ATT_KV_HEADS * HEAD_DIM
ML_W = ML_HEADS * ML_DIM
MIX_W = ATT_W + ML_W
IN_SIZES = (Q_RANK, KV_W, KV_W, IDX_DIM, IDX_HEADS, ML_W, ML_W, ML_W, ML_W, ML_HEADS, ML_HEADS)
IN_W = sum(IN_SIZES)
IDX_SCALE = (IDX_HEADS ** -0.5) * (IDX_DIM ** -0.5)


def rms_norm(x, g):
    xf = x.astype(jnp.float32)
    y = xf * lax.rsqrt(jnp.mean(xf * xf, axis=-1, keepdims=True) + EPS)
    return (y * g.astype(jnp.float32)).astype(x.dtype)

def rope_tables(positions):
    half = ROT_DIM // 2
    inv = ROPE_THETA ** (-(jnp.arange(half, dtype=jnp.float32) * 2.0) / ROT_DIM)
    ang = positions.astype(jnp.float32)[..., None] * inv
    return jnp.cos(ang), jnp.sin(ang)

def apply_partial_rope(x, cos, sin):
    half = ROT_DIM // 2
    c = cos[:, :, None, :].astype(x.dtype)
    s = sin[:, :, None, :].astype(x.dtype)
    x1 = x[..., :half]
    x2 = x[..., half:ROT_DIM]
    return jnp.concatenate([x1 * c - x2 * s, x2 * c + x1 * s, x[..., ROT_DIM:]], axis=-1)

def causal_dwconv(x, w, b):
    S = x.shape[1]
    xp = jnp.pad(x, ((0, 0), (CONV_W - 1, 0), (0, 0)))
    acc = xp[:, 0:S] * w[0]
    for j in range(1, CONV_W):
        acc = acc + xp[:, j:j + S] * w[j]
    return acc + b

def dsa_attention(q, k, v, q_idx, k_idx, w_idx):
    B, S, H, D = q.shape
    G = H // ATT_KV_HEADS
    n_sel = min(TOPK_MAX, S // 4)
    nb = S // Q_BLOCK
    key_pos = jnp.arange(S)
    scale = D ** -0.5

    def blk(a):
        return a.reshape(B, nb, Q_BLOCK, *a.shape[2:]).swapaxes(0, 1)

    def one_block(args):
        qb, qib, wb, qpos = args
        logits = jnp.einsum('bqhd,bsd->bqhs', qib, k_idx)
        score = jnp.einsum('bqh,bqhs->bqs', wb, jax.nn.relu(logits)).astype(jnp.float32)
        causal = key_pos[None, :] <= qpos[:, None]
        score = jnp.where(causal[None], score, -jnp.inf)
        _, sel = lax.top_k(score, n_sel)
        k_sel = jax.vmap(lambda kb, ib: kb[ib])(k, sel)
        v_sel = jax.vmap(lambda vb, ib: vb[ib])(v, sel)
        valid = sel <= qpos[None, :, None]
        qg = qb.reshape(B, Q_BLOCK, ATT_KV_HEADS, G, D)
        s = jnp.einsum('bqgrd,bqkgd->bqgrk', qg, k_sel).astype(jnp.float32) * scale
        s = jnp.where(valid[:, :, None, None, :], s, -jnp.inf)
        pr = jax.nn.softmax(s, axis=-1).astype(v.dtype)
        o = jnp.einsum('bqgrk,bqkgd->bqgrd', pr, v_sel)
        return o.reshape(B, Q_BLOCK, H, D)

    out = lax.map(one_block, (blk(q), blk(q_idx), blk(w_idx), key_pos.reshape(nb, Q_BLOCK)))
    return out.swapaxes(0, 1).reshape(B, S, H, D)

def mlstm_chunkwise(q, k, v, i_pre, f_pre):
    B, S, H, D = q.shape
    nc = S // CHUNK
    f32 = jnp.float32
    qf = q.astype(f32) * (D ** -0.5)
    kf = k.astype(f32)
    vf = v.astype(f32)
    log_f = jax.nn.log_sigmoid(f_pre.astype(f32))
    log_i = i_pre.astype(f32)

    def chunks(a):
        a = a.reshape(B, nc, CHUNK, H, *a.shape[3:])
        return jnp.moveaxis(a, (1, 3), (0, 2))

    tri = jnp.tril(jnp.ones((CHUNK, CHUNK), dtype=bool))

    def step(carry, xs):
        C, n, m = carry
        qc, kc, vc, lic, lfc = xs
        b = jnp.cumsum(lfc, axis=-1)
        log_d = b[..., :, None] - b[..., None, :] + lic[..., None, :]
        log_d = jnp.where(tri, log_d, -jnp.inf)
        inter = b + m[..., None]
        m_t = jnp.maximum(inter, jnp.max(log_d, axis=-1))
        dmat = jnp.exp(log_d - m_t[..., None])
        inter_w = jnp.exp(inter - m_t)
        qk = jnp.einsum('bhtd,bhsd->bhts', qc, kc) * dmat
        num = inter_w[..., None] * jnp.einsum('bhtd,bhde->bhte', qc, C) + jnp.einsum('bhts,bhse->bhte', qk, vc)
        den = inter_w * jnp.einsum('bhtd,bhd->bht', qc, n) + jnp.sum(qk, axis=-1)
        h = num / jnp.maximum(jnp.abs(den), jnp.exp(-m_t))[..., None]
        b_last = b[..., -1]
        log_g = b_last[..., None] - b + lic
        m_new = jnp.maximum(b_last + m, jnp.max(log_g, axis=-1))
        g = jnp.exp(log_g - m_new[..., None])
        decay = jnp.exp(b_last + m - m_new)
        C_new = decay[..., None, None] * C + jnp.einsum('bhs,bhsd,bhse->bhde', g, kc, vc)
        n_new = decay[..., None] * n + jnp.einsum('bhs,bhsd->bhd', g, kc)
        return (C_new, n_new, m_new), h

    init = (jnp.zeros((B, H, D, D), f32), jnp.zeros((B, H, D), f32), jnp.zeros((B, H), f32))
    _, hs = lax.scan(step, init, (chunks(qf), chunks(kf), chunks(vf), chunks(log_i), chunks(log_f)))
    hs = jnp.moveaxis(hs, (0, 2), (1, 3)).reshape(B, S, H, D)
    return hs.astype(q.dtype)

def hybrid_layer(h, p_i, cos, sin, g_mix, w_in, g_cq, w_q_up, w_iq_up, g_qn, g_kn, g_ik,
                 conv_w, conv_b, i_bias, f_bias, g_mh, w_out, g_mlp, w_ff1, w_ff2,
                 g_ple, w_ple_gate, b_ple_gate, w_ple):
    B, S, _ = h.shape
    xn = rms_norm(h, g_mix)
    proj = xn @ w_in
    split_at = np.cumsum(IN_SIZES)[:-1].tolist()
    c_q, a_k, a_v, i_k, i_w, m_q, m_k, m_v, m_o, m_i, m_f = jnp.split(proj, split_at, axis=-1)

    c_q = rms_norm(c_q, g_cq)
    a_q = (c_q @ w_q_up).reshape(B, S, ATT_HEADS, HEAD_DIM)
    i_q = (c_q @ w_iq_up).reshape(B, S, IDX_HEADS, IDX_DIM)
    a_q = apply_partial_rope(rms_norm(a_q, g_qn), cos, sin)
    a_k = apply_partial_rope(rms_norm(a_k.reshape(B, S, ATT_KV_HEADS, HEAD_DIM), g_kn), cos, sin)
    a_v = a_v.reshape(B, S, ATT_KV_HEADS, HEAD_DIM)
    i_q = apply_partial_rope(i_q, cos, sin)
    i_k = apply_partial_rope(rms_norm(i_k, g_ik)[:, :, None, :], cos, sin)[:, :, 0, :]
    i_w = i_w * IDX_SCALE
    att = dsa_attention(a_q, a_k, a_v, i_q, i_k, i_w).reshape(B, S, ATT_W)

    qk = jax.nn.silu(causal_dwconv(jnp.concatenate([m_q, m_k], axis=-1), conv_w, conv_b))
    m_q, m_k = qk[..., :ML_W], qk[..., ML_W:]
    hm = mlstm_chunkwise(m_q.reshape(B, S, ML_HEADS, ML_DIM), m_k.reshape(B, S, ML_HEADS, ML_DIM),
                         m_v.reshape(B, S, ML_HEADS, ML_DIM), m_i + i_bias, m_f + f_bias)
    hm = (jax.nn.sigmoid(m_o) * rms_norm(hm, g_mh).reshape(B, S, ML_W))

    h = h + jnp.concatenate([att, hm], axis=-1) @ w_out

    u = rms_norm(h, g_mlp) @ w_ff1
    h = h + jnp.square(jax.nn.relu(u)) @ w_ff2

    gate = jax.nn.sigmoid(rms_norm(h, g_ple) @ w_ple_gate + b_ple_gate)
    return h + gate * (p_i @ w_ple)

def second_inputs(seed: int = 0) -> dict:
    key = jax.random.key(seed)
    ks = iter(jax.random.split(key, 32))
    f32 = jnp.float32

    def nrm(shape, scale):
        return jax.random.normal(next(ks), shape, f32) * scale

    def gain(shape):
        return 1.0 + nrm(shape, 0.02)

    L = DEPTH_2
    x = nrm((BATCH, SEQ, D_MODEL), 1.0)
    p = nrm((L, BATCH, SEQ, PLE_DIM), 1.0)
    offs = jax.random.randint(next(ks), (BATCH, 1), 0, 4096, dtype=jnp.int32)
    positions = jnp.arange(SEQ, dtype=jnp.int32)[None, :] + offs
    return {
        "x": x,
        "p": p,
        "positions": positions,
        "g_mix": gain((L, D_MODEL)),
        "w_in": nrm((L, D_MODEL, IN_W), D_MODEL ** -0.5),
        "g_cq": gain((L, Q_RANK)),
        "w_q_up": nrm((L, Q_RANK, ATT_W), Q_RANK ** -0.5),
        "w_iq_up": nrm((L, Q_RANK, IDX_HEADS * IDX_DIM), Q_RANK ** -0.5),
        "g_qn": gain((L, HEAD_DIM)),
        "g_kn": gain((L, HEAD_DIM)),
        "g_ik": gain((L, IDX_DIM)),
        "conv_w": nrm((L, CONV_W, 2 * ML_W), CONV_W ** -0.5),
        "conv_b": nrm((L, 2 * ML_W), 0.01),
        "i_bias": nrm((L, ML_HEADS), 0.1),
        "f_bias": jnp.linspace(3.0, 6.0, ML_HEADS, dtype=f32)[None, :] + nrm((L, ML_HEADS), 0.1),
        "g_mh": gain((L, ML_HEADS, ML_DIM)),
        "w_out": nrm((L, MIX_W, D_MODEL), MIX_W ** -0.5),
        "g_mlp": gain((L, D_MODEL)),
        "w_ff1": nrm((L, D_MODEL, D_FF_2), D_MODEL ** -0.5),
        "w_ff2": nrm((L, D_FF_2, D_MODEL), D_FF_2 ** -0.5),
        "g_ple": gain((L, D_MODEL)),
        "w_ple_gate": nrm((L, D_MODEL, D_MODEL), D_MODEL ** -0.5),
        "b_ple_gate": nrm((L, D_MODEL), 0.01),
        "w_ple": nrm((L, PLE_DIM, D_MODEL), PLE_DIM ** -0.5),
    }

def second_block(x, p, positions, g_mix, w_in, g_cq, w_q_up, w_iq_up, g_qn, g_kn, g_ik,
              conv_w, conv_b, i_bias, f_bias, g_mh, w_out, g_mlp, w_ff1, w_ff2,
              g_ple, w_ple_gate, b_ple_gate, w_ple):
    cos, sin = rope_tables(positions)
    h = x
    for i in range(DEPTH_2):
        h = hybrid_layer(h, p[i], cos, sin, g_mix[i], w_in[i], g_cq[i], w_q_up[i], w_iq_up[i],
                         g_qn[i], g_kn[i], g_ik[i], conv_w[i], conv_b[i], i_bias[i], f_bias[i],
                         g_mh[i], w_out[i], g_mlp[i], w_ff1[i], w_ff2[i], g_ple[i],
                         w_ple_gate[i], b_ple_gate[i], w_ple[i])
    return h


def setup_inputs(seed=0):
    out = dict(first_inputs(seed))
    for name, value in second_inputs(seed + 1).items():
        if name != "x":
            out[name + "_2"] = value
    return out


def reference(
    x, c, ctx, c_ctx, w_ada, b_ada, w_in, ssd_conv_w, ssd_conv_b, ssd_dt_bias, ssd_a_log, ssd_d,
    ssd_norm_w, fnet_w, pool_w, pool_scale, w_out, ln1_g, ln1_b, ffn_w_up, ffn_conv_w,
    ffn_conv_b, ffn_w_down, ln2_g, ln2_b, p_2, positions_2, g_mix_2, w_in_2, g_cq_2, w_q_up_2,
    w_iq_up_2, g_qn_2, g_kn_2, g_ik_2, conv_w_2, conv_b_2, i_bias_2, f_bias_2, g_mh_2, w_out_2,
    g_mlp_2, w_ff1_2, w_ff2_2, g_ple_2, w_ple_gate_2, b_ple_gate_2, w_ple_2,
):
    x = first_block(
        x, c, ctx, c_ctx, w_ada, b_ada, w_in, ssd_conv_w, ssd_conv_b, ssd_dt_bias, ssd_a_log,
        ssd_d, ssd_norm_w, fnet_w, pool_w, pool_scale, w_out, ln1_g, ln1_b, ffn_w_up,
        ffn_conv_w, ffn_conv_b, ffn_w_down, ln2_g, ln2_b,
    )
    return second_block(
        x, p_2, positions_2, g_mix_2, w_in_2, g_cq_2, w_q_up_2, w_iq_up_2, g_qn_2, g_kn_2,
        g_ik_2, conv_w_2, conv_b_2, i_bias_2, f_bias_2, g_mh_2, w_out_2, g_mlp_2, w_ff1_2,
        w_ff2_2, g_ple_2, w_ple_gate_2, b_ple_gate_2, w_ple_2,
    )


_drawn_inputs = setup_inputs


def setup_inputs(seed=0):
    import zlib

    import numpy as np

    out = dict(_drawn_inputs(seed))
    spreads = {}
    factors = {'ctx': 6.95,
     'c_ctx': 5.055,
     'ssd_conv_b': 7.711,
     'ssd_d': 5.414,
     'ssd_norm_w': 2.976,
     'pool_scale': 4.839,
     'ffn_conv_b': 6.995,
     'g_mix_2': 2.675,
     'g_cq_2': 4.924,
     'g_qn_2': 8.0,
     'g_kn_2': 8.0,
     'g_ik_2': 5.038,
     'conv_b_2': 8.0,
     'i_bias_2': 64.0,
     'g_mh_2': 5.994,
     'g_ple_2': 8.0,
     'b_ple_gate_2': 8.0}
    for name, (base, spread) in spreads.items():
        noise = np.random.default_rng([zlib.crc32(name.encode()), seed]).standard_normal(out[name].shape)
        drawn = base * np.exp(spread * noise) if base else spread * noise
        out[name] = __import__('jax').numpy.asarray(drawn.astype(out[name].dtype))
    for name, factor in factors.items():
        out[name] = (out[name] * factor).astype(out[name].dtype)
    return out
```

```python
from contextlib import ExitStack

import numpy as np
import concourse.bass as bass
from concourse import mybir

ALU = mybir.AluOpType
ACT = mybir.ActivationFunctionType
F32 = mybir.dt.float32
I32 = mybir.dt.int32
X = mybir.AxisListType.X

T = 512
TC = 256
EPS = 1e-6
ALPHA = 2.0 ** 0.25
NEG = -3.0e38
GONE = -3.3e38
PEN = -1.0e30
FF1 = 2816
FF2 = 4096
NSLOT = 6
SLOT = 2048
TWO_PI = 2.0 * np.pi
C1 = 6.28125
C2 = float(np.float32(np.floor((TWO_PI - 6.28125) * 2.0 ** 20) / 2.0 ** 20))
C3 = float(np.float32(TWO_PI - 6.28125 - C2))
MAGIC = 12582912.0


def const_layout():
    names = [("ident", 128), ("ule", 128), ("uge", 128), ("ugt", 128), ("ult", 128), ("ones", 128),
             ("mean", 128), ("neg", 128), ("pen", 128), ("dft", 256), ("inv", 1024), ("sel", 512),
             ("freq", 8)]
    at, n = {}, 0
    for name, w in names:
        at[name] = n
        n += w
    return at, n


def const_arrays():
    at, n = const_layout()
    c = np.zeros((128, n), np.float32)
    p = np.arange(128)[:, None]
    f = np.arange(128)[None, :]

    def put(name, v):
        v = np.asarray(v, np.float32)
        c[:v.shape[0], at[name]:at[name] + v.shape[1]] = v

    put("ident", p == f)
    put("ule", p <= f)
    put("uge", p >= f)
    put("ugt", p > f)
    put("ult", p < f)
    put("ones", np.ones((128, 128)))
    put("mean", np.full((128, 128), 1.0 / 1024))
    put("neg", np.where(f <= p, 0.0, NEG))
    put("pen", np.where(f <= p, 0.0, PEN))
    q = np.arange(64)
    ang = 2 * np.pi * (np.outer(q, q) % 64) / 64
    d = np.zeros((128, 256))
    for g in range(2):
        d[g * 64:g * 64 + 64, g * 64:g * 64 + 64] = np.cos(ang) / 8
        d[g * 64:g * 64 + 64, 128 + g * 64:128 + g * 64 + 64] = np.sin(ang) / 8
    put("dft", d)
    pos = np.arange(T)
    inv = np.zeros((128, 1024))
    for g, w in enumerate((2, 4, 8, 16)):
        left = w // 2
        hi = np.minimum(pos + w - left, T)
        lo = np.maximum(pos - left, 0)
        i, half = g // 2, g % 2
        inv[half * 64:half * 64 + 64, i * 512:i * 512 + 512] = 1.0 / (hi - lo)
    put("inv", inv)
    sel = np.zeros((4, 512))
    for h in range(4):
        sel[h, h * 128:h * 128 + 128] = 1.0
    put("sel", sel)
    fr = np.float32(500000.0) ** (-(np.arange(8, dtype=np.float32) * np.float32(2.0)) / np.float32(16))
    put("freq", np.broadcast_to(fr[None, :], (128, 8)))
    k = np.arange(T)
    a = 2 * np.pi * (np.outer(k, k) % T) / T
    dl = np.stack([np.cos(a), -np.sin(a)]).astype(np.float64) / np.sqrt(512.0)
    return {"consts": c, "dftl": dl.astype(np.float32)}


PARAMS = [("c", 8), ("c_ctx", 8), ("b_ada", 48), ("ssd_conv_w", 24), ("ssd_conv_b", 8), ("ssd_norm_w", 4),
          ("pool_scale", 2), ("ln1_g", 8), ("ln1_b", 8), ("ffn_conv_w", 396), ("ffn_conv_b", 44), ("ln2_g", 8),
          ("ln2_b", 8), ("g_mix_2", 16), ("g_cq_2", 4), ("conv_w_2", 64), ("conv_b_2", 16), ("g_mh_2", 8),
          ("g_mlp_2", 16), ("g_ple_2", 16), ("b_ple_gate_2", 16)]
ROWS = [("ssd_dt_bias", 16), ("ssd_a_log", 16), ("ssd_d", 8), ("g_qn_2", 128), ("g_kn_2", 128), ("g_ik_2", 128)]


def offsets(table):
    at, n = {}, 0
    for name, w in table:
        at[name] = n
        n += w
    return at, n


class Sem:

    def __init__(self, h):
        self.h, self.n = h, 0

    def add(self, k):
        self.n += k
        return (self, self.n)


class Eng:

    def __init__(self, sem, chain):
        self.sem, self.chain, self.q, self.seen = sem, chain, [], {}

    def wait(self, *toks):
        for t in toks:
            if t is None:
                continue
            if isinstance(t, list):
                self.wait(*t)
                continue
            s, v = t
            if self.seen.get(id(s), 0) < v:
                self.seen[id(s)] = v
                self.q.append(("w", s.h, v))

    def do(self, fn, *toks, inc=True):
        self.wait(*toks)
        if self.chain and self.sem.n:
            self.wait((self.sem, self.sem.n))
        if inc:
            self.q.append(("i", fn, self.sem.h, 1))
            return self.sem.add(1)
        self.q.append(("i", fn, None, 0))
        return None

    def dma(self, sem, fn, *toks):
        self.wait(*toks)
        self.q.append(("i", fn, sem.h, 16))
        return sem.add(16)

    def play(self, eng):
        for it in self.q:
            if it[0] == "w":
                eng.wait_ge(it[1], it[2])
            else:
                ins = it[1](eng)
                if it[2] is not None:
                    ins.then_inc(it[2], it[3])


class Bank:
    def __init__(self, ap):
        self.ap, self.toks, self.idle = ap, [], True

    def free(self, *toks):
        self.toks, self.idle = list(toks), True


def build(nc, A, out):
    cat, cn = const_layout()
    pat, pn = offsets(PARAMS)
    rat, rn = offsets(ROWS)
    NPT = (pn + 127) // 128

    with ExitStack() as ctx:
        def sb(name, n, dt=F32, p=128):
            return ctx.enter_context(nc.sbuf_tensor(name, [p, n], dt))

        sems = {}

        def sem(name):
            sems[name] = Sem(ctx.enter_context(nc.semaphore(name)))
            return sems[name]

        V = Eng(sem("s_dve"), True)
        S = Eng(sem("s_act"), True)
        G = Eng(sem("s_pool"), True)
        E = Eng(sem("s_pe"), False)
        D = Eng(sem("s_sp"), False)
        s_slot = [sem(f"s_slot{i}") for i in range(NSLOT)]
        s_con, s_par, s_row, s_x, s_cx, s_fw, s_pw, s_gb, s_pos, s_p, s_out = [
            sem(n) for n in ("s_con", "s_par", "s_row", "s_x", "s_cx", "s_fw", "s_pw", "s_gb", "s_pos", "s_p",
                             "s_out")]

        h_t = sb("h", 4096)
        xn_t = sb("xn", 4096)
        mix_t = sb("mix", 4096)
        ring = sb("ring", NSLOT * SLOT)
        con = sb("con", cn)
        par = sb("par", pn)
        rb = sb("rb", rn)
        mod = sb("mod", 96)
        fw = sb("fw", 128)
        pw = sb("pw", 128)
        gb = sb("gb", 8)
        posi = sb("posi", 4, I32)
        rope = sb("rope", 64)
        eps = sb("eps", 2)
        AR = 22400
        arena = sb("arena", AR)
        arena_n = [0]

        def reset(to=0):
            arena_n[0] = to

        def tmp(n):
            a = arena_n[0]
            arena_n[0] += n
            assert arena_n[0] <= AR, arena_n[0]
            return arena[:, a:a + n]

        h = h_t[:, :].rearrange("p (j t) -> p j t", j=8)
        xn = xn_t[:, :].rearrange("p (j t) -> p j t", j=8)
        mix = mix_t[:, :].rearrange("p (j t) -> p j t", j=8)

        def cc(name, w=128, p=128):
            return con[0:p, cat[name]:cat[name] + w]

        ident, ule, uge, ones = cc("ident"), cc("ule"), cc("uge"), cc("ones")

        def pc(name, j, w=1):
            return par[:, pat[name] + j:pat[name] + j + w]

        def row(name, o, w):
            return rb[:, rat[name] + o:rat[name] + o + w]

        banks = [Bank(ctx.enter_context(nc.psum_tensor(f"ps{i}", [128, 512], F32))) for i in range(8)]
        turn = [0, 0]

        def bank(long=False):
            i = 6 + turn[1] % 2 if long else turn[0] % 6
            turn[1 if long else 0] += 1
            b = banks[i]
            assert b.idle, i
            b.idle = False
            return b

        def mm(b, out_ap, lhsT, rhs, start=True, stop=True, waits=(), inc=False):
            if start:
                E.wait(*b.toks)
            return E.do(lambda e: e.matmul(out_ap, lhsT, rhs, start=start, stop=stop), *waits, inc=inc)

        def tr(b, out_ap, src, waits=(), inc=False):
            p = src.shape[0]
            E.wait(*b.toks)
            return E.do(lambda e: e.transpose(out_ap, src, con[0:p, cat["ident"]:cat["ident"] + p]), *waits, inc=inc)

        def act(out_ap, in_ap, func, *toks, bias=0.0, scale=1.0, accum=None):
            if accum is None:
                return S.do(lambda e: e.activation(out_ap, in_ap, func, bias=bias, scale=scale), *toks)
            return S.do(lambda e: e.activation(out_ap, in_ap, func, bias=bias, scale=scale, accum_out=accum), *toks)

        def tt(out_ap, a, b, op, *toks, eng=None):
            return (eng or V).do(lambda e: e.tensor_tensor(out_ap, a, b, op), *toks)

        def ts(out_ap, a, s1, s2, op0, op1, *toks, eng=None):
            if op1 is None:
                return (eng or V).do(lambda e: e.tensor_scalar(out_ap, a, s1, None, op0), *toks)
            return (eng or V).do(lambda e: e.tensor_scalar(out_ap, a, s1, s2, op0, op1), *toks)

        def stt(out_ap, a, s, b, op0, op1, *toks):
            return V.do(lambda e: e.scalar_tensor_tensor(out=out_ap, in0=a, scalar=s, in1=b, op0=op0, op1=op1), *toks)

        def cp(out_ap, a, *toks, eng=None):
            if eng is S:
                return act(out_ap, a, ACT.Copy, *toks)
            return (eng or V).do(lambda e: e.tensor_copy(out_ap, a), *toks)

        def fence():
            now = [(e.sem, e.sem.n) for e in (V, S, G, E) if e.sem.n]
            for e in (V, S, G, E):
                e.wait(*now)
            return now

        nslot = [0]
        slot_free = [[] for _ in range(NSLOT)]

        class Slot:
            pass

        def load(src, kt, w):
            i = nslot[0] % NSLOT
            nslot[0] += 1
            s = Slot()
            s.i = i
            s.ap = ring[:, i * SLOT:i * SLOT + kt * w].rearrange("p (k n) -> p k n", k=kt)
            v = src.rearrange("(k p) n -> p k n", p=128)
            s.tok = D.dma(s_slot[i], lambda e: e.dma_start(s.ap, v), *slot_free[i])
            return s

        def done(s, tok):
            slot_free[s.i] = [tok]

        t_con = D.dma(s_con, lambda e: e.dma_start(con[:, :], A["consts"]))
        stage = tmp(NPT * 128)
        r = 0
        for name, w in PARAMS:
            src = A[name].rearrange(A["_flat"][name]) if A["_flat"][name] else A[name]
            src = src.rearrange("(r f) -> r f", f=128)
            a = 0
            while a < w:
                n = min(w - a, 128 - r % 128)
                t, q = r // 128, r % 128
                dst, sr = stage[q:q + n, t * 128:t * 128 + 128], src[a:a + n, :]
                t_par = D.dma(s_par, lambda e, dst=dst, sr=sr: e.dma_start(dst, sr))
                a += n
                r += n
        rowp = tmp(512)
        for name, w in ROWS:
            src = A[name].rearrange(A["_flat"][name]) if A["_flat"][name] else A[name]
            src = src.rearrange("(a f) -> a f", a=1)
            dst = rowp[0:1, rat[name]:rat[name] + w]
            t_row = S.dma(s_row, lambda e, dst=dst, src=src: e.dma_start(dst, src))
        xs_t = tmp(4096).rearrange("p (c d) -> p c d", c=4)
        cs_t = tmp(2048).rearrange("p (c d) -> p c d", c=2)
        t_x = S.dma(s_x, lambda e: e.dma_start(xs_t, A["x"].rearrange("a (c p) d -> p (a c) d", p=128)))
        t_cx = S.dma(s_cx, lambda e: e.dma_start(cs_t, A["ctx"].rearrange("a (c p) d -> p (a c) d", p=128)))
        fw3 = fw[:, :].rearrange("p (i d) -> p i d", i=2)
        pw3 = pw[:, :].rearrange("p (i d) -> p i d", i=2)
        t_fw = S.dma(s_fw, lambda e: e.dma_start(fw3, A["fnet_w"].rearrange("a (i g) c d -> (g c) (a i) d", i=2)))
        t_pw = S.dma(s_pw, lambda e: e.dma_start(pw3, A["pool_w"].rearrange("a (i g) c d -> (g c) (a i) d", i=2)))
        for n, name in enumerate(("i_bias_2", "f_bias_2")):
            src = A[name].rearrange("l h -> h l")
            dst = gb[0:4, 2 * n:2 * n + 2]
            t_gb = S.dma(s_gb, lambda e, dst=dst, src=src: e.dma_start(dst, src, allow_slow_non_contiguous=True))
        t_pos = S.dma(s_pos, lambda e: e.dma_start(
            posi[:, :], A["positions_2"].rearrange("a (c p) -> p (a c)", p=128), allow_slow_non_contiguous=True))

        V.do(lambda e: e.memset(eps[:, 0:1], EPS))
        t_eps = V.do(lambda e: e.memset(eps[:, 1:2], 1.0))
        S.wait(t_eps)
        E.wait(t_con)
        V.wait(t_con)
        G.wait(t_con)

        for i in range(NPT):
            n = min(128, pn - i * 128)
            b = bank()
            t = tr(b, b.ap[:, 0:n], stage[0:n, i * 128:i * 128 + 128], waits=(t_par,), inc=True)
            t_parT = cp(par[:, i * 128:i * 128 + n], b.ap[:, 0:n], t)
            b.free(t_parT)
        S.wait(t_parT)
        b = bank()
        t = mm(b, b.ap[:, 0:rn], ones[0:1, :], rowp[0:1, 0:rn], waits=(t_row,), inc=True)
        t_rb = cp(rb[:, :], b.ap[:, 0:rn], t)
        b.free(t_rb)

        csil = tmp(16).rearrange("p (k w) -> p k w", w=2)
        act(csil[:, :, 0], pc("c", 0, 8), ACT.Silu)
        t_cs = act(csil[:, :, 1], pc("c_ctx", 0, 8), ACT.Silu)

        mod3 = mod[:, :].rearrange("p (j w) -> p j w", w=2)
        arow = [tmp(512), tmp(512)]
        ada_n = [0]
        arow_free = [[], []]

        def ada_block():
            i = ada_n[0]
            ada_n[0] += 1
            b = bank()
            for half in range(2):
                s = load(A["w_ada"][0, :, i * 512 + half * 256:i * 512 + half * 256 + 256], 8, 256)
                for k in range(8):
                    t = mm(b, b.ap[0:2, half * 256:half * 256 + 256], csil[:, k, :], s.ap[:, k, :],
                           start=(k == 0), stop=(k == 7), waits=(s.tok, t_cs), inc=(k == 7))
                done(s, t)
            ar = arow[i % 2]
            t = cp(ar[0:2, :], b.ap[0:2, :], t, *arow_free[i % 2], eng=S)
            b.free(t)
            b = bank()
            for q in range(4):
                t2 = tr(b, b.ap[:, 2 * q:2 * q + 2], ar[0:2, q * 128:q * 128 + 128], waits=(t,), inc=(q == 3))
            arow_free[i % 2] = [t2]
            t = tt(mod3[:, 4 * i:4 * i + 4, :], b.ap[:, 0:8].rearrange("p (j w) -> p j w", w=2),
                   pc("b_ada", 4 * i, 4).unsqueeze(2).to_broadcast([128, 4, 2]), ALU.add, t2)
            b.free(t)
            if i // 2 in (1, 4):
                t = ts(mod3[:, 4 * i:4 * i + 4, :], mod3[:, 4 * i:4 * i + 4, :], 1.0, None, ALU.add, None)
            return t

        flip = [0]

        def evac(out_ap, in_ap, *toks):
            flip[0] ^= 1
            return cp(out_ap, in_ap, *toks, eng=S if flip[0] else V)

        t_h = []
        for j in range(8):
            b = bank()
            for c in range(4):
                t = tr(b, b.ap[:, c * 128:c * 128 + 128], xs_t[:, c, j * 128:j * 128 + 128], waits=(t_x,), inc=(c == 3))
            t = evac(h[:, j, :], b.ap[:, :], t)
            b.free(t)
            t_h.append(t)
        hc = tmp(2048).rearrange("p (j t) -> p j t", j=8)
        xc_ctx = tmp(2048).rearrange("p (j t) -> p j t", j=8)
        t_hc = []
        for jj in range(4):
            b = bank()
            for q in range(4):
                j, c = 2 * jj + q // 2, q % 2
                t = tr(b, b.ap[:, q * 128:q * 128 + 128], cs_t[:, c, j * 128:j * 128 + 128], waits=(t_cx,),
                       inc=(q == 3))
            t = evac(hc[:, 2 * jj:2 * jj + 2, :], b.ap[:, :].rearrange("p (j t) -> p j t", j=2), t)
            b.free(t)
            t_hc += [t, t]

        def norm_stats(src, toks, sq, n, rs, center=None, count=1024):
            xt = list(toks)
            if center is not None:
                b = bank()
                for j in range(8):
                    t = mm(b, b.ap[:, 0:n], cc("mean"), src[:, j, :], start=(j == 0), stop=(j == 7),
                           waits=(toks[j],), inc=(j == 7))
                for j in range(8):
                    xt[j] = tt(center[:, j, :], src[:, j, :], b.ap[:, 0:n], ALU.subtract, t, toks[j])
                b.free(xt[7])
                src = center
            b = bank()
            used = [None] * len(sq)
            for j in range(8):
                q = sq[j % len(sq)]
                t = act(q[:, 0:n], src[:, j, :], ACT.Square, xt[j], used[j % len(sq)])
                t = mm(b, b.ap[:, 0:n], ones, q[:, 0:n], start=(j == 0), stop=(j == 7), waits=(t,), inc=True)
                used[j % len(sq)] = t
            t = act(rs[:, 0:n], b.ap[:, 0:n], ACT.Sqrt, t, bias=eps[:, 0:1], scale=1.0 / count)
            b.free(t)
            return V.do(lambda e: e.reciprocal(rs[:, 0:n], rs[:, 0:n]), t)

        def apply_norm(src, dst, rs, n, g, bias=None):
            out_t = []
            for j in range(8):
                t = stt(dst[:, j, :], src[:, j, :], g(j), rs[:, 0:n], ALU.mult, ALU.mult)
                if bias is not None:
                    t = act(dst[:, j, :], dst[:, j, :], ACT.Identity, t, bias=bias(j))
                out_t.append(t)
            return out_t

        sq = [tmp(512) for _ in range(4)]
        rs = tmp(512)
        rs2 = tmp(256)
        norm_stats(h, t_h, sq, T, rs, center=xn)
        norm_stats(hc, t_hc, sq, TC, rs2, center=xc_ctx)
        for i in range(4):
            t_mod = ada_block()
        S.wait(t_mod)
        t_xc = apply_norm(xc_ctx, xc_ctx, rs2, TC, lambda j: mod3[:, 8 + j, 1:2], lambda j: mod3[:, j, 1:2])
        t_xn = apply_norm(xn, xn, rs, T, lambda j: mod3[:, 8 + j, 0:1], lambda j: mod3[:, j, 0:1])

        posf = tmp(4)
        ang = tmp(32)
        kk = tmp(32)
        rr = tmp(32)
        cosT, sinT = rope[:, 0:32], rope[:, 32:64]
        cp(posf, posi[:, :], t_pos)
        tt(ang.rearrange("p (c f) -> p c f", c=4), posf.unsqueeze(2).to_broadcast([128, 4, 8]),
           cc("freq", 8).unsqueeze(1).to_broadcast([128, 4, 8]), ALU.mult)
        for dst, shift, add in ((sinT, 0.0, 0.0), (cosT, 0.25, float(np.pi / 2))):
            ts(kk, ang, 1.0 / TWO_PI, shift, ALU.mult, ALU.add)
            ts(kk, kk, MAGIC, None, ALU.add, None)
            ts(kk, kk, MAGIC, None, ALU.subtract, None)
            stt(rr, kk, -C1, ang, ALU.mult, ALU.add)
            stt(rr, kk, -C2, rr, ALU.mult, ALU.add)
            stt(rr, kk, -C3, rr, ALU.mult, ALU.add)
            ts(rr, rr, add, 3.1415925, ALU.add, ALU.min)
            t = ts(rr, rr, -3.1415925, None, ALU.max, None)
            t = act(dst, rr, ACT.Sin, t)
            V.wait(t)
        f = fence()

        reset(0)
        Xt = tmp(2048 + 1024).rearrange("p (q n) -> p q n", q=6)
        Bt = tmp(1024 + 512).rearrange("p (q n) -> p q n", q=6)
        lo = NPT * 128 + 512 + 4096 + 2048
        assert arena_n[0] <= lo
        Z = tmp(2048).rearrange("p (q n) -> p q n", q=4)
        small = sb("small", 1024)
        dtr, dta, dtb, wst, dt = [small[:, i * 96:i * 96 + 96] for i in range(5)]
        ex = small[:, 480:960]
        aneg = small[:, 960:976]
        assert arena_n[0] <= lo, arena_n[0]
        reset(lo + 16 + 1024 + 4096)
        BT = tmp(1024).rearrange("p (g t) -> p g t", g=2)
        CT = tmp(1024).rearrange("p (g t) -> p g t", g=2)
        acc = [tmp(512) for _ in range(4)]
        acc_free = [[] for _ in range(4)]
        nacc = [0]
        after_conv = arena_n[0]

        def conv3(b, n, wname, j, toks, bname):
            i = nacc[0] % 4
            nacc[0] += 1
            a = acc[i]
            u = b.ap
            t = act(a[:, 0:n], u[:, 0:n], ACT.Identity, *toks, *acc_free[i], bias=pc(bname, j),
                    scale=pc(wname, 8 + j))
            stt(a[:, 1:n], u[:, 0:n - 1], pc(wname, j), a[:, 1:n], ALU.mult, ALU.add, t)
            t = stt(a[:, 0:n - 1], u[:, 1:n], pc(wname, 16 + j), a[:, 0:n - 1], ALU.mult, ALU.add)
            b.free(t)
            return i, a, t

        w_in = A["w_in"][0]
        q0 = {0: 0, 1: 2}
        for sl in range(4):
            s = load(w_in[:, 512 + sl * 256:512 + sl * 256 + 256], 8, 256)
            for jj in range(2):
                j = 2 * sl + jj
                for which in range(2):
                    if which == 1 and j >= 6:
                        continue
                    src, n, tk = (xn, T, t_xn) if which == 0 else (xc_ctx, TC, t_xc)
                    b = bank()
                    for k in range(8):
                        t = mm(b, b.ap[:, 0:n], s.ap[:, k, jj * 128:jj * 128 + 128], src[:, k, :], start=(k == 0),
                               stop=(k == 7), waits=(s.tok, tk[k]), inc=(k == 7))
                    last = t
                    i, a, t = conv3(b, n, "ssd_conv_w", j, (t,), "ssd_conv_b")
                    qs = 2 if which == 0 else 0
                    if j >= 6:
                        t = act(CT[:, j - 6, :], a, ACT.Silu, t)
                        acc_free[i] = [t]
                        continue
                    if j >= 4 and which == 0:
                        t = act(BT[:, j - 4, :], a, ACT.Silu, t)
                        acc_free[i] = [t]
                        a = BT[:, j - 4, :]
                    else:
                        t = act(a[:, 0:n], a[:, 0:n], ACT.Silu, t)
                    b = bank()
                    for c in range(n // 128):
                        t2 = tr(b, b.ap[:, c * 128:c * 128 + 128], a[:, c * 128:c * 128 + 128], waits=(t,),
                                inc=(c == n // 128 - 1))
                    if not (j >= 4 and which == 0):
                        acc_free[i] = [t2]
                    dst = Xt[:, qs:qs + n // 128, j * 128:j * 128 + 128] if j < 4 else \
                        Bt[:, qs:qs + n // 128, (j - 4) * 128:(j - 4) * 128 + 128]
                    t = evac(dst, b.ap[:, 0:n].rearrange("p (c f) -> p c f", f=128), t2)
                    b.free(t)
            done(s, last)
        s = load(w_in[:, 1536:1552], 8, 16)
        b = bank()
        for q in range(6):
            src, c = (xc_ctx, q) if q < 2 else (xn, q - 2)
            for k in range(8):
                t = mm(b, b.ap[:, q * 16:q * 16 + 16], src[:, k, c * 128:c * 128 + 128], s.ap[:, k, :],
                       start=(k == 0), stop=(k == 7), waits=(s.tok,), inc=(k == 7))
        done(s, t)

        def softplus(dst, raw, e1, e2, sign):
            t = ts(e1, raw, -1.0, None, ALU.mult, None)
            tt(e1, e1, raw, ALU.min)
            ts(dst, raw, sign, 0.0, ALU.mult, ALU.max)
            t = act(e1, e1, ACT.Exp, (V.sem, V.sem.n))
            ts(e2, e1, 1.0, None, ALU.add, None, t)
            t = act(e2, e2, ACT.Ln, (V.sem, V.sem.n))
            tt(dst, dst, e2, ALU.add, t)
            ts(e2, e1, 1.0, None, ALU.add, None)
            ts(raw, e2, 1.0, None, ALU.subtract, None)
            tt(e1, e1, raw, ALU.subtract)
            V.do(lambda e: e.reciprocal(e2, e2))
            tt(e1, e1, e2, ALU.mult)
            return tt(dst, dst, e1, ALU.add)

        t = tt(dtr.rearrange("p (q w) -> p q w", q=6), b.ap[:, 0:96].rearrange("p (q w) -> p q w", q=6),
               row("ssd_dt_bias", 0, 16).unsqueeze(1).to_broadcast([128, 6, 16]), ALU.add, t)
        b.free(t)
        softplus(dt, dtr, dta, dtb, 1.0)
        t = act(aneg, row("ssd_a_log", 0, 16), ACT.Exp, t_rb)
        ts(aneg, aneg, -1.0, None, ALU.mult, None, t)
        dt3 = dt.rearrange("p (q w) -> p q w", q=6)
        t_a = tt(dta.rearrange("p (q w) -> p q w", q=6), dt3, aneg.unsqueeze(1).to_broadcast([128, 6, 16]), ALU.mult)
        b = bank()
        for i, m in enumerate((ule, uge, cc("ugt"), cc("ult"), ones)):
            t = mm(b, b.ap[:, i * 96:i * 96 + 96], m, dta, waits=(t_a,), inc=(i == 4))
        t_ex = act(ex, b.ap[:, 0:480], ACT.Exp, t)
        b.free(t_ex)
        ex4 = ex.rearrange("p (i q w) -> p i q w", i=5, q=6)
        w3 = wst.rearrange("p (q w) -> p q w", q=6)
        tt(w3[:, :, 0:8], dt3[:, :, 0:8], ex4[:, 2, :, 0:8], ALU.mult, t_ex)
        tt(w3[:, :, 8:16], dt3[:, :, 8:16], ex4[:, 3, :, 8:16], ALU.mult)

        for sl in range(2):
            s = load(w_in[:, sl * 256:sl * 256 + 256], 8, 256)
            for c in range(4):
                b = bank()
                for k in range(8):
                    t = mm(b, b.ap[:, 0:256], xn[:, k, c * 128:c * 128 + 128], s.ap[:, k, :], start=(k == 0),
                           stop=(k == 7), waits=(s.tok,), inc=(k == 7))
                if c == 3:
                    done(s, t)
                t_z = act(Z[:, c, sl * 256:sl * 256 + 256], b.ap[:, 0:256], ACT.Silu, t)
                b.free(t_z)

        reset(after_conv)
        fT = acc
        fin = []
        for sl, name in ((0, "f"), (1, "p")):
            s = load(w_in[:, 1552 + sl * 256:1552 + sl * 256 + 256], 8, 256)
            for i in range(2):
                b = bank()
                for k in range(8):
                    t = mm(b, b.ap[:, :], s.ap[:, k, i * 128:i * 128 + 128], xn[:, k, :], start=(k == 0),
                           stop=(k == 7), waits=(s.tok,), inc=(k == 7))
                fin.append((b, t))
            done(s, t)
        fA = tmp(2048).rearrange("p (c i s f) -> p c i s f", c=4, i=2, s=2)
        for i in range(2):
            b, t = fin[i]
            t = evac(acc[i], b.ap[:, :], t, *acc_free[i])
            b.free(t)
            fin[i] = t
        PW = 544
        pb = [tmp(2 * PW).rearrange("p (i t) -> p i t", i=2) for _ in range(3)]
        V.do(lambda e: e.memset(pb[0][:, :, 0:16], 0.0))
        t = V.do(lambda e: e.memset(pb[0][:, :, 528:544], 0.0))
        for i in range(2):
            b, t = fin[2 + i]
            t = cp(pb[0][:, i, 16:528], b.ap[:, :], t)
            b.free(t)
        P0, P1, P2 = pb
        tt(P1[:, :, 1:544], P0[:, :, 0:543], P0[:, :, 1:544], ALU.add)
        tt(P2[:, :, 2:543], P1[:, :, 1:542], P1[:, :, 3:544], ALU.add)
        iv = cc("inv", 1024).rearrange("p (i t) -> p i t", i=2)
        po = acc[2:4]
        for a_ in acc_free[2:4]:
            V.wait(*a_)
        tt(po[0][0:64, :], P1[0:64, 0, 16:528], iv[0:64, 0, :], ALU.mult)
        tt(po[0][64:128, :], P2[64:128, 0, 16:528], iv[64:128, 0, :], ALU.mult)
        tt(P1[:, 1, 4:541], P2[:, 1, 2:539], P2[:, 1, 6:543], ALU.add)
        tt(po[1][0:64, :], P1[0:64, 1, 16:528], iv[0:64, 1, :], ALU.mult)
        tt(P2[:, 1, 16:528], P1[:, 1, 12:524], P1[:, 1, 20:532], ALU.add)
        tt(po[1][64:128, :], P2[64:128, 1, 16:528], iv[64:128, 1, :], ALU.mult)
        tt(po[0], po[0], P0[:, 0, 16:528], ALU.subtract)
        t_po = tt(po[1], po[1], P0[:, 1, 16:528], ALU.subtract)
        for c in range(4):
            b = bank()
            for i in range(2):
                t = mm(b, b.ap[:, i * 256:i * 256 + 256], acc[i][:, c * 128:c * 128 + 128], cc("dft", 256),
                       waits=(fin[0], fin[1]), inc=(i == 1))
            t_fA = evac(fA[:, c].rearrange("p i s f -> p (i s f)"), b.ap[:, :], t)
            b.free(t_fA)
            E.wait(t_fA)
        sC = [load(A["dftl"][i], 4, 512) for i in range(2)]
        spec = [acc[0], acc[1]]
        t_sp = []
        for i in range(2):
            b = bank()
            n = 0
            for cs_ in range(2):
                for c in range(4):
                    t = mm(b, b.ap[:, :], fA[:, c, i, cs_, :], sC[cs_].ap[:, c, :], start=(n == 0), stop=(n == 7),
                           waits=(sC[cs_].tok,), inc=(n == 7))
                    n += 1
            t_e = evac(spec[i], b.ap[:, :], t)
            b.free(t_e)
            t_sp.append(t_e)
        done(sC[0], t)
        done(sC[1], t)
        for src, w, t_w, base, tk in ((spec, fw3, t_fw, 4, t_sp), (po, pw3, t_pw, 6, [t_po, t_po])):
            for i in range(2):
                b = bank()
                for g in range(2):
                    t = mm(b, b.ap[g * 64:g * 64 + 64, :], w[g * 64:g * 64 + 64, i, :], src[i][g * 64:g * 64 + 64, :],
                           waits=(t_w, tk[i]), inc=(g == 1))
                if base == 4:
                    t = evac(mix[:, 4 + i, :], b.ap[:, :], t)
                else:
                    t = ts(mix[:, 6 + i, :], b.ap[:, :], pc("pool_scale", i), None, ALU.mult, None, t)
                b.free(t)
        fence()

        reset(after_conv)
        Sf = tmp(2048).rearrange("p (q n) -> p q n", q=4)
        Sb = tmp(2048).rearrange("p (q n) -> p q n", q=4)
        Xs = [acc[0], acc[1]]
        Stmp = acc[2]
        Xs_free = [[], []]
        nxs = [0]

        def v8(ap):
            return ap.rearrange("p (h d) -> p h d", h=8)

        def bc8(ap):
            return ap.unsqueeze(2).to_broadcast([128, 8, 64])

        def chunk_state(q, d):
            i = nxs[0] % 2
            nxs[0] += 1
            t = tt(v8(Xs[i]), v8(Xt[:, q, :]), bc8(w3[:, q, d * 8:d * 8 + 8]), ALU.mult, *Xs_free[i])
            b = bank()
            for g in range(2):
                t = mm(b, b.ap[:, g * 256:g * 256 + 256], Bt[:, q, g * 128:g * 128 + 128],
                       Xs[i][:, g * 256:g * 256 + 256], waits=(t,), inc=(g == 1))
            Xs_free[i] = [t]
            return b, t

        t_st = {}
        for d, first, order in ((0, (0, 1), (2, 3, 4)), (1, (1, 0), (5, 4, 3))):
            St = (Sf, Sb)[d]
            where = (0, 1, 2, 3) if d == 0 else (3, 2, 1, 0)
            b, t = chunk_state(first[0], d)
            t = cp(Stmp, b.ap[:, :], t)
            b.free(t)
            cur = Stmp
            for n, q in enumerate((first[1],) + order):
                b, t = chunk_state(q, d)
                dst = St[:, where[n], :]
                tt(v8(dst), v8(cur), bc8(ex4[:, 4, q, d * 8:d * 8 + 8]), ALU.mult)
                t = tt(dst, dst, b.ap[:, :], ALU.add, t)
                b.free(t)
                cur = dst
                t_st[(d, where[n])] = t

        reset(lo + 16 + 1024)
        Y = tmp(2048).rearrange("p (q n) -> p q n", q=4)
        Rf = tmp(1024)
        Ex = tmp(1024)
        dmb = Rf
        Rb, dmf, Rf = [xn_t[:, i * 1024:i * 1024 + 1024] for i in range(3)]
        ssq = xn_t[:, 3072:3088]

        def v3(ap):
            return ap.rearrange("p (h l) -> p h l", h=8)

        def masks(m):
            return m.unsqueeze(1).to_broadcast([128, 8, 128])

        def cols(ap):
            return ap.unsqueeze(2).to_broadcast([128, 8, 128])

        R_free = []
        M_free = []
        a3 = dta.rearrange("p (q w) -> p q w", q=6)
        for c in range(4):
            q = c + 2
            if c < 4:
                ada_block()
            tg1 = tt(v3(Rf), cols(a3[:, q, 0:8]), masks(ule), ALU.mult, t_a, *R_free, eng=G)
            tg2 = tt(v3(Rb), cols(a3[:, q, 8:16]), masks(uge), ALU.mult, eng=G)
            bs = []
            for half in range(2):
                b = bank()
                mm(b, b.ap[:, :], cc("ugt"), Rf[:, half * 512:half * 512 + 512], start=True, stop=False, waits=(tg2,))
                t = mm(b, b.ap[:, :], cc("ult"), Rb[:, half * 512:half * 512 + 512], start=False, stop=True, inc=True)
                bs.append((b, t))
            R_free = [t]
            for half in range(2):
                b, t = bs[half]
                t_E = act(Ex[:, half * 512:half * 512 + 512], b.ap[:, :], ACT.Exp, t, *M_free)
                b.free(t_E)
            bg = bank()
            for g in range(2):
                t_g = mm(bg, bg.ap[:, g * 128:g * 128 + 128], BT[:, g, c * 128:c * 128 + 128],
                         CT[:, g, c * 128:c * 128 + 128], inc=(g == 1))
            tt(v3(dmf), cols(dt3[:, q, 0:8]), masks(ule), ALU.mult, *M_free)
            tt(v3(dmb), cols(dt3[:, q, 8:16]), masks(uge), ALU.mult)
            tt(dmf, dmf, dmb, ALU.add)
            tt(dmf, dmf, Ex, ALU.mult, t_E)
            for g in range(2):
                t_M = tt(v3(dmf)[:, 4 * g:4 * g + 4, :], v3(dmf)[:, 4 * g:4 * g + 4, :],
                         bg.ap[:, g * 128:g * 128 + 128].unsqueeze(1).to_broadcast([128, 4, 128]), ALU.mult, t_g)
            bg.free(t_M)
            bf, bb = bank(), bank()
            for bx, St, d in ((bf, Sf, 0), (bb, Sb, 1)):
                for g in range(2):
                    t_off = mm(bx, bx.ap[:, g * 256:g * 256 + 256], CT[:, g, c * 128:c * 128 + 128],
                               St[:, c, g * 256:g * 256 + 256], waits=(t_st[(d, c)],), inc=(g == 1))
            bd = bank()
            for hh in range(8):
                t_d = mm(bd, bd.ap[:, hh * 64:hh * 64 + 64], dmf[:, hh * 128:hh * 128 + 128],
                         Xt[:, q, hh * 64:hh * 64 + 64], waits=(t_M,), inc=(hh == 7))
            M_free = [t_d]
            y = Y[:, c, :]
            y1 = acc[3]
            tt(v8(y), v8(Xt[:, q, :]), bc8(row("ssd_d", 0, 8)), ALU.mult, t_rb)
            tt(y, y, bd.ap[:, :], ALU.add, t_d)
            bd.free((V.sem, V.sem.n))
            tt(v8(y1), v8(bf.ap[:, :]), bc8(ex4[:, 0, q, 0:8]), ALU.mult, t_off)
            bf.free((V.sem, V.sem.n))
            tt(y, y, y1, ALU.add)
            tt(v8(y1), v8(bb.ap[:, :]), bc8(ex4[:, 1, q, 8:16]), ALU.mult)
            bb.free((V.sem, V.sem.n))
            tt(y, y, y1, ALU.add)
            t = tt(y, y, Z[:, c, :], ALU.mult, t_z)
            for g in range(2):
                t_q = act(acc[2][:, g * 256:g * 256 + 256], y[:, g * 256:g * 256 + 256], ACT.Square, t,
                          accum=ssq[:, 2 * c + g:2 * c + g + 1])
        t = act(ssq[:, 8:16], ssq[:, 0:8], ACT.Sqrt, bias=eps[:, 0:1], scale=1.0 / 256)
        V.do(lambda e: e.reciprocal(ssq[:, 8:16], ssq[:, 8:16]), t)
        for c in range(4):
            for g in range(2):
                t = ts(Y[:, c, g * 256:g * 256 + 256], Y[:, c, g * 256:g * 256 + 256],
                       ssq[:, 8 + 2 * c + g:9 + 2 * c + g], None, ALU.mult, None)
            E.wait(t)
        t_mix = []
        for j in range(4):
            b = bank()
            for c in range(4):
                t = tr(b, b.ap[:, c * 128:c * 128 + 128], Y[:, c, j * 128:j * 128 + 128], inc=(c == 3))
            t = ts(mix[:, j, :], b.ap[:, :], pc("ssd_norm_w", j), None, ALU.mult, None, t)
            b.free(t)
            t_mix.append(t)
        while ada_n[0] < 12:
            t_mod = ada_block()
        S.wait(t_mod)
        E.wait(t_mix[3], (S.sem, S.sem.n))

        def project(W, kt, src, evac_fn):
            for cb in range(4):
                bs = [bank(), bank()]
                k0 = 0
                while k0 < kt:
                    n = min(8, kt - k0)
                    s = load(W[k0 * 128:(k0 + n) * 128, cb * 256:cb * 256 + 256], n, 256)
                    for jj in range(2):
                        for k in range(k0, k0 + n):
                            t = mm(bs[jj], bs[jj].ap[:, :], s.ap[:, k - k0, jj * 128:jj * 128 + 128], src(k),
                                   start=(k == 0), stop=(k == kt - 1), waits=(s.tok,), inc=(k == k0 + n - 1))
                        bs[jj].last = t
                    done(s, t)
                    k0 += n
                for jj in range(2):
                    evac_fn(2 * cb + jj, bs[jj], bs[jj].last)

        def residual(gcol, tbufs):
            toks = [None] * 8

            def fn(j, b, t):
                y = tbufs[j % 2]
                t = act(y, b.ap[:, :], ACT.Copy, t, *fn.free[j % 2], scale=mod3[:, gcol + j, 0:1])
                b.free(t)
                toks[j] = stt(h[:, j, :], h[:, j, :], ALPHA, y, ALU.mult, ALU.add, t)
                fn.free[j % 2] = [toks[j]]
            fn.free = [[], []]
            return fn, toks

        f = fence()
        reset(0)
        G1 = tmp(22 * 512).rearrange("p (j t) -> p j t", j=22)
        sq = [tmp(512) for _ in range(4)]
        rs = tmp(512)
        acc = [tmp(512) for _ in range(8)]
        fn, toks = residual(16, acc[0:2])
        project(A["w_out"][0], 8, lambda k: mix[:, k, :], fn)

        def post_norm(toks, g, bb_):
            norm_stats(h, toks, sq, T, rs, center=xn)
            return apply_norm(xn, h, rs, T, lambda j: pc(g, j), lambda j: pc(bb_, j))

        t_h = post_norm(toks, "ln1_g", "ln1_b")
        norm_stats(h, t_h, sq, T, rs, center=xn)
        t_xn = apply_norm(xn, xn, rs, T, lambda j: mod3[:, 32 + j, 0:1], lambda j: mod3[:, 24 + j, 0:1])
        fence()

        w_up = A["ffn_w_up"][0]
        acc_free = [[] for _ in range(8)]
        na = 0

        def grid(ap, dr, dc, src):
            v = ap.rearrange("p (r c) -> p r c", r=8)
            r0, r1 = max(0, -dr), min(8, 8 - dr)
            c0, c1 = max(0, -dc), min(64, 64 - dc)
            if src:
                return v[:, r0 + dr:r1 + dr, c0 + dc:c1 + dc]
            return v[:, r0:r1, c0:c1]

        for jp in range(11):
            sv = load(w_up[:, jp * 256:jp * 256 + 256], 8, 256)
            sg = load(w_up[:, FF1 + jp * 256:FF1 + jp * 256 + 256], 8, 256)
            for jj in range(2):
                j = 2 * jp + jj
                got = []
                for s, col in ((sg, 22 + j), (sv, j)):
                    b = bank()
                    for k in range(8):
                        t = mm(b, b.ap[:, :], s.ap[:, k, jj * 128:jj * 128 + 128], xn[:, k, :], start=(k == 0),
                               stop=(k == 7), waits=(s.tok,), inc=(k == 7))
                    if jj == 1:
                        done(s, t)
                    i = na % 8
                    na += 1
                    a = acc[i]
                    t = act(a, b.ap[:, :], ACT.Identity, t, *acc_free[i], bias=pc("ffn_conv_b", col),
                            scale=pc("ffn_conv_w", 4 * 44 + col))
                    for dr in (-1, 0, 1):
                        for dc in (-1, 0, 1):
                            if dr == 0 and dc == 0:
                                continue
                            tap = (dr + 1) * 3 + dc + 1
                            o = grid(a, dr, dc, False)
                            t = stt(o, grid(b.ap[:, :], dr, dc, True), pc("ffn_conv_w", tap * 44 + col), o,
                                    ALU.mult, ALU.add, t)
                    b.free(t)
                    got.append((i, a, t))
                (ig, ga, tg), (iv_, va, tv) = got
                tg = act(ga, ga, ACT.Gelu_apprx_tanh, tg)
                t = tt(G1[:, j, :], ga, va, ALU.mult, tg, tv, eng=G)
                acc_free[ig] = [t]
                acc_free[iv_] = [t]
        E.wait(t)
        V.wait(t)
        S.wait(t)
        fn, toks = residual(40, acc[0:2])
        project(A["ffn_w_down"][0], 22, lambda k: G1[:, k, :], fn)
        t_h = post_norm(toks, "ln2_g", "ln2_b")
        fence()

        def rms(gname, l):
            norm_stats(h, t_h, sq, T, rs)
            return apply_norm(h, xn, rs, T, lambda j: pc(gname, 8 * l + j))

        for l in range(2):
            reset(0)
            sq = [tmp(512) for _ in range(4)]
            rs = tmp(512)
            t_xn = rms("g_mix_2", l)
            E.wait(t_xn[7])
            qt = tmp(2048).rearrange("p (c n) -> p c n", c=4)
            it = tmp(2048).rearrange("p (c n) -> p c n", c=4)
            ct = tmp(1024).rearrange("p (c n) -> p c n", c=4)
            ctT = tmp(1024).rearrange("p (k t) -> p k t", k=2)
            kt = tmp(1024).rearrange("p (c n) -> p c n", c=4)
            ikt = tmp(512).rearrange("p (c n) -> p c n", c=4)
            iw = tmp(32).rearrange("p (c n) -> p c n", c=4)
            vt = tmp(512).rearrange("p (c n) -> p c n", c=4)
            ro = [tmp(256) for _ in range(4)]
            st8 = tmp(64)
            mark = arena_n[0]
            mq = tmp(2048).rearrange("p (j t) -> p j t", j=4)
            mk = tmp(2048).rearrange("p (j t) -> p j t", j=4)
            mv = tmp(2048).rearrange("p (c n) -> p c n", c=4)
            mo = tmp(2048).rearrange("p (j t) -> p j t", j=4)
            fr = tmp(512)
            ir = tmp(512)
            er = tmp(512)
            w2 = A["w_in_2"][l]
            ksrc = kt.rearrange("p c (v r d) -> p c v r d", v=2, r=2)
            s0 = load(w2[:, 0:256], 8, 256)
            s1 = load(w2[:, 256:512], 8, 256)
            s2 = load(w2[:, 512:584], 8, 72)
            for c in range(4):
                b1, b2 = bank(), bank()
                for b, s, o, w in ((b1, s0, 0, 256), (b1, s1, 256, 256), (b2, s2, 0, 72)):
                    for k in range(8):
                        t = mm(b, b.ap[:, o:o + w], xn[:, k, c * 128:c * 128 + 128], s.ap[:, k, :], start=(k == 0),
                               stop=(k == 7), waits=(s.tok,), inc=(k == 7))
                    if c == 3:
                        done(s, t)
                act(ct[:, c, :], b1.ap[:, 0:256], ACT.Copy, t)
                act(ksrc[:, c, :, 0, :], b1.ap[:, 256:384].rearrange("p (v d) -> p v d", v=2), ACT.Copy)
                t = act(vt[:, c, :], b1.ap[:, 384:512], ACT.Copy)
                b1.free(t)
                act(ikt[:, c, 0:64], b2.ap[:, 0:64], ACT.Copy)
                t = act(iw[:, c, :], b2.ap[:, 64:72], ACT.Copy, scale=float(8 ** -0.5 * 64 ** -0.5))
                b2.free(t)

            def group_rs(src, ng, w, dst, scratch, count, tk=None):
                t = act(scratch, src, ACT.Square, tk)
                t = V.do(lambda e: e.tensor_reduce(dst, scratch, X, ALU.add), t)
                t = act(dst, dst, ACT.Sqrt, t, bias=eps[:, 0:1], scale=1.0 / count)
                return V.do(lambda e: e.reciprocal(dst, dst), t)

            scr = er
            big = sq[0]
            sv = mv[:, 0:2, :].rearrange("p c n -> p (c n)").rearrange("p (c n) -> p c n", c=4)
            group_rs(ct, 4, 256, st8[:, 0:4], sv, 256)
            t = tt(ct, ct, st8[:, 0:4].unsqueeze(2).to_broadcast([128, 4, 256]), ALU.mult)
            for k in range(2):
                b = bank()
                for c in range(4):
                    t2 = tr(b, b.ap[:, c * 128:c * 128 + 128], ct[:, c, k * 128:k * 128 + 128], waits=(t,), inc=(c == 3))
                t3 = ts(ctT[:, k, :], b.ap[:, :], pc("g_cq_2", 2 * l + k), None, ALU.mult, None, t2)
                b.free(t3)
            sq_ = load(A["w_q_up_2"][l], 2, 512)
            si_ = load(A["w_iq_up_2"][l], 2, 512)
            for s, dst in ((sq_, qt), (si_, it)):
                for c in range(4):
                    b = bank()
                    for k in range(2):
                        t = mm(b, b.ap[:, :], ctT[:, k, c * 128:c * 128 + 128], s.ap[:, k, :], start=(k == 0),
                               stop=(k == 1), waits=(s.tok, t3), inc=(k == 1))
                    t_q = evac(dst[:, c, :], b.ap[:, :], t)
                    b.free(t_q)
                    V.wait(t_q)
                    S.wait(t_q)
                done(s, t)

            def rope_on(src, nh, dup=False):
                co = cosT.rearrange("p (c f) -> p c f", c=4).unsqueeze(2).to_broadcast([128, 4, nh, 8])
                si = sinT.rearrange("p (c f) -> p c f", c=4).unsqueeze(2).to_broadcast([128, 4, nh, 8])
                x1, x2 = src[:, :, :, 0:8], src[:, :, :, 8:16]
                r4 = [r_[:, 0:32 * nh].rearrange("p (c n f) -> p c n f", c=4, n=nh) for r_ in ro]
                tt(r4[0], x1, co, ALU.mult)
                tt(r4[1], x2, si, ALU.mult)
                tt(r4[2], x2, co, ALU.mult)
                tt(r4[3], x1, si, ALU.mult)
                tt(x1, r4[0], r4[1], ALU.subtract)
                return tt(x2, r4[2], r4[3], ALU.add)

            q4 = qt.rearrange("p c (n d) -> p c n d", n=8)
            i4 = it.rearrange("p c (n d) -> p c n d", n=8)
            qf = qt.rearrange("p c (n d) -> p (c n) d", n=8)
            s2_ = mv.rearrange("p c (n d) -> p (c n) d", n=8)
            group_rs(qf, 32, 64, st8[:, 0:32], s2_, 64)
            tt(qf, qf, st8[:, 0:32].unsqueeze(2).to_broadcast([128, 32, 64]), ALU.mult)
            tt(qf, qf, row("g_qn_2", 64 * l, 64).unsqueeze(1).to_broadcast([128, 32, 64]), ALU.mult)
            rope_on(q4, 8)
            t_i = rope_on(i4, 8)
            k3 = ksrc[:, :, :, 0, :]
            kz = sq[0].rearrange("p (c v d) -> p c v d", c=4, v=2)
            t = act(kz, k3, ACT.Square)
            t = V.do(lambda e: e.tensor_reduce(st8[:, 32:40].rearrange("p (c v) -> p c v", c=4), kz, X, ALU.add), t)
            t = act(st8[:, 32:40], st8[:, 32:40], ACT.Sqrt, t, bias=eps[:, 0:1], scale=1.0 / 64)
            V.do(lambda e: e.reciprocal(st8[:, 32:40], st8[:, 32:40]), t)
            tt(k3, k3, st8[:, 32:40].rearrange("p (c v) -> p c v", c=4).unsqueeze(3).to_broadcast([128, 4, 2, 64]),
               ALU.mult)
            tt(k3, k3, row("g_kn_2", 64 * l, 64).unsqueeze(1).unsqueeze(1).to_broadcast([128, 4, 2, 64]), ALU.mult)
            rope_on(k3, 2)
            t = cp(ksrc[:, :, :, 1, :], k3)
            ik3 = ikt[:, :, 0:64]
            iz = sq[1][:, 0:256].rearrange("p (c d) -> p c d", c=4)
            group_rs(ik3, 4, 64, st8[:, 40:44], iz, 64)
            tt(ik3, ik3, st8[:, 40:44].unsqueeze(2).to_broadcast([128, 4, 64]), ALU.mult)
            tt(ik3, ik3, row("g_ik_2", 64 * l, 64).unsqueeze(1).to_broadcast([128, 4, 64]), ALU.mult)
            rope_on(ik3.unsqueeze(2), 1)
            t_k = cp(ikt[:, :, 64:128], ik3)

            nacc = [0]
            cacc = [sq[i] for i in range(4)]
            cfree = [[(V.sem, V.sem.n)] for _ in range(4)]
            for sl in range(4):
                s = load(w2[:, 584 + sl * 256:584 + sl * 256 + 256], 8, 256)
                for jj in range(2):
                    j = 2 * sl + jj
                    b = bank()
                    for k in range(8):
                        t = mm(b, b.ap[:, :], s.ap[:, k, jj * 128:jj * 128 + 128], xn[:, k, :], start=(k == 0),
                               stop=(k == 7), waits=(s.tok,), inc=(k == 7))
                    if jj == 1:
                        done(s, t)
                    i = nacc[0] % 4
                    nacc[0] += 1
                    a = cacc[i]
                    t = act(a, b.ap[:, :], ACT.Identity, t, *cfree[i], bias=pc("conv_b_2", 8 * l + j),
                            scale=pc("conv_w_2", 32 * l + 24 + j))
                    for sh in (3, 2, 1):
                        t = stt(a[:, sh:512], b.ap[:, 0:512 - sh], pc("conv_w_2", 32 * l + (3 - sh) * 8 + j),
                                a[:, sh:512], ALU.mult, ALU.add, t)
                    b.free(t)
                    dst = mq[:, j, :] if j < 4 else mk[:, j - 4, :]
                    t = act(dst, a, ACT.Silu, t)
                    cfree[i] = [t]
            for sl in range(2):
                s = load(w2[:, 1608 + sl * 256:1608 + sl * 256 + 256], 8, 256)
                for c in range(4):
                    b = bank()
                    for k in range(8):
                        t = mm(b, b.ap[:, 0:256], xn[:, k, c * 128:c * 128 + 128], s.ap[:, k, :], start=(k == 0),
                               stop=(k == 7), waits=(s.tok,), inc=(k == 7))
                    if c == 3:
                        done(s, t)
                    t = evac(mv[:, c, sl * 256:sl * 256 + 256], b.ap[:, 0:256], t, t_i)
                    b.free(t)
            for sl in range(2):
                s = load(w2[:, 2120 + sl * 256:2120 + sl * 256 + 256], 8, 256)
                for jj in range(2):
                    j = 2 * sl + jj
                    b = bank()
                    for k in range(8):
                        t = mm(b, b.ap[:, :], s.ap[:, k, jj * 128:jj * 128 + 128], xn[:, k, :], start=(k == 0),
                               stop=(k == 7), waits=(s.tok,), inc=(k == 7))
                    if jj == 1:
                        done(s, t)
                    t = act(mo[:, j, :], b.ap[:, :], ACT.Sigmoid, t)
                    b.free(t)
            s = load(w2[:, 2632:2640], 8, 8)
            for o, dst, bcol in ((0, ir, l), (4, fr, 2 + l)):
                b = bank()
                for k in range(8):
                    t = mm(b, b.ap[0:4, :], s.ap[:, k, o:o + 4], xn[:, k, :], start=(k == 0), stop=(k == 7),
                           waits=(s.tok,), inc=(k == 7))
                t = ts(dst[0:4, :], b.ap[0:4, :], gb[0:4, bcol:bcol + 1], None, ALU.add, None, t, t_gb)
                b.free(t)
            done(s, (E.sem, E.sem.n))

            fence()
            xa = [xn_t[:, i * 2048:i * 2048 + 2048] for i in range(2)]
            qT = xa[0].rearrange("p (j t) -> p j t", j=4)
            iT = xa[1].rearrange("p (j t) -> p j t", j=4)
            kT = [ct.rearrange("p c n -> p (c n)")[:, 0:512], ct.rearrange("p c n -> p (c n)")[:, 512:1024]]
            ikT = ctT[:, 0, :]
            for j in range(4):
                for src, dst in ((qt, qT), (it, iT)):
                    b = bank()
                    for c in range(4):
                        t = tr(b, b.ap[:, c * 128:c * 128 + 128], src[:, c, j * 128:j * 128 + 128], inc=(c == 3))
                    t = evac(dst[:, j, :], b.ap[:, :], t)
                    b.free(t)
            for src, o, dst in ((kt, 0, kT[0]), (kt, 128, kT[1]), (ikt, 0, ikT)):
                b = bank()
                for c in range(4):
                    t = tr(b, b.ap[:, c * 128:c * 128 + 128], src[:, c, o:o + 128], inc=(c == 3))
                t = evac(dst, b.ap[:, :], t)
                b.free(t)

            fence()
            qf_ = qt.rearrange("p c n -> p (c n)")
            lg, mrow, thr, e2r = [qf_[0:4, i * 512:i * 512 + 512] for i in range(4)]
            f4, i4r, e4 = fr[0:4, :], ir[0:4, :], er[0:4, :]
            softplus(lg, f4, e4, e2r, -1.0)
            ts(lg, lg, -1.0, None, ALU.mult, None)
            one = sq[0][0:4, :]
            V.do(lambda e: e.memset(one, 1.0))
            V.do(lambda e: e.tensor_tensor_scan(f4, one, lg, 0.0, ALU.mult, ALU.add))
            tt(i4r, i4r, f4, ALU.subtract)
            V.do(lambda e: e.tensor_tensor_scan(mrow, one, i4r, 0.0, ALU.mult, ALU.max))
            t = tt(thr, f4, mrow, ALU.add)
            t_thr = act(thr, thr, ACT.Exp, t, scale=-1.0)
            b = bank()
            for c in range(4):
                t2 = tr(b, b.ap[:, c * 4:c * 4 + 4], i4r[:, c * 128:c * 128 + 128], waits=(t,), inc=(c == 3))
            aT = st8[:, 0:16]
            t_aT = cp(aT, b.ap[:, 0:16], t2)
            b.free(t_aT)

            i_flat = it.rearrange("p c n -> p (c n)")
            work = i_flat[:, 0:512]
            rl = [i_flat[:, 512:1024], i_flat[:, 1024:1536]]
            rl_free = [[], []]
            m8 = st8[:, 32:40]
            pens = {0: cc("pen")}
            scb = [mark + 0]
            score_bufs = [kt.rearrange("p c n -> p (c n)")[:, 0:512], kt.rearrange("p c n -> p (c n)")[:, 512:1024],
                          i_flat[:, 1536:2048]]
            n = 0
            for c in (1, 2, 3):
                W = 128 * (c + 1)
                sc = score_bufs[c - 1]
                for hh in range(8):
                    o = 64 * (hh % 2)
                    b = bank()
                    t = mm(b, b.ap[:, 0:W], iT[o:o + 64, hh // 2, c * 128:c * 128 + 128], ikT[o:o + 64, 0:W], inc=True)
                    i = n % 2
                    n += 1
                    t = act(rl[i][:, 0:W], b.ap[:, 0:W], ACT.Relu, t, *rl_free[i])
                    b.free(t)
                    if hh == 0:
                        t = ts(sc[:, 0:W], rl[i][:, 0:W], iw[:, c, 0:1], None, ALU.mult, None, t)
                    else:
                        t = stt(sc[:, 0:W], rl[i][:, 0:W], iw[:, c, hh:hh + 1], sc[:, 0:W], ALU.mult, ALU.add, t)
                    rl_free[i] = [t]
                tt(sc[:, W - 128:W], sc[:, W - 128:W], cc("neg"), ALU.add)
                for r_ in range(16):
                    src = sc if r_ == 0 else work
                    V.do(lambda e, src=src, W=W: e.max(m8, src[:, 0:W]))
                    V.do(lambda e, src=src, W=W: e.match_replace(work[:, 0:W], m8, src[:, 0:W], GONE))
                tt(sc[:, 0:W], work[:, 0:W], sc[:, 0:W], ALU.is_equal)
                t_pen = ts(sc[:, 0:W], sc[:, 0:W], PEN, None, ALU.mult, None)
                pens[c] = sc

            f = fence()
            o_t = qf_.rearrange("p (c n) -> p c n", c=4)
            sm = [i_flat[:, 0:512], i_flat[:, 512:1024], sq[0], sq[1]]
            PT = [i_flat[:, 1024:1536], sq[2], sq[3]]
            mx, rsum = st8[:, 32:40], st8[:, 40:48]
            sm_free = [[] for _ in sm]
            PT_free = [[] for _ in PT]
            np_ = 0
            ofree = []
            o_buf = ctT[:, 1, :]
            for c in range(4):
                W = 128 * (c + 1)
                bo = bank(long=True)

                def scores(hh):
                    o = 64 * (hh % 2)
                    b = bank()
                    t = mm(b, b.ap[:, 0:W], qT[o:o + 64, hh // 2, c * 128:c * 128 + 128],
                           kT[hh // 4][o:o + 64, 0:W], inc=True)
                    i = hh % 4
                    t = tt(sm[i][:, 0:W], b.ap[:, 0:W], pens[c][:, 0:W], ALU.add, t, *sm_free[i])
                    b.free(t)
                    V.do(lambda e, W=W: e.tensor_reduce(mx[:, hh:hh + 1], sm[i][:, 0:W], X, ALU.max))
                    t = ts(mx[:, hh:hh + 1], mx[:, hh:hh + 1], -0.125, None, ALU.mult, None)
                    return act(sm[i][:, 0:W], sm[i][:, 0:W], ACT.Exp, t, bias=mx[:, hh:hh + 1], scale=0.125,
                               accum=rsum[:, hh:hh + 1])

                te = {0: scores(0), 1: scores(1)}
                for hh in range(8):
                    if hh + 2 < 8:
                        te[hh + 2] = scores(hh + 2)
                    i = hh % 4
                    b = bank()
                    for kb in range(c + 1):
                        t = tr(b, b.ap[:, kb * 128:kb * 128 + 128], sm[i][:, kb * 128:kb * 128 + 128],
                               waits=(te[hh],), inc=(kb == c))
                    sm_free[i] = [t]
                    p = np_ % 3
                    np_ += 1
                    t = evac(PT[p][:, 0:W], b.ap[:, 0:W], t, *PT_free[p])
                    b.free(t)
                    for kb in range(c + 1):
                        t2 = mm(bo, bo.ap[:, hh * 64:hh * 64 + 64], PT[p][:, kb * 128:kb * 128 + 128],
                                vt[:, kb, (hh // 4) * 64:(hh // 4) * 64 + 64], start=(kb == 0), stop=(kb == c),
                                waits=(t,), inc=(kb == c))
                    PT_free[p] = [t2]
                V.do(lambda e: e.reciprocal(rsum, rsum), te[7])
                t = tt(v8(o_buf), v8(bo.ap[:, :]), bc8(rsum), ALU.mult, t2, *ofree)
                bo.free(t)
                b = bank()
                for j in range(4):
                    t2 = tr(b, b.ap[:, j * 128:j * 128 + 128], o_buf[:, j * 128:j * 128 + 128], waits=(t,), inc=(j == 3))
                ofree = [t2]
                t = evac(mix[:, 0:4, c * 128:c * 128 + 128], b.ap[:, :].rearrange("p (j t) -> p j t", j=4), t2)
                b.free(t)
                S.wait((V.sem, V.sem.n))

            f = fence()
            dm = [i_flat[:, 0:512], i_flat[:, 512:1024]]
            pp = [i_flat[:, 1024:1536], sq[0]]
            dm_free, pp_free = [[], []], [[], []]
            n = 0
            for hh in range(4):
                bm = bank()
                t_m = mm(bm, bm.ap[:, :], con[0:4, cat["sel"] + hh * 128:cat["sel"] + hh * 128 + 128], mrow, inc=True)
                bn, bden = bank(long=True), bank(long=True)
                for j in range(4):
                    W = 512 - 128 * j
                    i = n % 2
                    n += 1
                    bs_ = bank()
                    t_s = mm(bs_, bs_.ap[:, 0:W], mk[:, hh, j * 128:j * 128 + 128], mq[:, hh, 128 * j:512], inc=True)
                    t = ts(dm[i][:, 0:W], bm.ap[:, 128 * j:512], aT[:, 4 * j + hh:4 * j + hh + 1], 0.0, ALU.subtract,
                           ALU.max, t_m, *dm_free[i])
                    if j == 3:
                        bm.free(t)
                    t = act(dm[i][:, 0:W], dm[i][:, 0:W], ACT.Exp, t, scale=-1.0)
                    t = stt(pp[i][:, 0:W], bs_.ap[:, 0:W], float(128 ** -0.5), dm[i][:, 0:W], ALU.mult, ALU.mult, t,
                            t_s, *pp_free[i])
                    bs_.free(t)
                    dm_free[i] = [t]
                    t = tt(pp[i][:, 0:128], pp[i][:, 0:128], ule, ALU.mult)
                    mm(bden, bden.ap[:, 128 * j:512], ones, pp[i][:, 0:W], start=(j == 0), stop=(j == 3), waits=(t,))
                    t_n = mm(bn, bn.ap[:, 128 * j:512], mv[:, j, hh * 128:hh * 128 + 128], pp[i][:, 0:W],
                             start=(j == 0), stop=(j == 3), inc=True)
                    pp_free[i] = [t_n]
                bt = bank()
                t_t = mm(bt, bt.ap[:, :], con[0:4, cat["sel"] + hh * 128:cat["sel"] + hh * 128 + 128], thr,
                         waits=(t_thr,), inc=True)
                hm = mk[:, hh, :]
                t = act(hm, bden.ap[:, :], ACT.Abs, t_n)
                bden.free(t)
                t = tt(hm, hm, bt.ap[:, :], ALU.max, t, t_t)
                bt.free(t)
                V.do(lambda e, hm=hm: e.reciprocal(hm, hm))
                t = tt(hm, hm, bn.ap[:, :], ALU.mult)
                bn.free(t)
            for hh in range(4):
                hm = mk[:, hh, :]
                t = act(mq[:, hh, :], hm, ACT.Square, (V.sem, V.sem.n))
                b = bank()
                t = mm(b, b.ap[:, :], ones, mq[:, hh, :], waits=(t,), inc=True)
                t = act(mq[:, hh, :], b.ap[:, :], ACT.Sqrt, t, bias=eps[:, 0:1], scale=1.0 / 128)
                b.free(t)
                V.do(lambda e, hh=hh: e.reciprocal(mq[:, hh, :], mq[:, hh, :]), t)
                stt(hm, hm, pc("g_mh_2", 4 * l + hh), mq[:, hh, :], ALU.mult, ALU.mult)
                t = tt(mix[:, 4 + hh, :], hm, mo[:, hh, :], ALU.mult)
            f = fence()

            def add_h(j, b, t):
                t = tt(h[:, j, :], h[:, j, :], b.ap[:, :], ALU.add, t)
                b.free(t)
                add_h.toks[j] = t

            add_h.toks = [None] * 8
            project(A["w_out_2"][l], 8, lambda k: mix[:, k, :], add_h)
            t_h = add_h.toks

            reset(0)
            sq = [tmp(512) for _ in range(4)]
            rs = tmp(512)
            t_xn = rms("g_mlp_2", l)
            E.wait(t_xn[7])
            U = tmp(16384).rearrange("p (j t) -> p j t", j=32)
            wf1 = A["w_ff1_2"][l]
            rfree = [[] for _ in range(4)]
            for sl in range(16):
                s = load(wf1[:, sl * 256:sl * 256 + 256], 8, 256)
                for jj in range(2):
                    j = 2 * sl + jj
                    b = bank()
                    for k in range(8):
                        t = mm(b, b.ap[:, :], s.ap[:, k, jj * 128:jj * 128 + 128], xn[:, k, :], start=(k == 0),
                               stop=(k == 7), waits=(s.tok,), inc=(k == 7))
                    if jj == 1:
                        done(s, t)
                    i = j % 4
                    t = act(sq[i], b.ap[:, :], ACT.Relu, t, *rfree[i])
                    b.free(t)
                    t = tt(U[:, j, :], sq[i], sq[i], ALU.mult, t)
                    rfree[i] = [t]
            E.wait(t)
            add_h.toks = [None] * 8
            project(A["w_ff2_2"][l], 32, lambda k: U[:, k, :], add_h)
            t_h = add_h.toks
            f = fence()
            t_xn = rms("g_ple_2", l)
            pst = U[:, 0:2, :].rearrange("p j t -> p (j t)").rearrange("p (c d) -> p c d", c=4)
            pT = U[:, 2:4, :]
            t_p = S.dma(s_p, lambda e, l=l: e.dma_start(pst, A["p_2"][l].rearrange("a (c p) d -> p (a c) d", p=128)))
            for k in range(2):
                b = bank()
                for c in range(4):
                    t = tr(b, b.ap[:, c * 128:c * 128 + 128], pst[:, c, k * 128:k * 128 + 128], waits=(t_p,),
                           inc=(c == 3))
                t_pT = evac(pT[:, k, :], b.ap[:, :], t)
                b.free(t_pT)
                E.wait(t_pT)
            sp_ = load(A["w_ple_2"][l], 2, 1024)
            gates = U[:, 4:6, :]
            gfree = [[], []]

            def gate_fn(j, b, t):
                g = gates[:, j % 2, :]
                t = act(g, b.ap[:, :], ACT.Sigmoid, t, *gfree[j % 2], bias=pc("b_ple_gate_2", 8 * l + j))
                b.free(t)
                b2 = bank()
                for k in range(2):
                    t2 = mm(b2, b2.ap[:, :], sp_.ap[:, k, j * 128:j * 128 + 128], pT[:, k, :], start=(k == 0),
                            stop=(k == 1), waits=(sp_.tok,), inc=(k == 1))
                if j == 7:
                    done(sp_, t2)
                t = tt(g, g, b2.ap[:, :], ALU.mult, t, t2)
                b2.free(t)
                add_h.toks[j] = tt(h[:, j, :], h[:, j, :], g, ALU.add)
                gfree[j % 2] = [add_h.toks[j]]

            add_h.toks = [None] * 8
            E.wait(t_xn[7])
            project(A["w_ple_gate_2"][l], 8, lambda k: xn[:, k, :], gate_fn)
            t_h = add_h.toks
            fence()

        reset(0)
        ot = tmp(4096).rearrange("p (c d) -> p c d", c=4)
        for c in range(4):
            for jj in range(2):
                b = bank()
                for q in range(4):
                    j = 4 * jj + q
                    t = tr(b, b.ap[:, q * 128:q * 128 + 128], h[:, j, c * 128:c * 128 + 128], waits=(t_h[j],),
                           inc=(q == 3))
                t = evac(ot[:, c, jj * 512:jj * 512 + 512], b.ap[:, :], t)
                b.free(t)
                D.wait(t)
            t_out = D.dma(s_out, lambda e, c=c: e.dma_start(out[0, c * 128:c * 128 + 128, :], ot[:, c, :]))
        D.wait(t_out)

        block = ctx.enter_context(nc.Block())

        @block.sync
        def _(eng):
            D.play(eng)

        @block.gpsimd
        def _(eng):
            G.play(eng)

        @block.scalar
        def _(eng):
            S.play(eng)

        @block.tensor
        def _(eng):
            E.play(eng)

        @block.vector
        def _(eng):
            V.play(eng)


_INS = ["x", "c", "ctx", "c_ctx", "w_ada", "b_ada", "w_in", "ssd_conv_w", "ssd_conv_b", "ssd_dt_bias", "ssd_a_log",
        "ssd_d", "ssd_norm_w", "fnet_w", "pool_w", "pool_scale", "w_out", "ln1_g", "ln1_b", "ffn_w_up", "ffn_conv_w",
        "ffn_conv_b", "ffn_w_down", "ln2_g", "ln2_b", "p_2", "positions_2", "g_mix_2", "w_in_2", "g_cq_2",
        "w_q_up_2", "w_iq_up_2", "g_qn_2", "g_kn_2", "g_ik_2", "conv_w_2", "conv_b_2", "i_bias_2", "f_bias_2",
        "g_mh_2", "w_out_2", "g_mlp_2", "w_ff1_2", "w_ff2_2", "g_ple_2", "w_ple_gate_2", "b_ple_gate_2", "w_ple_2"]
_FLAT = {1: "", 2: "a b -> (a b)", 3: "a b c -> (a b c)", 4: "a b c d -> (a b c d)"}


def kernel(**inputs):
    import concourse.bacc as _bacc
    from concourse.bass_utils import run_bass_kernel_spmd as _run

    nc = _bacc.Bacc("TRN2", target_bir_lowering=False, num_devices=1)
    arrays, A = {}, {"_flat": {}}
    for name in _INS:
        a = np.ascontiguousarray(inputs[name])
        arrays[f"in_{name}_dram"] = a
        A[name] = nc.dram_tensor(f"in_{name}_dram", a.shape, mybir.dt.from_np(a.dtype), kind="ExternalInput").ap()
        A["_flat"][name] = _FLAT[a.ndim]
    for name, a in const_arrays().items():
        arrays[f"in_{name}_dram"] = a
        A[name] = nc.dram_tensor(f"in_{name}_dram", a.shape, F32, kind="ExternalInput").ap()
    out = nc.dram_tensor("out_0_dram", (1, T, 1024), F32, kind="ExternalOutput").ap()
    build(nc, A, out)
    r = _run(nc, [arrays], core_ids=[0])
    return r.results[0]["out_0_dram"]
```

```python
from contextlib import ExitStack

import numpy as np
import concourse.bass as bass
from concourse import mybir

ALU = mybir.AluOpType
ACT = mybir.ActivationFunctionType
F32 = mybir.dt.float32
I32 = mybir.dt.int32
F32R = mybir.dt.float32r
X = mybir.AxisListType.X

T = 512
TC = 256
EPS = 1e-6
ALPHA = 2.0 ** 0.25
NEG = -3.0e38
GONE = -3.3e38
PEN = -1.0e30
FF1 = 2816
FF2 = 4096
NSLOT = 2
SLOT = 2048
TWO_PI = 2.0 * np.pi
C1 = 6.28125
C2 = float(np.float32(np.floor((TWO_PI - 6.28125) * 2.0 ** 20) / 2.0 ** 20))
C3 = float(np.float32(TWO_PI - 6.28125 - C2))
MAGIC = 12582912.0


def const_layout():
    names = [("ident", 128), ("ule", 128), ("uge", 128), ("ugt", 128), ("ult", 128), ("ones", 128),
             ("mean", 128), ("neg", 128), ("pen", 128), ("freq", 8)]
    at, n = {}, 0
    for name, w in names:
        at[name] = n
        n += w
    return at, n


def const_arrays():
    at, n = const_layout()
    c = np.zeros((128, n), np.float32)
    p = np.arange(128)[:, None]
    f = np.arange(128)[None, :]

    def put(name, v):
        v = np.asarray(v, np.float32)
        c[:v.shape[0], at[name]:at[name] + v.shape[1]] = v

    put("ident", p == f)
    put("ule", p <= f)
    put("uge", p >= f)
    put("ugt", p > f)
    put("ult", p < f)
    put("ones", np.ones((128, 128)))
    put("mean", np.full((128, 128), 1.0 / 1024))
    put("neg", np.where(f <= p, 0.0, NEG))
    put("pen", np.where(f <= p, 0.0, PEN))
    q = np.arange(64)
    ang = 2 * np.pi * (np.outer(q, q) % 64) / 64
    d = np.zeros((128, 256))
    for g in range(2):
        d[g * 64:g * 64 + 64, g * 64:g * 64 + 64] = np.cos(ang) / 8
        d[g * 64:g * 64 + 64, 128 + g * 64:128 + g * 64 + 64] = np.sin(ang) / 8
    c1 = np.zeros((128, 1280), np.float32)
    c1[:, 0:256] = d
    pos = np.arange(T)
    inv = np.zeros((128, 1024))
    for g, w in enumerate((2, 4, 8, 16)):
        left = w // 2
        hi = np.minimum(pos + w - left, T)
        lo = np.maximum(pos - left, 0)
        i, half = g // 2, g % 2
        inv[half * 64:half * 64 + 64, i * 512:i * 512 + 512] = 1.0 / (hi - lo)
    c1[:, 256:1280] = inv
    fr = np.float32(500000.0) ** (-(np.arange(8, dtype=np.float32) * np.float32(2.0)) / np.float32(16))
    put("freq", np.broadcast_to(fr[None, :], (128, 8)))
    k = np.arange(T)
    a = 2 * np.pi * (np.outer(k, k) % T) / T
    dl = np.stack([np.cos(a), -np.sin(a)]).astype(np.float64) / np.sqrt(512.0)
    return {"consts": c, "consts1": c1, "dftl": dl.astype(np.float32)}


PARAMS = [("c", 8), ("c_ctx", 8), ("b_ada", 48), ("ssd_conv_w", 24), ("ssd_conv_b", 8), ("ssd_norm_w", 4),
          ("pool_scale", 2), ("ln1_g", 8), ("ln1_b", 8), ("ffn_conv_w", 396), ("ffn_conv_b", 44), ("ln2_g", 8),
          ("ln2_b", 8), ("g_mix_2", 16), ("g_cq_2", 4), ("conv_w_2", 64), ("conv_b_2", 16), ("g_mh_2", 8),
          ("g_mlp_2", 16), ("g_ple_2", 16), ("b_ple_gate_2", 16)]
ROWS = [("ssd_dt_bias", 16), ("ssd_a_log", 16), ("ssd_d", 8), ("g_qn_2", 128), ("g_kn_2", 128), ("g_ik_2", 128)]


def offsets(table):
    at, n = {}, 0
    for name, w in table:
        at[name] = n
        n += w
    return at, n


OWN = object()


class Sem:

    def __init__(self, h):
        self.h, self.n = h, 0

    def add(self, k):
        self.n += k
        return (self, self.n)


class Eng:

    def __init__(self, sem, chain):
        self.sem, self.chain, self.q, self.seen = sem, chain, [], {}

    def wait(self, *toks):
        for t in toks:
            if t is None or t is OWN:
                continue
            if isinstance(t, list):
                self.wait(*t)
                continue
            s, v = t
            if self.seen.get(id(s), 0) < v:
                self.seen[id(s)] = v
                self.q.append(("w", s.h, v))

    def do(self, fn, *toks, inc=True):
        self.wait(*toks)
        if self.chain and self.sem.n and OWN not in toks:
            self.wait((self.sem, self.sem.n))
        if inc:
            self.q.append(("i", fn, self.sem.h, 1))
            return self.sem.add(1)
        self.q.append(("i", fn, None, 0))
        return None

    def dma(self, sem, fn, *toks):
        self.wait(*toks)
        self.q.append(("i", fn, sem.h, 16))
        return sem.add(16)

    def play(self, eng):
        for it in self.q:
            if it[0] == "w":
                eng.wait_ge(it[1], it[2])
            else:
                ins = it[1](eng)
                if it[2] is not None:
                    ins.then_inc(it[2], it[3])


class Bank:
    def __init__(self, ap):
        self.ap, self.toks, self.idle, self.age = ap, [], True, 0

    def free(self, *toks):
        Bank.now += 1
        self.toks, self.idle, self.age = list(toks), True, Bank.now


Bank.now = 0


def in_step(units):
    live = []
    units = list(units)
    while units or live:
        for u in list(live):
            if next(u, "end") == "end":
                live.remove(u)
        if units:
            u = units.pop(0)()
            next(u, None)
            live.append(u)
        yield


def build(nc, A, out):
    cat, cn = const_layout()
    pat, pn = offsets(PARAMS)
    rat, rn = offsets(ROWS)
    NPT = (pn + 127) // 128

    with ExitStack() as ctx:
        def sb(name, n, dt=F32, p=128):
            return ctx.enter_context(nc.sbuf_tensor(name, [p, n], dt))

        sems = {}

        def sem(name):
            sems[name] = Sem(ctx.enter_context(nc.semaphore(name)))
            return sems[name]

        V = Eng(sem("s_dve"), True)
        S = Eng(sem("s_act"), True)
        G = Eng(sem("s_pool"), True)
        E = Eng(sem("s_pe"), False)
        D = Eng(sem("s_sp"), False)
        s_slot = [sem(f"s_slot{i}") for i in range(NSLOT)]
        s_con, s_wq, s_con1, s_par, s_row, s_x, s_cx, s_fw, s_pw, s_gb, s_pos, s_p, s_out = [
            sem(n) for n in ("s_con", "s_wq", "s_con1", "s_par", "s_row", "s_x", "s_cx", "s_fw", "s_pw", "s_gb", "s_pos", "s_p",
                             "s_out")]

        h_t = sb("h", 4096)
        xh_t = sb("xh", 4096, F32R)
        xl_t = sb("xl", 4096, F32R)
        wh_t = sb("wh", 2 * SLOT, F32R)
        wl_t = sb("wl", 2 * SLOT, F32R)
        mix_t = sb("mix", 4096)
        ring = sb("ring", NSLOT * SLOT)
        con = sb("con", cn)
        par = sb("par", pn)
        rb = sb("rb", rn)
        mod = sb("mod", 96)
        fw = sb("fw", 128)
        pw = sb("pw", 128)
        gb = sb("gb", 8)
        posi = sb("posi", 4, I32)
        rope = sb("rope", 64)
        eps = sb("eps", 2)
        scope = [ctx.enter_context(ExitStack()), ctx.enter_context(ExitStack())]
        small = sb("small", 1024)
        arena_n = [0, 0, None]

        def region(name, n, dt=F32, lvl=0):
            return scope[lvl].enter_context(nc.sbuf_tensor(name, [128, n], dt))

        def close(lvl):
            for i in range(1, lvl - 1, -1):
                scope[i].close()
                scope[i] = ctx.enter_context(ExitStack())

        def use(t, n, at=0):
            arena_n[0], arena_n[1], arena_n[2] = at, n, t

        def reset(to=0):
            arena_n[0] = to

        def tmp(n):
            a = arena_n[0]
            arena_n[0] += n
            assert arena_n[0] <= arena_n[1], arena_n[0]
            return arena_n[2][:, a:a + n]

        h = h_t[:, :].rearrange("p (j t) -> p j t", j=8)
        xh = xh_t[:, :].rearrange("p (j t) -> p j t", j=8)
        xl = xl_t[:, :].rearrange("p (j t) -> p j t", j=8)
        mix = mix_t[:, :].rearrange("p (j t) -> p j t", j=8)

        def cc(name, w=128, p=128):
            return con[0:p, cat[name]:cat[name] + w]

        ident, ule, uge, ones = cc("ident"), cc("ule"), cc("uge"), cc("ones")

        def pc(name, j, w=1):
            return par[:, pat[name] + j:pat[name] + j + w]

        def row(name, o, w):
            return rb[:, rat[name] + o:rat[name] + o + w]

        banks = [Bank(ctx.enter_context(nc.psum_tensor(f"ps{i}", [128, 512], F32))) for i in range(8)]
        turn = [0]

        def bank():
            b = min((x for x in banks if x.idle), key=lambda x: x.age)
            b.idle = False
            return b

        def mm(b, out_ap, lhsT, rhs, start=True, stop=True, waits=(), inc=False):
            if start:
                E.wait(*b.toks)
            return E.do(lambda e: e.matmul(out_ap, lhsT, rhs, start=start, stop=stop), *waits, inc=inc)

        def tr(b, out_ap, src, waits=(), inc=False):
            p = src.shape[0]
            E.wait(*b.toks)
            return E.do(lambda e: e.transpose(out_ap, src, con[0:p, cat["ident"]:cat["ident"] + p]), *waits, inc=inc)

        def act(out_ap, in_ap, func, *toks, bias=0.0, scale=1.0, accum=None):
            if accum is None:
                return S.do(lambda e: e.activation(out_ap, in_ap, func, bias=bias, scale=scale), *toks)
            return S.do(lambda e: e.activation(out_ap, in_ap, func, bias=bias, scale=scale, accum_out=accum), *toks)

        def tt(out_ap, a, b, op, *toks, eng=None):
            return (eng or V).do(lambda e: e.tensor_tensor(out_ap, a, b, op), *toks)

        def ts(out_ap, a, s1, s2, op0, op1, *toks, eng=None):
            if op1 is None:
                return (eng or V).do(lambda e: e.tensor_scalar(out_ap, a, s1, None, op0), *toks)
            return (eng or V).do(lambda e: e.tensor_scalar(out_ap, a, s1, s2, op0, op1), *toks)

        def stt(out_ap, a, s, b, op0, op1, *toks):
            return V.do(lambda e: e.scalar_tensor_tensor(out=out_ap, in0=a, scalar=s, in1=b, op0=op0, op1=op1), *toks)

        def recip(out_ap, a, *toks):
            return V.do(lambda e: e.reciprocal(out_ap, a), *toks)

        def reduce(out_ap, a, op, *toks):
            return V.do(lambda e: e.tensor_reduce(out_ap, a, X, op), *toks)

        def fill(out_ap, v, *toks):
            return V.do(lambda e: e.memset(out_ap, v), *toks)

        def scan(out_ap, one, a, op):
            return V.do(lambda e: e.tensor_tensor_scan(out_ap, one, a, 0.0, ALU.mult, op))

        def top8(m8, a):
            return V.do(lambda e: e.max(m8, a))

        def drop8(out_ap, m8, a):
            return V.do(lambda e: e.match_replace(out_ap, m8, a, GONE))

        def cp(out_ap, a, *toks, eng=None):
            if eng is S:
                return act(out_ap, a, ACT.Copy, *toks)
            return (eng or V).do(lambda e: e.tensor_copy(out_ap, a), *toks)

        def fence():
            now = [(e.sem, e.sem.n) for e in (V, S, G, E) if e.sem.n]
            for e in (V, S, G, E):
                e.wait(*now)
            return now

        class Load:
            pass

        loads = []
        order = []
        head = [0, 0, 0, 0]

        def plan(src, kt, w, split=True, halves=(0, 1)):
            s = Load()
            s.src, s.kt, s.w, s.split, s.users, s.toks, s.tok = src, kt, w, split, (2 if split and w > 128 else 1), [], None
            loads.append(s)
            if split:
                s.at = head[2] % 2
                head[2] += 1
                s.part = {}
                for hf in halves[:s.users]:
                    order.append((s, hf))
            return s

        split_free = [[[], []], [[], []]]

        def pump():
            while head[0] < len(loads):
                i = head[0]
                if i >= NSLOT and loads[i - NSLOT].users:
                    return
                s = loads[i]
                prev = loads[i - NSLOT].toks if i >= NSLOT else []
                o = i % NSLOT * SLOT
                s.ap = ring[:, o:o + s.kt * s.w].rearrange("p (k n) -> p k n", k=s.kt)
                v = s.src.rearrange("(k p) n -> p k n", p=128)
                s.tok = D.dma(s_slot[i % NSLOT], lambda e, s=s, v=v: e.dma_start(s.ap, v), *prev)
                head[0] += 1

        lo_eng = [None]
        x_read = [None]

        def split_next():
            s, hf = order[head[1]]
            if s.tok is None:
                return False
            head[1] += 1
            a, w = 128 * hf, min(128, s.w - 128 * hf)
            wide = 256 if s.w > 128 else s.w
            o = s.at * SLOT
            hi = wh_t[:, o:o + s.kt * wide].rearrange("p (k n) -> p k n", k=s.kt)
            lo = wl_t[:, o:o + s.kt * wide].rearrange("p (k n) -> p k n", k=s.kt)
            both = split_free[s.at]
            fr = both[hf] if s.w > 128 else both[0] + both[1]
            t1 = act(hi[:, :, a:a + w], s.ap[:, :, a:a + w], ACT.Copy, s.tok, *fr)
            t2 = tt(lo[:, :, a:a + w], s.ap[:, :, a:a + w], hi[:, :, a:a + w].bitcast(F32), ALU.subtract, t1, s.tok,
                    *fr, eng=lo_eng[0])
            both[hf] = None
            if s.w <= 128:
                both[1] = None
            s.hi, s.lo = hi, lo
            s.part[hf] = [t1, t2]
            s.toks += [t1, t2]
            s.users -= 1
            pump()
            return True

        def need(s, hf, ahead=3):
            pump()
            while hf not in s.part:
                assert split_next()
            for _ in range(ahead):
                if head[1] >= len(order):
                    break
                n, nh = order[head[1]]
                fr = split_free[n.at]
                if n.tok is None or fr[nh] is None or (n.w <= 128 and fr[1] is None):
                    break
                split_next()
            return s.part[hf]

        def freed(s, hf, tok):
            split_free[s.at][hf] = [tok]
            if s.w <= 128:
                split_free[s.at][1] = [tok]

        def raw(s):
            pump()
            assert s.tok is not None
            return s

        def done(s, tok):
            s.toks.append(tok)
            s.users -= 1
            pump()

        def mm3(b, out_ap, a, x, start, stop, waits=(), inc=False):
            mm(b, out_ap, a[0], x[0], start=start, stop=False, waits=waits)
            mm(b, out_ap, a[0], x[1], start=False, stop=False)
            return mm(b, out_ap, a[1], x[0], start=False, stop=stop, inc=inc)

        t_con = D.dma(s_con, lambda e: e.dma_start(con[:, :], A["consts"]))
        N1 = 16240
        arena = region("arena", N1)
        use(arena, N1)
        csil = tmp(16).rearrange("p (k w) -> p k w", w=2)
        arow = [tmp(512), tmp(512)]
        con1 = tmp(1280)
        t_con1 = S.dma(s_con1, lambda e: e.dma_start(con1, A["consts1"]))
        lo = arena_n[0]
        stage = tmp(NPT * 128)
        w_in, w_up, w_dn = A["w_in"][0], A["ffn_w_up"][0], A["ffn_w_down"][0]
        GR = (8, 8, 6)

        def cols_of(W, o, n, w=256):
            return [plan(W[:, o + i * w:o + i * w + w], 8, w) for i in range(n)]

        def plan_ada(n):
            return [plan(A["w_ada"][0, :, i * 256:i * 256 + 256], 8, 256, split=False) for i in n]

        L_ada = plan_ada(range(8))
        L_xbc = cols_of(w_in, 512, 4)
        L_dt = plan(w_in[:, 1536:1552], 8, 16)
        L_z = cols_of(w_in, 0, 2)
        L_fp = cols_of(w_in, 1552, 2)
        L_dft = [plan(A["dftl"][i], 4, 512, split=False) for i in range(2)]
        L_ada += plan_ada(range(8, 24))
        L_wout = cols_of(A["w_out"][0], 0, 4)

        def plan_up(g):
            out_ = []
            for jp in range(GR[g] // 2):
                o = (sum(GR[:g]) // 2 + jp) * 256
                n0 = len(order)
                sg = plan(w_up[:, FF1 + o:FF1 + o + 256], 8, 256)
                sv = plan(w_up[:, o:o + 256], 8, 256)
                order[n0:] = [(sg, 0), (sv, 0), (sg, 1), (sv, 1)]
                out_.append((sg, sv))
            return out_

        def plan_down(W, k0, kt):
            return [plan(W[k0 * 128:(k0 + kt) * 128, i * 256:i * 256 + 256], kt, 256) for i in range(4)]

        L_up, L_dn = [None] * 3, [None] * 3
        for kind, g in (("u", 0), ("u", 1), ("d", 0), ("u", 2), ("d", 1), ("d", 2)):
            if kind == "u":
                L_up[g] = plan_up(g)
            else:
                L_dn[g] = plan_down(w_dn, sum(GR[:g]), GR[g])
        L2 = []
        for l in range(2):
            n = Load()
            w2 = A["w_in_2"][l]
            n.tok_ = cols_of(w2, 0, 3)
            n.mqk = cols_of(w2, 584, 4)
            n.mv = cols_of(w2, 1608, 2)
            n.gate = plan(w2[:, 2632:2640], 8, 8)
            n.mo = cols_of(w2, 2120, 2)
            n.wout = cols_of(A["w_out_2"][l], 0, 4)
            n.up, n.dn = [None] * 4, [None] * 4
            for kind, g in (("u", 0), ("u", 1), ("d", 0), ("u", 2), ("d", 1), ("u", 3), ("d", 2), ("d", 3)):
                if kind == "u":
                    n.up[g] = cols_of(A["w_ff1_2"][l], g * 1024, 4)
                else:
                    n.dn[g] = plan_down(A["w_ff2_2"][l], 8 * g, 8)
            n.ple = plan(A["w_ple_2"][l], 2, 1024, split=False)
            n.pg = cols_of(A["w_ple_gate_2"][l], 0, 4)
            L2.append(n)

        r = 0
        for name, w in PARAMS:
            src = A[name].rearrange(A["_flat"][name]) if A["_flat"][name] else A[name]
            src = src.rearrange("(r f) -> r f", f=128)
            a = 0
            while a < w:
                n = min(w - a, 128 - r % 128)
                t, q = r // 128, r % 128
                dst, sr = stage[q:q + n, t * 128:t * 128 + 128], src[a:a + n, :]
                t_par = D.dma(s_par, lambda e, dst=dst, sr=sr: e.dma_start(dst, sr))
                a += n
                r += n
        rowp = tmp(512)
        for name, w in ROWS:
            src = A[name].rearrange(A["_flat"][name]) if A["_flat"][name] else A[name]
            src = src.rearrange("(a f) -> a f", a=1)
            dst = rowp[0:1, rat[name]:rat[name] + w]
            t_row = S.dma(s_row, lambda e, dst=dst, src=src: e.dma_start(dst, src))
        xs_t = mix_t[:, :].rearrange("p (c d) -> p c d", c=4)
        cs_t = tmp(2048).rearrange("p (c d) -> p c d", c=2)
        t_x = S.dma(s_x, lambda e: e.dma_start(xs_t, A["x"].rearrange("a (c p) d -> p (a c) d", p=128)))
        t_cx = S.dma(s_cx, lambda e: e.dma_start(cs_t, A["ctx"].rearrange("a (c p) d -> p (a c) d", p=128)))
        fw3 = fw[:, :].rearrange("p (i d) -> p i d", i=2)
        pw3 = pw[:, :].rearrange("p (i d) -> p i d", i=2)
        t_fw = S.dma(s_fw, lambda e: e.dma_start(fw3, A["fnet_w"].rearrange("a (i g) c d -> (g c) (a i) d", i=2)))
        t_pw = S.dma(s_pw, lambda e: e.dma_start(pw3, A["pool_w"].rearrange("a (i g) c d -> (g c) (a i) d", i=2)))
        for n, name in enumerate(("i_bias_2", "f_bias_2")):
            src = A[name].rearrange("l h -> h l")
            dst = gb[0:4, 2 * n:2 * n + 2]
            t_gb = S.dma(s_gb, lambda e, dst=dst, src=src: e.dma_start(dst, src, allow_slow_non_contiguous=True))
        t_pos = S.dma(s_pos, lambda e: e.dma_start(
            posi[:, :], A["positions_2"].rearrange("a (c p) -> p (a c)", p=128), allow_slow_non_contiguous=True))

        fill(eps[:, 0:1], EPS)
        t_eps = fill(eps[:, 1:2], 1.0)
        S.wait(t_eps)
        E.wait(t_con)
        V.wait(t_con)
        G.wait(t_con)

        for i in range(NPT):
            n = min(128, pn - i * 128)
            b = bank()
            t = tr(b, b.ap[:, 0:n], stage[0:n, i * 128:i * 128 + 128], waits=(t_par,), inc=True)
            t_parT = cp(par[:, i * 128:i * 128 + n], b.ap[:, 0:n], t)
            b.free(t_parT)
        S.wait(t_parT)
        b = bank()
        t = mm(b, b.ap[:, 0:rn], ones[0:1, :], rowp[0:1, 0:rn], waits=(t_row,), inc=True)
        t_rb = cp(rb[:, :], b.ap[:, 0:rn], t)
        b.free(t_rb)

        act(csil[:, :, 0], pc("c", 0, 8), ACT.Silu)
        t_cs = act(csil[:, :, 1], pc("c_ctx", 0, 8), ACT.Silu)

        mod3 = mod[:, :].rearrange("p (j w) -> p j w", w=2)
        ada_n = [0]
        arow_free = [[], []]

        def ada_block():
            i = ada_n[0]
            ada_n[0] += 1
            b = bank()
            for half in range(2):
                s = raw(L_ada[2 * i + half])
                for k in range(8):
                    t = mm(b, b.ap[0:2, half * 256:half * 256 + 256], csil[:, k, :], s.ap[:, k, :],
                           start=(k == 0), stop=(k == 7), waits=(s.tok, t_cs), inc=(k == 7))
                done(s, t)
            ar = arow[i % 2]
            t = cp(ar[0:2, :], b.ap[0:2, :], t, *arow_free[i % 2], eng=S)
            b.free(t)
            b = bank()
            for q in range(4):
                t2 = tr(b, b.ap[:, 2 * q:2 * q + 2], ar[0:2, q * 128:q * 128 + 128], waits=(t,), inc=(q == 3))
            arow_free[i % 2] = [t2]
            t = tt(mod3[:, 4 * i:4 * i + 4, :], b.ap[:, 0:8].rearrange("p (j w) -> p j w", w=2),
                   pc("b_ada", 4 * i, 4).unsqueeze(2).to_broadcast([128, 4, 2]), ALU.add, t2)
            b.free(t)
            if i // 2 in (1, 4):
                t = ts(mod3[:, 4 * i:4 * i + 4, :], mod3[:, 4 * i:4 * i + 4, :], 1.0, None, ALU.add, None)
            return t

        flip = [0]

        def evac(out_ap, in_ap, *toks):
            flip[0] ^= 1
            return cp(out_ap, in_ap, *toks, eng=S if flip[0] else V)

        t_h = []
        for j in range(8):
            b = bank()
            for c in range(4):
                t = tr(b, b.ap[:, c * 128:c * 128 + 128], xs_t[:, c, j * 128:j * 128 + 128], waits=(t_x,), inc=(c == 3))
            t = evac(h[:, j, :], b.ap[:, :], t)
            b.free(t)
            t_h.append(t)
        hc = tmp(2048).rearrange("p (j t) -> p j t", j=8)
        xc_ctx = tmp(2048).rearrange("p (j t) -> p j t", j=8)
        t_hc = []
        for jj in range(4):
            b = bank()
            for q in range(4):
                j, c = 2 * jj + q // 2, q % 2
                t = tr(b, b.ap[:, q * 128:q * 128 + 128], cs_t[:, c, j * 128:j * 128 + 128], waits=(t_cx,),
                       inc=(q == 3))
            t = evac(hc[:, 2 * jj:2 * jj + 2, :], b.ap[:, :].rearrange("p (j t) -> p j t", j=2), t)
            b.free(t)
            t_hc += [t, t]

        def norm_stats(src, toks, sq, n, rs, center=None, count=1024):
            xt = list(toks)
            if center is not None:
                b = bank()
                for j in range(8):
                    t = mm(b, b.ap[:, 0:n], cc("mean"), src[:, j, :], start=(j == 0), stop=(j == 7),
                           waits=(toks[j],), inc=(j == 7))
                for j in range(8):
                    xt[j] = tt(center[:, j, :], src[:, j, :], b.ap[:, 0:n], ALU.subtract, t, toks[j])
                b.free(xt[7])
                src = center
            b = bank()
            used = [None] * len(sq)
            for j in range(8):
                q = sq[j % len(sq)]
                t = act(q[:, 0:n], src[:, j, :], ACT.Square, xt[j], used[j % len(sq)])
                t = mm(b, b.ap[:, 0:n], ones, q[:, 0:n], start=(j == 0), stop=(j == 7), waits=(t,), inc=True)
                used[j % len(sq)] = t
            t = act(rs[:, 0:n], b.ap[:, 0:n], ACT.Sqrt, t, bias=eps[:, 0:1], scale=1.0 / count)
            b.free(t)
            return recip(rs[:, 0:n], rs[:, 0:n], t)

        def apply_norm(src, dst, rs, n, g, bias=None):
            out_t = []
            for j in range(8):
                t = stt(dst[:, j, :], src[:, j, :], g(j), rs[:, 0:n], ALU.mult, ALU.mult)
                if bias is not None:
                    t = act(dst[:, j, :], dst[:, j, :], ACT.Identity, t, bias=bias(j))
                out_t.append(t)
            return out_t

        sq = [tmp(512) for _ in range(4)]
        rs = tmp(512)
        rs2 = tmp(256)
        def modulate(src, hi, lo, rs, n, g, bias):
            out_t = []
            S.wait(x_read[0])
            for j in range(8):
                t = stt(src[:, j, :], src[:, j, :], g(j), rs[:, 0:n], ALU.mult, ALU.mult)
                t = act(hi[:, j, :], src[:, j, :], ACT.Identity, t, bias=bias(j))
                out_t.append([t, stt(lo[:, j, :], src[:, j, :], bias(j), hi[:, j, :].bitcast(F32), ALU.add,
                                     ALU.subtract, t)])
            return out_t

        def split_x(src, g, toks, engs=None):
            out_t = []
            S.wait(x_read[0])
            for j in range(8):
                if g is None:
                    t = act(xh[:, j, :], src[:, j, :], ACT.Copy, toks[j])
                    t2 = tt(xl[:, j, :], src[:, j, :], xh[:, j, :].bitcast(F32), ALU.subtract, t, toks[j])
                else:
                    t = act(xh[:, j, :], src[:, j, :], ACT.Copy, toks[j], scale=g(j))
                    t2 = stt(xl[:, j, :], src[:, j, :], g(j), xh[:, j, :].bitcast(F32), ALU.mult, ALU.subtract, t,
                             toks[j])
                out_t.append([t, t2])
            return out_t

        norm_stats(h, t_h, sq, T, rs, center=mix)
        norm_stats(hc, t_hc, sq, TC, rs2, center=xc_ctx)
        for i in range(4):
            t_mod = ada_block()
        S.wait(t_mod)
        ctxr = region("ctxr", 4096, F32R, lvl=1)
        ch = ctxr[:, 0:2048].rearrange("p (j t) -> p j t", j=8)
        cl = ctxr[:, 2048:4096].rearrange("p (j t) -> p j t", j=8)
        t_xn = modulate(mix, xh, xl, rs, T, lambda j: mod3[:, 8 + j, 0:1], lambda j: mod3[:, j, 0:1])
        t_xc = modulate(xc_ctx, ch, cl, rs2, TC, lambda j: mod3[:, 8 + j, 1:2], lambda j: mod3[:, j, 1:2])

        posf = tmp(4)
        ang = tmp(32)
        kk = tmp(32)
        rr = tmp(32)
        cosT, sinT = rope[:, 0:32], rope[:, 32:64]
        cp(posf, posi[:, :], t_pos)
        tt(ang.rearrange("p (c f) -> p c f", c=4), posf.unsqueeze(2).to_broadcast([128, 4, 8]),
           cc("freq", 8).unsqueeze(1).to_broadcast([128, 4, 8]), ALU.mult)
        for dst, shift, add in ((sinT, 0.0, 0.0), (cosT, 0.25, float(np.pi / 2))):
            ts(kk, ang, 1.0 / TWO_PI, shift, ALU.mult, ALU.add)
            ts(kk, kk, MAGIC, None, ALU.add, None)
            ts(kk, kk, MAGIC, None, ALU.subtract, None)
            stt(rr, kk, -C1, ang, ALU.mult, ALU.add)
            stt(rr, kk, -C2, rr, ALU.mult, ALU.add)
            stt(rr, kk, -C3, rr, ALU.mult, ALU.add)
            ts(rr, rr, add, 3.1415925, ALU.add, ALU.min)
            t = ts(rr, rr, -3.1415925, None, ALU.max, None)
            t = act(dst, rr, ACT.Sin, t)
            V.wait(t)
        f = fence()

        def product(s, hf, x2, n, toks, m=128, k0=0, kt=8, o=0, extra=()):
            t_w = need(s, hf)
            b = bank()
            a = 128 * hf + o
            for k in range(kt):
                w = ([t_w] if k == 0 else []) + ([toks[k0 + k]] if toks else []) + list(extra)
                t = mm3(b, b.ap[0:m, 0:n], (s.hi[:, k, a:a + m], s.lo[:, k, a:a + m]),
                        (x2[0][:, k, :], x2[1][:, k, :]), start=(k == 0), stop=(k == kt - 1), waits=w,
                        inc=(k == kt - 1))
            if x2[0] is xh:
                x_read[0] = t
            return b, t

        def product_t(s, c, width=256):
            t_w = [need(s, 0, 0), need(s, 1)]
            b = bank()
            for k in range(8):
                t = mm3(b, b.ap[:, 0:256], (xh[:, k, c * 128:c * 128 + 128], xl[:, k, c * 128:c * 128 + 128]),
                        (s.hi[:, k, :], s.lo[:, k, :]), start=(k == 0), stop=(k == 7),
                        waits=t_w if k == 0 else (), inc=(k == 7))
            x_read[0] = t
            return b, t

        reset(lo)
        Xt = tmp(2048 + 1024).rearrange("p (q n) -> p q n", q=6)
        Bt = tmp(1024 + 512).rearrange("p (q n) -> p q n", q=6)
        Z = tmp(2048).rearrange("p (q n) -> p q n", q=4)
        dtr, dta, dtb, wst, dt = [small[:, i * 96:i * 96 + 96] for i in range(5)]
        ex = small[:, 480:960]
        aneg = small[:, 960:976]
        BT = tmp(1024).rearrange("p (g t) -> p g t", g=2)
        CT = tmp(1024).rearrange("p (g t) -> p g t", g=2)
        acc = [tmp(512) for _ in range(4)]
        acc_free = [[] for _ in range(4)]
        nacc = [0]
        after_conv = arena_n[0]

        def conv3(b, n, wname, j, toks, bname):
            i = nacc[0] % 4
            nacc[0] += 1
            a = acc[i]
            u = b.ap
            t = act(a[:, 0:n], u[:, 0:n], ACT.Identity, *toks, *acc_free[i], bias=pc(bname, j),
                    scale=pc(wname, 8 + j))
            stt(a[:, 1:n], u[:, 0:n - 1], pc(wname, j), a[:, 1:n], ALU.mult, ALU.add, t)
            t = stt(a[:, 0:n - 1], u[:, 1:n], pc(wname, 16 + j), a[:, 0:n - 1], ALU.mult, ALU.add)
            b.free(t)
            return i, a, t

        for sl in range(4):
            s = L_xbc[sl]
            for jj in range(2):
                j = 2 * sl + jj
                for which in range(2):
                    if which == 1 and j >= 6:
                        continue
                    x2, n, tk = ((xh, xl), T, t_xn) if which == 0 else ((ch, cl), TC, t_xc)
                    b, t = product(s, jj, x2, n, tk)
                    last = t
                    i, a, t = conv3(b, n, "ssd_conv_w", j, (t,), "ssd_conv_b")
                    qs = 2 if which == 0 else 0
                    if j >= 6:
                        t = act(CT[:, j - 6, :], a, ACT.Silu, t)
                        acc_free[i] = [t]
                        continue
                    if j >= 4 and which == 0:
                        t = act(BT[:, j - 4, :], a, ACT.Silu, t)
                        acc_free[i] = [t]
                        a = BT[:, j - 4, :]
                    else:
                        t = act(a[:, 0:n], a[:, 0:n], ACT.Silu, t)
                    b = bank()
                    for c in range(n // 128):
                        t2 = tr(b, b.ap[:, c * 128:c * 128 + 128], a[:, c * 128:c * 128 + 128], waits=(t,),
                                inc=(c == n // 128 - 1))
                    if not (j >= 4 and which == 0):
                        acc_free[i] = [t2]
                    dst = Xt[:, qs:qs + n // 128, j * 128:j * 128 + 128] if j < 4 else \
                        Bt[:, qs:qs + n // 128, (j - 4) * 128:(j - 4) * 128 + 128]
                    t = evac(dst, b.ap[:, 0:n].rearrange("p (c f) -> p c f", f=128), t2)
                    b.free(t)
                freed(s, jj, last)
        dtw = [acc[i] for i in (0, 1)]
        for i, (x2, n) in enumerate((((ch, cl), TC), ((xh, xl), T))):
            b, t = product(L_dt, 0, x2, n, None, m=16)
            t_dw = cp(dtw[i][0:16, 0:n], b.ap[0:16, 0:n], t, *acc_free[i])
            b.free(t_dw)
        freed(L_dt, 0, t)
        b = bank()
        for q in range(6):
            src, c = (dtw[0], q) if q < 2 else (dtw[1], q - 2)
            t = tr(b, b.ap[:, q * 16:q * 16 + 16], src[0:16, c * 128:c * 128 + 128], waits=(t_dw,), inc=(q == 5))
        acc_free[0] = acc_free[1] = [t]

        def softplus(dst, raw, e1, e2, sign):
            t = ts(e1, raw, -1.0, None, ALU.mult, None)
            tt(e1, e1, raw, ALU.min)
            ts(dst, raw, sign, 0.0, ALU.mult, ALU.max)
            t = act(e1, e1, ACT.Exp, (V.sem, V.sem.n))
            ts(e2, e1, 1.0, None, ALU.add, None, t)
            t = act(e2, e2, ACT.Ln, (V.sem, V.sem.n))
            tt(dst, dst, e2, ALU.add, t)
            ts(e2, e1, 1.0, None, ALU.add, None)
            ts(raw, e2, 1.0, None, ALU.subtract, None)
            tt(e1, e1, raw, ALU.subtract)
            recip(e2, e2)
            tt(e1, e1, e2, ALU.mult)
            return tt(dst, dst, e1, ALU.add)

        t = tt(dtr.rearrange("p (q w) -> p q w", q=6), b.ap[:, 0:96].rearrange("p (q w) -> p q w", q=6),
               row("ssd_dt_bias", 0, 16).unsqueeze(1).to_broadcast([128, 6, 16]), ALU.add, t)
        b.free(t)
        softplus(dt, dtr, dta, dtb, 1.0)
        t = act(aneg, row("ssd_a_log", 0, 16), ACT.Exp, t_rb)
        ts(aneg, aneg, -1.0, None, ALU.mult, None, t)
        dt3 = dt.rearrange("p (q w) -> p q w", q=6)
        t_a = tt(dta.rearrange("p (q w) -> p q w", q=6), dt3, aneg.unsqueeze(1).to_broadcast([128, 6, 16]), ALU.mult)
        b = bank()
        for i, m in enumerate((ule, uge, cc("ugt"), cc("ult"), ones)):
            t = mm(b, b.ap[:, i * 96:i * 96 + 96], m, dta, waits=(t_a,), inc=(i == 4))
        t_ex = act(ex, b.ap[:, 0:480], ACT.Exp, t)
        b.free(t_ex)
        ex4 = ex.rearrange("p (i q w) -> p i q w", i=5, q=6)
        w3 = wst.rearrange("p (q w) -> p q w", q=6)
        tt(w3[:, :, 0:8], dt3[:, :, 0:8], ex4[:, 2, :, 0:8], ALU.mult, t_ex)
        tt(w3[:, :, 8:16], dt3[:, :, 8:16], ex4[:, 3, :, 8:16], ALU.mult)

        for sl in range(2):
            s = L_z[sl]
            for c in range(4):
                b, t = product_t(s, c)
                if c == 3:
                    freed(s, 0, t)
                    freed(s, 1, t)
                t_z = act(Z[:, c, sl * 256:sl * 256 + 256], b.ap[:, 0:256], ACT.Silu, t)
                b.free(t_z)

        fin = []
        for sl in range(2):
            for i in range(2):
                b, t = product(L_fp[sl], i, (xh, xl), T, None)
                freed(L_fp[sl], i, t)
                fin.append((b, t))
        fA = tmp(2048).rearrange("p (c i s f) -> p c i s f", c=4, i=2, s=2)
        for i in range(2):
            b, t = fin[i]
            t = evac(acc[i], b.ap[:, :], t, *acc_free[i])
            b.free(t)
            fin[i] = t
        PW = 544
        fence()
        close(1)
        arena2 = region("arena2", 4096, lvl=1)
        use(arena2, 4096)
        pb = [tmp(2 * PW).rearrange("p (i t) -> p i t", i=2) for _ in range(3)]
        fill(pb[0][:, :, 0:16], 0.0)
        t = fill(pb[0][:, :, 528:544], 0.0)
        for i in range(2):
            b, t = fin[2 + i]
            t = cp(pb[0][:, i, 16:528], b.ap[:, :], t)
            b.free(t)
        P0, P1, P2 = pb
        tt(P1[:, :, 1:544], P0[:, :, 0:543], P0[:, :, 1:544], ALU.add)
        tt(P2[:, :, 2:543], P1[:, :, 1:542], P1[:, :, 3:544], ALU.add)
        V.wait(t_con1)
        iv = con1[:, 256:1280].rearrange("p (i t) -> p i t", i=2)
        po = acc[2:4]
        for a_ in acc_free[2:4]:
            V.wait(*a_)
        tt(po[0][0:64, :], P1[0:64, 0, 16:528], iv[0:64, 0, :], ALU.mult)
        tt(po[0][64:128, :], P2[64:128, 0, 16:528], iv[64:128, 0, :], ALU.mult)
        tt(P1[:, 1, 4:541], P2[:, 1, 2:539], P2[:, 1, 6:543], ALU.add)
        tt(po[1][0:64, :], P1[0:64, 1, 16:528], iv[0:64, 1, :], ALU.mult)
        tt(P2[:, 1, 16:528], P1[:, 1, 12:524], P1[:, 1, 20:532], ALU.add)
        tt(po[1][64:128, :], P2[64:128, 1, 16:528], iv[64:128, 1, :], ALU.mult)
        tt(po[0], po[0], P0[:, 0, 16:528], ALU.subtract)
        t_po = tt(po[1], po[1], P0[:, 1, 16:528], ALU.subtract)
        for c in range(4):
            b = bank()
            for i in range(2):
                t = mm(b, b.ap[:, i * 256:i * 256 + 256], acc[i][:, c * 128:c * 128 + 128], con1[:, 0:256],
                       waits=(fin[0], fin[1], t_con1), inc=(i == 1))
            t_fA = evac(fA[:, c].rearrange("p i s f -> p (i s f)"), b.ap[:, :], t)
            b.free(t_fA)
            E.wait(t_fA)
        sC = [raw(x) for x in L_dft]
        spec = [acc[0], acc[1]]
        t_sp = []
        for i in range(2):
            b = bank()
            n = 0
            for cs_ in range(2):
                for c in range(4):
                    t = mm(b, b.ap[:, :], fA[:, c, i, cs_, :], sC[cs_].ap[:, c, :], start=(n == 0), stop=(n == 7),
                           waits=(sC[cs_].tok,), inc=(n == 7))
                    n += 1
            t_e = evac(spec[i], b.ap[:, :], t)
            b.free(t_e)
            t_sp.append(t_e)
        done(sC[0], t)
        done(sC[1], t)
        for src, w, t_w, base, tk in ((spec, fw3, t_fw, 4, t_sp), (po, pw3, t_pw, 6, [t_po, t_po])):
            for i in range(2):
                b = bank()
                for g in range(2):
                    t = mm(b, b.ap[g * 64:g * 64 + 64, :], w[g * 64:g * 64 + 64, i, :], src[i][g * 64:g * 64 + 64, :],
                           waits=(t_w, tk[i]), inc=(g == 1))
                if base == 4:
                    t = evac(mix[:, 4 + i, :], b.ap[:, :], t)
                else:
                    t = ts(mix[:, 6 + i, :], b.ap[:, :], pc("pool_scale", i), None, ALU.mult, None, t)
                b.free(t)
        fence()

        reset(0)
        Sf = tmp(2048).rearrange("p (q n) -> p q n", q=4)
        Sb = tmp(2048).rearrange("p (q n) -> p q n", q=4)
        Xs = [acc[0], acc[1]]
        Stmp = acc[2]
        Xs_free = [[], []]
        nxs = [0]

        def v8(ap):
            return ap.rearrange("p (h d) -> p h d", h=8)

        def bc8(ap):
            return ap.unsqueeze(2).to_broadcast([128, 8, 64])

        def chunk_state(q, d):
            i = nxs[0] % 2
            nxs[0] += 1
            t = tt(v8(Xs[i]), v8(Xt[:, q, :]), bc8(w3[:, q, d * 8:d * 8 + 8]), ALU.mult, *Xs_free[i])
            b = bank()
            for g in range(2):
                t = mm(b, b.ap[:, g * 256:g * 256 + 256], Bt[:, q, g * 128:g * 128 + 128],
                       Xs[i][:, g * 256:g * 256 + 256], waits=(t,), inc=(g == 1))
            Xs_free[i] = [t]
            return b, t

        t_st = {}
        for d, first, rest in ((0, (0, 1), (2, 3, 4)), (1, (1, 0), (5, 4, 3))):
            St = (Sf, Sb)[d]
            where = (0, 1, 2, 3) if d == 0 else (3, 2, 1, 0)
            b, t = chunk_state(first[0], d)
            t = cp(Stmp, b.ap[:, :], t)
            b.free(t)
            cur = Stmp
            for n, q in enumerate((first[1],) + rest):
                b, t = chunk_state(q, d)
                dst = St[:, where[n], :]
                tt(v8(dst), v8(cur), bc8(ex4[:, 4, q, d * 8:d * 8 + 8]), ALU.mult)
                t = tt(dst, dst, b.ap[:, :], ALU.add, t)
                b.free(t)
                cur = dst
                t_st[(d, where[n])] = t

        use(arena, N1, after_conv)
        Rf = tmp(1024)
        Ex = tmp(1024)
        dmb = Rf
        Rb, Rf = [mix_t[:, i * 1024:i * 1024 + 1024] for i in range(2)]
        dmf = tmp(1024)
        ssq = small[:, 984:1000]

        def v3(ap):
            return ap.rearrange("p (h l) -> p h l", h=8)

        def masks(m):
            return m.unsqueeze(1).to_broadcast([128, 8, 128])

        def cols(ap):
            return ap.unsqueeze(2).to_broadcast([128, 8, 128])

        R_free = []
        M_free = []
        a3 = dta.rearrange("p (q w) -> p q w", q=6)
        for c in range(4):
            q = c + 2
            if c < 4:
                ada_block()
            tg1 = tt(v3(Rf), cols(a3[:, q, 0:8]), masks(ule), ALU.mult, t_a, *R_free, eng=G)
            tg2 = tt(v3(Rb), cols(a3[:, q, 8:16]), masks(uge), ALU.mult, eng=G)
            bs = []
            for half in range(2):
                b = bank()
                mm(b, b.ap[:, :], cc("ugt"), Rf[:, half * 512:half * 512 + 512], start=True, stop=False, waits=(tg2,))
                t = mm(b, b.ap[:, :], cc("ult"), Rb[:, half * 512:half * 512 + 512], start=False, stop=True, inc=True)
                bs.append((b, t))
            R_free = [t]
            for half in range(2):
                b, t = bs[half]
                t_E = act(Ex[:, half * 512:half * 512 + 512], b.ap[:, :], ACT.Exp, t, *M_free)
                b.free(t_E)
            bg = bank()
            for g in range(2):
                t_g = mm(bg, bg.ap[:, g * 128:g * 128 + 128], BT[:, g, c * 128:c * 128 + 128],
                         CT[:, g, c * 128:c * 128 + 128], inc=(g == 1))
            tt(v3(dmf), cols(dt3[:, q, 0:8]), masks(ule), ALU.mult, *M_free)
            tt(v3(dmb), cols(dt3[:, q, 8:16]), masks(uge), ALU.mult)
            tt(dmf, dmf, dmb, ALU.add)
            tt(dmf, dmf, Ex, ALU.mult, t_E)
            for g in range(2):
                t_M = tt(v3(dmf)[:, 4 * g:4 * g + 4, :], v3(dmf)[:, 4 * g:4 * g + 4, :],
                         bg.ap[:, g * 128:g * 128 + 128].unsqueeze(1).to_broadcast([128, 4, 128]), ALU.mult, t_g)
            bg.free(t_M)
            bf, bb = bank(), bank()
            for bx, St, d in ((bf, Sf, 0), (bb, Sb, 1)):
                for g in range(2):
                    t_off = mm(bx, bx.ap[:, g * 256:g * 256 + 256], CT[:, g, c * 128:c * 128 + 128],
                               St[:, c, g * 256:g * 256 + 256], waits=(t_st[(d, c)],), inc=(g == 1))
            bd = bank()
            for hh in range(8):
                t_d = mm(bd, bd.ap[:, hh * 64:hh * 64 + 64], dmf[:, hh * 128:hh * 128 + 128],
                         Xt[:, q, hh * 64:hh * 64 + 64], waits=(t_M,), inc=(hh == 7))
            M_free = [t_d]
            y = acc[c % 2]
            y1 = acc[3]
            tt(v8(y), v8(Xt[:, q, :]), bc8(row("ssd_d", 0, 8)), ALU.mult, t_rb)
            tt(y, y, bd.ap[:, :], ALU.add, t_d)
            bd.free((V.sem, V.sem.n))
            tt(v8(y1), v8(bf.ap[:, :]), bc8(ex4[:, 0, q, 0:8]), ALU.mult, t_off)
            bf.free((V.sem, V.sem.n))
            tt(y, y, y1, ALU.add)
            tt(v8(y1), v8(bb.ap[:, :]), bc8(ex4[:, 1, q, 8:16]), ALU.mult)
            bb.free((V.sem, V.sem.n))
            tt(y, y, y1, ALU.add)
            t = tt(Z[:, c, :], y, Z[:, c, :], ALU.mult, t_z)
            y = Z[:, c, :]
            for g in range(2):
                t_q = act(acc[2][:, g * 256:g * 256 + 256], y[:, g * 256:g * 256 + 256], ACT.Square, t,
                          accum=ssq[:, 2 * c + g:2 * c + g + 1])
        t = act(ssq[:, 8:16], ssq[:, 0:8], ACT.Sqrt, bias=eps[:, 0:1], scale=1.0 / 256)
        recip(ssq[:, 8:16], ssq[:, 8:16], t)
        for c in range(4):
            for g in range(2):
                t = ts(Z[:, c, g * 256:g * 256 + 256], Z[:, c, g * 256:g * 256 + 256],
                       ssq[:, 8 + 2 * c + g:9 + 2 * c + g], None, ALU.mult, None)
            E.wait(t)
        t_mix = []
        for j in range(4):
            b = bank()
            for c in range(4):
                t = tr(b, b.ap[:, c * 128:c * 128 + 128], Z[:, c, j * 128:j * 128 + 128], inc=(c == 3))
            t = ts(mix[:, j, :], b.ap[:, :], pc("ssd_norm_w", j), None, ALU.mult, None, t)
            b.free(t)
            t_mix.append(t)
        while ada_n[0] < 12:
            t_mod = ada_block()
        S.wait(t_mod)
        E.wait(t_mix[3], (S.sem, S.sem.n))

        def project(L, x2, toks, evac_fn, kt=8, k0=0):
            for j in range(8):
                s = L[j // 2]
                b, t = product(s, j % 2, x2, T, toks, k0=k0, kt=kt)
                freed(s, j % 2, t)
                evac_fn(j, b, t)

        toks = [None] * 8

        def scale_h(toks):
            return [S.do(lambda e, j=j: e.activation(h[:, j, :], h[:, j, :], ACT.Copy, scale=ALPHA), toks[j])
                    for j in range(8)]

        def residual(gcol):
            def fn(j, b, t):
                toks[j] = stt(h[:, j, :], b.ap[:, :], mod3[:, gcol + j, 0:1], h[:, j, :], ALU.mult, ALU.add, t,
                              toks[j])
                b.free(toks[j])
            return fn

        fence()
        close(0)
        acts = region("acts", 16384, F32R)
        U = [[acts[:, (2 * u + v) * 4096:(2 * u + v + 1) * 4096].rearrange("p (j t) -> p j t", j=8)
              for v in range(2)] for u in range(2)]
        arena = region("arena_f", 1536)
        use(arena, 1536)
        sq = [tmp(512) for _ in range(2)]
        rs = tmp(512)
        acc = [mix[:, i, :] for i in range(8)]
        toks[:] = scale_h(t_h)
        t_xn = split_x(mix, None, [None] * 8)
        project(L_wout, (xh, xl), t_xn, residual(16))

        def post_norm(g, bb_):
            norm_stats(h, toks, sq, T, rs, center=mix)
            return apply_norm(mix, h, rs, T, lambda j: pc(g, j), lambda j: pc(bb_, j))

        t_h = post_norm("ln1_g", "ln1_b")
        norm_stats(h, t_h, sq, T, rs, center=mix)
        t_xn = modulate(mix, xh, xl, rs, T, lambda j: mod3[:, 32 + j, 0:1], lambda j: mod3[:, 24 + j, 0:1])
        toks[:] = scale_h([(V.sem, V.sem.n)] * 8)

        acc_free = [[(V.sem, V.sem.n)] for _ in range(8)]
        U_free = [[], []]
        U_tok = [[None] * 8, [None] * 8]
        na = [0]

        def grid(ap, dr, dc, src):
            v = ap.rearrange("p (r c) -> p r c", r=8)
            r0, r1 = max(0, -dr), min(8, 8 - dr)
            c0, c1 = max(0, -dc), min(64, 64 - dc)
            if src:
                return v[:, r0 + dr:r1 + dr, c0 + dc:c1 + dc]
            return v[:, r0:r1, c0:c1]

        def store_u(u, jl, src, *tk):
            t1 = act(U[u][0][:, jl, :], src, ACT.Copy, *tk, *U_free[u])
            t2 = tt(U[u][1][:, jl, :], src, U[u][0][:, jl, :].bitcast(F32), ALU.subtract, t1, *tk, *U_free[u], eng=G)
            U_tok[u][jl] = [t1, t2]
            return t2

        def up_tile(g, jl):
            j = sum(GR[:g]) + jl
            pair = L_up[g][jl // 2]
            got = []
            for s, col in ((pair[0], 22 + j), (pair[1], j)):
                b, t = product(s, jl % 2, (xh, xl), T, t_xn)
                freed(s, jl % 2, t)
                i = na[0] % 8
                na[0] += 1
                a = acc[i]
                t = act(a, b.ap[:, :], ACT.Identity, t, *acc_free[i], OWN, bias=pc("ffn_conv_b", col),
                        scale=pc("ffn_conv_w", 4 * 44 + col))
                got.append([i, a, t, b, col])
            for dr in (-1, 0, 1):
                for dc in (-1, 0, 1):
                    if dr == 0 and dc == 0:
                        continue
                    tap = (dr + 1) * 3 + dc + 1
                    for q in got:
                        o = grid(q[1], dr, dc, False)
                        q[2] = stt(o, grid(q[3].ap[:, :], dr, dc, True), pc("ffn_conv_w", tap * 44 + q[4]), o,
                                   ALU.mult, ALU.add, q[2], OWN)
            for q in got:
                q[3].free(q[2])
            return g, jl, got

        def up_end(g, jl, got):
            (ig, ga, tg, _, _), (iv_, va, tv, _, _) = got
            tg = act(ga, ga, ACT.Gelu_apprx_tanh, tg, OWN)
            t = tt(va, ga, va, ALU.mult, tg, tv, eng=G)
            acc_free[ig] = [t]
            t = store_u(g % 2, jl, va, t)
            acc_free[iv_] = [t]

        def up(g):
            late = None
            for jl in range(GR[g]):
                now = up_tile(g, jl)
                if late is not None:
                    up_end(*late)
                late = now
            up_end(*late)

        def down(L, g, kt, fn):
            project(L, U[g % 2], U_tok[g % 2], fn, kt=kt)
            U_free[g % 2] = [(E.sem, E.sem.n)]

        lo_eng[0] = G
        up(0)
        up(1)
        down(L_dn[0], 0, 8, residual(40))
        up(2)
        down(L_dn[1], 1, 8, residual(40))
        down(L_dn[2], 2, 6, residual(40))
        lo_eng[0] = None
        t_h = post_norm("ln2_g", "ln2_b")
        fence()

        def rms(gname, l, t_h):
            return split_x(h, lambda j: pc(gname, 8 * l + j), t_h)

        def add_h(j, b, t):
            toks[j] = tt(h[:, j, :], h[:, j, :], b.ap[:, :], ALU.add, t, toks[j])
            b.free(toks[j])

        for l in range(2):
            Ln = L2[l]
            close(0)
            AM = 20600
            arena = region(f"arena_m{l}", AM)
            use(arena, AM)
            sq = [tmp(512) for _ in range(4)]
            rs = tmp(512)
            rsT = small[:, 976:980]
            t_xn = rms("g_mix_2", l, t_h)
            t_rs = norm_stats(h, t_h, sq, T, rs)
            b = bank()
            for c in range(4):
                t = tr(b, b.ap[:, c:c + 1], rs[0:1, c * 128:c * 128 + 128], waits=(t_rs,), inc=(c == 3))
            t_rsT = cp(rsT, b.ap[:, 0:4], t)
            b.free(t_rsT)
            S.wait(t_rsT)
            qt = tmp(2048).rearrange("p (c n) -> p c n", c=4)
            it = tmp(2048).rearrange("p (c n) -> p c n", c=4)
            ct = tmp(1024).rearrange("p (c n) -> p c n", c=4)
            ctT = tmp(1024).rearrange("p (k t) -> p k t", k=2)
            kt_t = tmp(1024)
            kt = kt_t.rearrange("p (c n) -> p c n", c=4)
            ikt = tmp(512).rearrange("p (c n) -> p c n", c=4)
            iw = tmp(32).rearrange("p (c n) -> p c n", c=4)
            vt = tmp(512).rearrange("p (c n) -> p c n", c=4)
            ro_t = tmp(1024)
            ro = [ro_t[:, i * 256:i * 256 + 256] for i in range(4)]
            st8 = tmp(64)
            mark = arena_n[0]
            mq = tmp(2048).rearrange("p (j t) -> p j t", j=4)
            mk = tmp(2048).rearrange("p (j t) -> p j t", j=4)
            mv_t, mo_t = tmp(2048), tmp(2048)
            mv = mv_t.rearrange("p (c n) -> p c n", c=4)
            mo = mo_t.rearrange("p (j t) -> p j t", j=4)
            fr, ir, er = sq[1], sq[2], sq[3]
            ksrc = kt.rearrange("p c (v r d) -> p c v r d", v=2, r=2)
            rsI = small[:, 980:984]
            t_rsI = ts(rsI, rsT, float(8 ** -0.5 * 64 ** -0.5), None, ALU.mult, None)
            S.wait(t_rsI)
            V.wait((S.sem, S.sem.n))
            wq = mo_t.rearrange("p (s k n) -> p s k n", s=2, k=2)
            behind = fence()
            t_wq = [S.dma(s_wq, lambda e, src=src, dst=dst: e.dma_start(dst, src), *behind) for src, dst in (
                (A["w_iq_up_2"][l].rearrange("(k p) n -> p k n", p=128), wq[:, 0]),
                (A["w_q_up_2"][l].rearrange("(k p) n -> p k n", p=128), wq[:, 1]))]
            t_vt = []
            for n, s in enumerate(Ln.tok_):
                for c in range(4):
                    if n == 0 and c == 0:
                        E.wait(*t_xn)
                    b, t = product_t(s, c)
                    if c == 3:
                        freed(s, 0, t)
                        freed(s, 1, t)
                    rc = rsT[:, c:c + 1]
                    if n == 0:
                        t_ct = act(ct[:, c, :], b.ap[:, 0:256], ACT.Copy, t, OWN, scale=rc)
                        b.free(t_ct)
                    elif n == 1:
                        act(ksrc[:, c, :, 0, :], b.ap[:, 0:128].rearrange("p (v d) -> p v d", v=2), ACT.Copy, t,
                            OWN, scale=rc)
                        t_kt = act(vt[:, c, :], b.ap[:, 128:256], ACT.Copy, t, OWN, scale=rc)
                        b.free(t_kt)
                    else:
                        act(ikt[:, c, 0:64], b.ap[:, 0:64], ACT.Copy, t, OWN, scale=rc)
                        t_ik = act(iw[:, c, :], b.ap[:, 64:72], ACT.Copy, t, OWN, scale=rsI[:, c:c + 1])
                        b.free(t_ik)

            cfree = [None] * 4
            t_mk = [None] * 8
            t_mv = [None] * 4
            t_mo = [None] * 4
            scratch_read = [None, None]

            def mqk_unit(j):
                def unit():
                    s = Ln.mqk[j // 2]
                    b, t = product(s, j % 2, (xh, xl), T, None)
                    freed(s, j % 2, t)
                    i, i2 = (2 * j) % 4, (2 * j + 1) % 4
                    a, u = sq[i], sq[i2]
                    t = tt(u, b.ap[:, :], rs, ALU.mult, t, cfree[i2], OWN)
                    b.free(t)
                    yield
                    t = act(a, u, ACT.Identity, t, cfree[i], OWN, bias=pc("conv_b_2", 8 * l + j),
                            scale=pc("conv_w_2", 32 * l + 24 + j))
                    for sh in (3, 2, 1):
                        t = stt(a[:, sh:512], u[:, 0:512 - sh], pc("conv_w_2", 32 * l + (3 - sh) * 8 + j),
                                a[:, sh:512], ALU.mult, ALU.add, t, OWN)
                    cfree[i2] = t
                    yield
                    dst = mq[:, j, :] if j < 4 else mk[:, j - 4, :]
                    t_mk[j] = cfree[i] = act(dst, a, ACT.Silu, t, OWN)
                return unit

            def mv_unit(n, c):
                def unit():
                    s = Ln.mv[n]
                    b, t = product_t(s, c)
                    if c == 3:
                        freed(s, 0, t)
                        freed(s, 1, t)
                    t_mv[c] = act(mv[:, c, n * 256:n * 256 + 256], b.ap[:, 0:256], ACT.Copy, t, scratch_read[0], OWN,
                                  scale=rsT[:, c:c + 1])
                    b.free(t_mv[c])
                    yield
                return unit

            def mo_unit(j):
                def unit():
                    s = Ln.mo[j // 2]
                    b, t = product(s, j % 2, (xh, xl), T, None)
                    freed(s, j % 2, t)
                    t = tt(mo[:, j, :], b.ap[:, :], rs, ALU.mult, t, scratch_read[1], OWN)
                    b.free(t)
                    yield
                    t_mo[j] = act(mo[:, j, :], mo[:, j, :], ACT.Sigmoid, t, OWN)
                return unit

            gate_t = [None, None]

            def gate_unit():
                for i, (o, dst, bcol) in enumerate(((0, ir, l), (4, fr, 2 + l))):
                    b, t = product(Ln.gate, 0, (xh, xl), T, None, m=4, o=o)
                    t2 = tt(dst[0:4, :], b.ap[0:4, :], rs[0:4, :], ALU.mult, t, *cfree, OWN)
                    b.free(t2)
                    gate_t[i] = ts(dst[0:4, :], dst[0:4, :], gb[0:4, bcol:bcol + 1], None, ALU.add, None, t_gb, t2,
                                   OWN)
                freed(Ln.gate, 0, t)
                yield

            i_flat = it.rearrange("p c n -> p (c n)")
            q_flat = qt.rearrange("p c n -> p (c n)")
            qT, iT = mix[:, 4:8, :], mix[:, 0:4, :]
            kT = [ct.rearrange("p c n -> p (c n)")[:, 0:512], ct.rearrange("p c n -> p (c n)")[:, 512:1024]]
            ikT = ctT[:, 0, :]
            k3 = ksrc[:, :, :, 0, :]
            ik3 = ikt[:, :, 0:64]
            got = {}

            def rope_on(src, nh, *tk):
                co = cosT.rearrange("p (c f) -> p c f", c=4).unsqueeze(2).to_broadcast([128, 4, nh, 8])
                si = sinT.rearrange("p (c f) -> p c f", c=4).unsqueeze(2).to_broadcast([128, 4, nh, 8])
                x1, x2 = src[:, :, :, 0:8], src[:, :, :, 8:16]
                r4 = [r_[:, 0:32 * nh].rearrange("p (c n f) -> p c n f", c=4, n=nh) for r_ in ro]
                t0 = [(V.sem, V.sem.n)] + list(tk)
                tt(r4[0], x1, co, ALU.mult, *t0, OWN)
                tt(r4[1], x2, si, ALU.mult, *t0, OWN)
                t2 = tt(r4[2], x2, co, ALU.mult, *t0, OWN)
                t4 = tt(r4[3], x1, si, ALU.mult, *t0, OWN)
                tt(x1, r4[0], r4[1], ALU.subtract, t4, OWN)
                return tt(x2, r4[2], r4[3], ALU.add, t4, OWN)

            def turned(src, j, dst, *tk):
                b = bank()
                for c in range(4):
                    t = tr(b, b.ap[:, c * 128:c * 128 + 128], src[:, c, j * 128:j * 128 + 128], waits=tk, inc=(c == 3))
                t = act(dst, b.ap[:, :], ACT.Copy, t, OWN)
                b.free(t)
                return t

            score = {1: i_flat[:, 1536:1792], 2: ctT[:, 1, 0:384], 3: ikt.rearrange("p c n -> p (c n)")}
            work = i_flat[:, 0:512]
            rl = [i_flat[:, 512:1024], i_flat[:, 1024:1536]]
            m8 = st8[:, 48:56]
            pens = {0: cc("pen")}
            t_pens = {0: None}

            def main_path():
                sv = mv_t[:, 0:1024].rearrange("p (c n) -> p c n", c=4)
                t = act(sv, ct, ACT.Square, t_ct, OWN)
                t = reduce(st8[:, 0:4], sv, ALU.add, t)
                t = act(st8[:, 0:4], st8[:, 0:4], ACT.Sqrt, t, OWN, bias=eps[:, 0:1], scale=1.0 / 256)
                recip(st8[:, 0:4], st8[:, 0:4], t)
                t = tt(ct, ct, st8[:, 0:4].unsqueeze(2).to_broadcast([128, 4, 256]), ALU.mult)
                yield
                for k in range(2):
                    b = bank()
                    for c in range(4):
                        t2 = tr(b, b.ap[:, c * 128:c * 128 + 128], ct[:, c, k * 128:k * 128 + 128], waits=(t,),
                                inc=(c == 3))
                    t3 = ts(ctT[:, k, :], b.ap[:, :], pc("g_cq_2", 2 * l + k), None, ALU.mult, None, t2)
                    b.free(t3)
                t_c = t3
                yield
                for w, dst in ((0, it), (1, qt)):
                    for c in range(4):
                        b = bank()
                        for k in range(2):
                            t = mm(b, b.ap[:, :], ctT[:, k, c * 128:c * 128 + 128], wq[:, w, k, :], start=(k == 0),
                                   stop=(k == 1), waits=(*t_wq, t_c), inc=(k == 1))
                        t_e = act(dst[:, c, :], b.ap[:, :], ACT.Copy, t, OWN)
                        b.free(t_e)
                    got[w] = t_e
                    yield
                qf = qt.rearrange("p c (n d) -> p (c n) d", n=8)
                mo3 = mo_t.rearrange("p (n d) -> p n d", n=32)
                t = act(mo3, qf, ACT.Square, t, got[1], OWN)
                t1 = act(sv[:, :, 0:128].rearrange("p c (v d) -> p c v d", v=2), k3, ACT.Square, t_kt, OWN)
                t2 = act(sv[:, :, 128:192], ik3, ACT.Square, t_ik, OWN)
                reduce(st8[:, 0:32], mo3, ALU.add, t, OWN)
                scratch_read[1] = (V.sem, V.sem.n)
                reduce(st8[:, 32:40].rearrange("p (c v) -> p c v", c=4),
                       sv[:, :, 0:128].rearrange("p c (v d) -> p c v d", v=2), ALU.add, t1, OWN)
                t = reduce(st8[:, 40:44], sv[:, :, 128:192], ALU.add, t2, OWN)
                scratch_read[0] = t
                act(st8[:, 0:44], st8[:, 0:44], ACT.Sqrt, t, OWN, bias=eps[:, 0:1], scale=1.0 / 64)
                i4 = it.rearrange("p c (n d) -> p c n d", n=8)
                t_i = rope_on(i4, 8, got[0])
                yield
                recip(st8[:, 0:44], st8[:, 0:44], (S.sem, S.sem.n))
                tt(ik3, ik3, st8[:, 40:44].unsqueeze(2).to_broadcast([128, 4, 64]), ALU.mult)
                tt(ik3, ik3, row("g_ik_2", 64 * l, 64).unsqueeze(1).to_broadcast([128, 4, 64]), ALU.mult)
                rope_on(ik3.unsqueeze(2), 1)
                t_k = cp(ikt[:, :, 64:128], ik3)
                yield
                t_I = turned(ikt, 0, ikT, t_k)
                for j in range(4):
                    t_I = turned(it, j, iT[:, j, :], t_i)
                yield
                rl_free = [t_I, t_I]
                n = 0
                for c in (3, 2, 1):
                    W = 128 * (c + 1)
                    sc = score[c]
                    queue = []

                    def index_mm(hh):
                        o = 64 * (hh % 2)
                        b = bank()
                        t = mm(b, b.ap[:, 0:W], iT[o:o + 64, hh // 2, c * 128:c * 128 + 128], ikT[o:o + 64, 0:W],
                               waits=(t_I,), inc=True)
                        return b, t

                    nxt = index_mm(0)
                    for hh in range(8):
                        b, t = nxt
                        i = n % 2
                        n += 1
                        t = act(rl[i][:, 0:W], b.ap[:, 0:W], ACT.Relu, t, rl_free[i], OWN)
                        b.free(t)
                        if hh < 7:
                            nxt = index_mm(hh + 1)
                        if hh == 0:
                            t = ts(sc[:, 0:W], rl[i][:, 0:W], iw[:, c, 0:1], None, ALU.mult, None, t, t_I, OWN)
                        else:
                            t = stt(sc[:, 0:W], rl[i][:, 0:W], iw[:, c, hh:hh + 1], sc[:, 0:W], ALU.mult, ALU.add,
                                    t, ts_, OWN)
                        ts_ = t
                        rl_free[i] = t
                        if hh % 2:
                            yield
                    t = tt(sc[:, W - 128:W], sc[:, W - 128:W], cc("neg"), ALU.add)
                    for r_ in range(16):
                        src = sc if r_ == 0 else work
                        top8(m8, src[:, 0:W])
                        drop8(work[:, 0:W], m8, src[:, 0:W])
                        if r_ % 2:
                            yield
                    tt(sc[:, 0:W], work[:, 0:W], sc[:, 0:W], ALU.is_equal)
                    t_pens[c] = ts(sc[:, 0:W], sc[:, 0:W], PEN, None, ALU.mult, None)
                    pens[c] = sc
                tt(qf, qf, st8[:, 0:32].unsqueeze(2).to_broadcast([128, 32, 64]), ALU.mult)
                tt(qf, qf, row("g_qn_2", 64 * l, 64).unsqueeze(1).to_broadcast([128, 32, 64]), ALU.mult)
                yield
                t = rope_on(qt.rearrange("p c (n d) -> p c n d", n=8), 8)
                for j in range(4):
                    turned(qt, j, qT[:, j, :], t)
                yield
                tt(k3, k3, st8[:, 32:40].rearrange("p (c v) -> p c v", c=4).unsqueeze(3).to_broadcast([128, 4, 2, 64]),
                   ALU.mult)
                tt(k3, k3, row("g_kn_2", 64 * l, 64).unsqueeze(1).unsqueeze(1).to_broadcast([128, 4, 2, 64]),
                   ALU.mult)
                rope_on(k3, 2)
                t = cp(ksrc[:, :, :, 1, :], k3)
                turned(kt, 0, kT[0], t)
                got["k"] = turned(kt, 1, kT[1], t)
                yield

            units = [mqk_unit(j) for j in range(8)] + [mv_unit(n, c) for n in range(2) for c in range(4)] \
                + [gate_unit] + [mo_unit(j) for j in range(4)]
            fill_ = in_step(units)
            path = main_path()
            going = [True, True]
            step = 0
            while any(going):
                step += 1
                if going[0]:
                    going[0] = next(path, "end") != "end"
                if going[1] and (step < 9 or step % 2 == 0 or not going[0]):
                    going[1] = next(fill_, "end") != "end"

            behind = fence()
            lg, mrow, thr, e2r = q_flat[0:4, 0:512], ro_t[0:4, 0:512], ro_t[0:4, 512:1024], q_flat[0:4, 512:1024]
            f4, i4r, e4 = fr[0:4, :], ir[0:4, :], er[0:4, :]
            softplus(lg, f4, e4, e2r, -1.0)
            ts(lg, lg, -1.0, None, ALU.mult, None)
            one = sq[0][0:4, :]
            fill(one, 1.0)
            scan(f4, one, lg, ALU.add)
            tt(i4r, i4r, f4, ALU.subtract)
            scan(mrow, one, i4r, ALU.max)
            t_mrow = (V.sem, V.sem.n)
            t = tt(thr, f4, mrow, ALU.add)
            t_thr = act(thr, thr, ACT.Exp, t, scale=-1.0)
            b = bank()
            for c in range(4):
                t2 = tr(b, b.ap[:, c * 4:c * 4 + 4], i4r[:, c * 128:c * 128 + 128], waits=(t,), inc=(c == 3))
            aT = st8[:, 0:16]
            t_aT = cp(aT, b.ap[:, 0:16], t2)
            b.free(t_aT)
            behind = fence()

            sm = [q_flat[:, 0:512], q_flat[:, 512:1024], q_flat[:, 1024:1536], sq[3]]
            PT = [q_flat[:, 1536:2048], i_flat[:, 0:512]]
            dg, bcs = i_flat[:, 512:1024], i_flat[:, 1024:1536]
            sm_free, PT_free, misc_free = [None] * 4, [None] * 2, [None, None]
            bo = {}
            t_pv = {}
            t_exp = {}

            def att_unit(c, hh):
                def unit():
                    W = 128 * (c + 1)
                    n = 8 * c + hh
                    i, p = n % 4, n % 2
                    mx = st8[:, 16 + 8 * (c % 2) + hh:17 + 8 * (c % 2) + hh]
                    rsum = st8[:, 32 + 8 * (c % 2) + hh:33 + 8 * (c % 2) + hh]
                    o = 64 * (hh % 2)
                    b = bank()
                    t = mm(b, b.ap[:, 0:W], qT[o:o + 64, hh // 2, c * 128:c * 128 + 128], kT[hh // 4][o:o + 64, 0:W],
                           inc=True)
                    yield
                    t = tt(sm[i][:, 0:W], b.ap[:, 0:W], pens[c][:, 0:W], ALU.add, t, sm_free[i], OWN)
                    b.free(t)
                    t = reduce(mx, sm[i][:, 0:W], ALU.max, t, OWN)
                    t = ts(mx, mx, -0.125, None, ALU.mult, None, t, OWN)
                    yield
                    t = act(sm[i][:, 0:W], sm[i][:, 0:W], ACT.Exp, t, misc_free[0], OWN, bias=mx, scale=0.125, accum=rsum)
                    t_exp[(c, hh)] = t
                    yield
                    b = bank()
                    for kb in range(c + 1):
                        t2 = tr(b, b.ap[:, kb * 128:kb * 128 + 128], sm[i][:, kb * 128:kb * 128 + 128], waits=(t,),
                                inc=(kb == c))
                    sm_free[i] = t2
                    t = act(PT[p][:, 0:W], b.ap[:, 0:W], ACT.Copy, t2, PT_free[p], OWN)
                    b.free(t)
                    yield
                    if hh == 0:
                        bo[c] = bank()
                    d = bo[c].ap[o:o + 64, (hh // 2) * 128:(hh // 2) * 128 + 128]
                    for kb in range(c + 1):
                        t2 = mm(bo[c], d, vt[:, kb, (hh // 4) * 64:(hh // 4) * 64 + 64],
                                PT[p][:, kb * 128:kb * 128 + 128], start=(kb == 0), stop=(kb == c), waits=(t,),
                                inc=(kb == c))
                    PT_free[p] = t2
                    t_pv[c] = t2
                return unit

            def att_end(c):
                def unit():
                    yield
                    yield
                    yield
                    rsum = st8[:, 32 + 8 * (c % 2):40 + 8 * (c % 2)]
                    t_r = recip(rsum, rsum, t_exp[(c, 7)], OWN)
                    for g in range(2):
                        b = bank()
                        t = tt(dg.rearrange("p (n q) -> p n q", n=4), ident.unsqueeze(1).to_broadcast([128, 4, 128]),
                               rsum[:, g:8:2].unsqueeze(2).to_broadcast([128, 4, 128]), ALU.mult, t_r, misc_free[1],
                               OWN)
                        t = mm(b, b.ap[:, :], ones, dg, waits=(t,), inc=True)
                        misc_free[1] = t
                        yield
                        o = 64 * g
                        t = act(bcs[o:o + 64, :], b.ap[o:o + 64, :], ACT.Copy, t, got.get(("m", g)), OWN)
                        b.free(t)
                        t = tt(mix[o:o + 64, 0:4, c * 128:c * 128 + 128],
                               bo[c].ap[o:o + 64, :].rearrange("p (j q) -> p j q", j=4),
                               bcs[o:o + 64, :].rearrange("p (j q) -> p j q", j=4), ALU.mult, t, t_pv[c], OWN)
                        got[("m", g)] = t
                    misc_free[0] = t
                    bo[c].free(t)
                return unit

            dm = [kt_t[:, 0:512], kt_t[:, 512:1024]]
            pp = [sq[0], sq[1]]
            Mb = sq[2]
            dm_free, pp_free, Mb_free = [None] * 2, [None] * 2, [None]
            acc2 = {}

            def head_row(r_, hh):
                return ident[0:4, hh:hh + 1].to_broadcast([4, 128]), r_

            def ml_unit(hh, j):
                def unit():
                    W = 512 - 128 * j
                    i = (4 * hh + j) % 2
                    if j == 0:
                        bm = bank()
                        t = mm(bm, bm.ap[:, :], *head_row(mrow, hh), inc=True)
                        acc2["M"] = act(Mb, bm.ap[:, :], ACT.Copy, t, Mb_free[0], OWN)
                        bm.free(acc2["M"])
                    t = ts(dm[i][:, 0:W], Mb[:, 128 * j:512], aT[:, 4 * j + hh:4 * j + hh + 1], 0.0, ALU.subtract,
                           ALU.max, acc2["M"], dm_free[i], OWN)
                    Mb_free[0] = t
                    yield
                    t = act(dm[i][:, 0:W], dm[i][:, 0:W], ACT.Exp, t, OWN, scale=-1.0)
                    bs_ = bank()
                    t_s = mm(bs_, bs_.ap[:, 0:W], mk[:, hh, j * 128:j * 128 + 128], mq[:, hh, 128 * j:512], inc=True)
                    yield
                    t = stt(pp[i][:, 0:W], bs_.ap[:, 0:W], float(128 ** -0.5), dm[i][:, 0:W], ALU.mult, ALU.mult, t,
                            t_s, pp_free[i], OWN)
                    bs_.free(t)
                    dm_free[i] = t
                    t2 = tt(pp[i][:, 0:128], pp[i][:, 0:128], ule, ALU.mult, t, OWN, eng=G)
                    yield
                    if j == 0:
                        acc2[hh] = (bank(), bank())
                    bn, bden = acc2[hh]
                    mm(bden, bden.ap[:, 128 * j:512], ones, pp[i][:, 0:W], start=(j == 0), stop=(j == 3),
                       waits=(t, t2))
                    t_n = mm(bn, bn.ap[:, 128 * j:512], mv[:, j, hh * 128:hh * 128 + 128], pp[i][:, 0:W],
                             start=(j == 0), stop=(j == 3), inc=True)
                    pp_free[i] = t_n
                    if j < 3:
                        return
                    bt = bank()
                    t_t = mm(bt, bt.ap[:, :], *head_row(thr, hh), inc=True)
                    yield
                    hm = mk[:, hh, :]
                    t = act(hm, bden.ap[:, :], ACT.Abs, t_n, OWN)
                    bden.free(t)
                    t = tt(hm, hm, bt.ap[:, :], ALU.max, t, t_t, OWN)
                    bt.free(t)
                    t = recip(hm, hm, t, OWN)
                    t = tt(hm, hm, bn.ap[:, :], ALU.mult, t, OWN)
                    bn.free(t)
                    got[("h", hh)] = t
                return unit

            att = in_step([f_ for c in range(4) for f_ in [att_unit(c, hh) for hh in range(8)] + [att_end(c)]])
            mls = in_step([ml_unit(hh, j) for hh in range(4) for j in range(4)])
            going = [True, True]
            step = 0
            while any(going):
                step += 1
                if going[0]:
                    going[0] = next(att, "end") != "end"
                if going[1] and (step % 2 == 0 or not going[0]):
                    going[1] = next(mls, "end") != "end"
            tsq = []
            for hh in range(4):
                t = act(mq[:, hh, :], mk[:, hh, :], ACT.Square, got[("h", hh)], OWN)
                b = bank()
                tsq.append((b, mm(b, b.ap[:, :], ones, mq[:, hh, :], waits=(t,), inc=True)))
            for hh, (b, t) in enumerate(tsq):
                t = act(mq[:, hh, :], b.ap[:, :], ACT.Sqrt, t, OWN, bias=eps[:, 0:1], scale=1.0 / 128)
                b.free(t)
                t = recip(mq[:, hh, :], mq[:, hh, :], t, OWN)
                tsq[hh] = t
            t_mix2 = []
            for hh in range(4):
                t = stt(mk[:, hh, :], mk[:, hh, :], pc("g_mh_2", 4 * l + hh), mq[:, hh, :], ALU.mult, ALU.mult,
                        tsq[hh], OWN)
                t = tt(mix[:, 4 + hh, :], mk[:, hh, :], mo[:, hh, :], ALU.mult, t, OWN)
            f = fence()

            close(0)
            acts = region(f"acts{l}", 16384, F32R)
            U = [[acts[:, (2 * u + v) * 4096:(2 * u + v + 1) * 4096].rearrange("p (j t) -> p j t", j=8)
                  for v in range(2)] for u in range(2)]
            arena = region(f"arena_f{l}", 1536)
            use(arena, 1536)
            sq = [tmp(512) for _ in range(2)]
            rs = tmp(512)
            uu = [mix[:, i, :] for i in range(4)]
            toks[:] = t_h
            t_xn = split_x(mix, None, [None] * 8)
            project(Ln.wout, (xh, xl), t_xn, add_h)
            t_xn = rms("g_mlp_2", l, toks)
            rs_of = [None]
            U_free = [[], []]
            U_tok = [[None] * 8, [None] * 8]
            ufree = [[(V.sem, V.sem.n), (S.sem, S.sem.n)] for _ in range(4)]
            nu = [0]

            def ff_up(g):
                for jl in range(8):
                    s = Ln.up[g][jl // 2]
                    b, t = product(s, jl % 2, (xh, xl), T, t_xn)
                    freed(s, jl % 2, t)
                    if rs_of[0] is None:
                        rs_of[0] = norm_stats(h, toks, sq, T, rs)
                    i = nu[0] % 4
                    nu[0] += 1
                    t = stt(uu[i], b.ap[:, :], 0.0, rs, ALU.max, ALU.mult, t, rs_of[0], *ufree[i])
                    b.free(t)
                    t1 = act(U[g % 2][0][:, jl, :], uu[i], ACT.Square, t, *U_free[g % 2])
                    t2 = tt(uu[i], uu[i], uu[i], ALU.mult, t1)
                    t2 = tt(U[g % 2][1][:, jl, :], uu[i], U[g % 2][0][:, jl, :].bitcast(F32), ALU.subtract, t2, t1,
                            *U_free[g % 2])
                    U_tok[g % 2][jl] = [t1, t2]
                    ufree[i] = [t2]

            lo_eng[0] = G
            ff_up(0)
            ff_up(1)
            down(Ln.dn[0], 0, 8, add_h)
            ff_up(2)
            down(Ln.dn[1], 1, 8, add_h)
            ff_up(3)
            down(Ln.dn[2], 2, 8, add_h)
            down(Ln.dn[3], 3, 8, add_h)
            lo_eng[0] = None

            t_xn = rms("g_ple_2", l, toks)
            f = fence()
            close(0)
            arena = region(f"arena_p{l}", 12000)
            use(arena, 12000)
            sq = [tmp(512) for _ in range(4)]
            rs = tmp(512)
            pst = tmp(1024).rearrange("p (c d) -> p c d", c=4)
            pT = tmp(1024).rearrange("p (k t) -> p k t", k=2)
            pw_ = tmp(4096).rearrange("p (j t) -> p j t", j=8)
            gates = tmp(1024).rearrange("p (j t) -> p j t", j=2)
            t_p = S.dma(s_p, lambda e, l=l, pst=pst: e.dma_start(
                pst, A["p_2"][l].rearrange("a (c p) d -> p (a c) d", p=128)), *f)
            for k in range(2):
                b = bank()
                for c in range(4):
                    t = tr(b, b.ap[:, c * 128:c * 128 + 128], pst[:, c, k * 128:k * 128 + 128], waits=(t_p,),
                           inc=(c == 3))
                t_pT = evac(pT[:, k, :], b.ap[:, :], t)
                b.free(t_pT)
                E.wait(t_pT)
            raw(Ln.ple)
            t_pw = []
            for j in range(8):
                b = bank()
                for k in range(2):
                    t = mm(b, b.ap[:, :], Ln.ple.ap[:, k, j * 128:j * 128 + 128], pT[:, k, :], start=(k == 0),
                           stop=(k == 1), waits=(Ln.ple.tok,), inc=(k == 1))
                t2 = evac(pw_[:, j, :], b.ap[:, :], t)
                b.free(t2)
                t_pw.append(t2)
            done(Ln.ple, t)
            t_rs = norm_stats(h, toks, sq, T, rs)
            gfree = [[], []]

            def gate_fn(j, b, t):
                g = gates[:, j % 2, :]
                t = tt(g, b.ap[:, :], rs, ALU.mult, t, t_rs, *gfree[j % 2])
                b.free(t)
                t = act(g, g, ACT.Sigmoid, t, bias=pc("b_ple_gate_2", 8 * l + j))
                t = tt(g, g, pw_[:, j, :], ALU.mult, t, t_pw[j])
                toks[j] = tt(h[:, j, :], h[:, j, :], g, ALU.add)
                gfree[j % 2] = [toks[j]]

            project(Ln.pg, (xh, xl), t_xn, gate_fn)
            t_h = list(toks)
            fence()

        ot = mix_t[:, :].rearrange("p (c d) -> p c d", c=4)
        for c in range(4):
            for jj in range(2):
                b = bank()
                for q in range(4):
                    j = 4 * jj + q
                    t = tr(b, b.ap[:, q * 128:q * 128 + 128], h[:, j, c * 128:c * 128 + 128], waits=(t_h[j],),
                           inc=(q == 3))
                t = evac(ot[:, c, jj * 512:jj * 512 + 512], b.ap[:, :], t)
                b.free(t)
                D.wait(t)
            t_out = D.dma(s_out, lambda e, c=c: e.dma_start(out[0, c * 128:c * 128 + 128, :], ot[:, c, :]))
        D.wait(t_out)

        block = ctx.enter_context(nc.Block())

        @block.sync
        def _(eng):
            D.play(eng)

        @block.gpsimd
        def _(eng):
            G.play(eng)

        @block.scalar
        def _(eng):
            S.play(eng)

        @block.tensor
        def _(eng):
            E.play(eng)

        @block.vector
        def _(eng):
            V.play(eng)


_INS = ["x", "c", "ctx", "c_ctx", "w_ada", "b_ada", "w_in", "ssd_conv_w", "ssd_conv_b", "ssd_dt_bias", "ssd_a_log",
        "ssd_d", "ssd_norm_w", "fnet_w", "pool_w", "pool_scale", "w_out", "ln1_g", "ln1_b", "ffn_w_up", "ffn_conv_w",
        "ffn_conv_b", "ffn_w_down", "ln2_g", "ln2_b", "p_2", "positions_2", "g_mix_2", "w_in_2", "g_cq_2",
        "w_q_up_2", "w_iq_up_2", "g_qn_2", "g_kn_2", "g_ik_2", "conv_w_2", "conv_b_2", "i_bias_2", "f_bias_2",
        "g_mh_2", "w_out_2", "g_mlp_2", "w_ff1_2", "w_ff2_2", "g_ple_2", "w_ple_gate_2", "b_ple_gate_2", "w_ple_2"]
_FLAT = {1: "", 2: "a b -> (a b)", 3: "a b c -> (a b c)", 4: "a b c d -> (a b c d)"}


def kernel(**inputs):
    import concourse.bacc as _bacc
    from concourse.bass_utils import run_bass_kernel_spmd as _run

    nc = _bacc.Bacc("TRN2", target_bir_lowering=False, num_devices=1)
    arrays, A = {}, {"_flat": {}}
    for name in _INS:
        a = np.ascontiguousarray(inputs[name])
        arrays[f"in_{name}_dram"] = a
        A[name] = nc.dram_tensor(f"in_{name}_dram", a.shape, mybir.dt.from_np(a.dtype), kind="ExternalInput").ap()
        A["_flat"][name] = _FLAT[a.ndim]
    for name, a in const_arrays().items():
        arrays[f"in_{name}_dram"] = a
        A[name] = nc.dram_tensor(f"in_{name}_dram", a.shape, F32, kind="ExternalInput").ap()
    out = nc.dram_tensor("out_0_dram", (1, T, 1024), F32, kind="ExternalOutput").ap()
    build(nc, A, out)
    r = _run(nc, [arrays], core_ids=[0])
    return r.results[0]["out_0_dram"]
```

```python
from contextlib import ExitStack

import numpy as np
import concourse.bass as bass
from concourse import mybir

ALU = mybir.AluOpType
ACT = mybir.ActivationFunctionType
F32 = mybir.dt.float32
I32 = mybir.dt.int32
F32R = mybir.dt.float32r
X = mybir.AxisListType.X

T = 512
TC = 256
EPS = 1e-6
ALPHA = 2.0 ** 0.25
NEG = -3.0e38
GONE = -3.3e38
PEN = -1.0e30
FF1 = 2816
FF2 = 4096
NSLOT = 2
SLOT = 2048
TWO_PI = 2.0 * np.pi
C1 = 6.28125
C2 = float(np.float32(np.floor((TWO_PI - 6.28125) * 2.0 ** 20) / 2.0 ** 20))
C3 = float(np.float32(TWO_PI - 6.28125 - C2))
MAGIC = 12582912.0


def const_layout():
    names = [("ident", 128), ("ule", 128), ("uge", 128), ("ugt", 128), ("ult", 128), ("ones", 128),
             ("mean", 128), ("neg", 128), ("pen", 128), ("freq", 8), ("sel", 16)]
    at, n = {}, 0
    for name, w in names:
        at[name] = n
        n += w
    return at, n


def const_arrays():
    at, n = const_layout()
    c = np.zeros((128, n), np.float32)
    p = np.arange(128)[:, None]
    f = np.arange(128)[None, :]

    def put(name, v):
        v = np.asarray(v, np.float32)
        c[:v.shape[0], at[name]:at[name] + v.shape[1]] = v

    put("ident", p == f)
    put("ule", p <= f)
    put("uge", p >= f)
    put("ugt", p > f)
    put("ult", p < f)
    put("ones", np.ones((128, 128)))
    put("mean", np.full((128, 128), 1.0 / 1024))
    put("neg", np.where(f <= p, 0.0, NEG))
    put("pen", np.where(f <= p, 0.0, PEN))
    put("sel", np.broadcast_to(np.eye(4).reshape(1, 16), (128, 16)))
    q = np.arange(64)
    ang = 2 * np.pi * (np.outer(q, q) % 64) / 64
    d = np.zeros((128, 256))
    for g in range(2):
        d[g * 64:g * 64 + 64, g * 64:g * 64 + 64] = np.cos(ang) / 8
        d[g * 64:g * 64 + 64, 128 + g * 64:128 + g * 64 + 64] = np.sin(ang) / 8
    c1 = np.zeros((128, 1280), np.float32)
    c1[:, 0:256] = d
    pos = np.arange(T)
    inv = np.zeros((128, 1024))
    for g, w in enumerate((2, 4, 8, 16)):
        left = w // 2
        hi = np.minimum(pos + w - left, T)
        lo = np.maximum(pos - left, 0)
        i, half = g // 2, g % 2
        inv[half * 64:half * 64 + 64, i * 512:i * 512 + 512] = 1.0 / (hi - lo)
    c1[:, 256:1280] = inv
    fr = np.float32(500000.0) ** (-(np.arange(8, dtype=np.float32) * np.float32(2.0)) / np.float32(16))
    put("freq", np.broadcast_to(fr[None, :], (128, 8)))
    k = np.arange(T)
    a = 2 * np.pi * (np.outer(k, k) % T) / T
    dl = np.stack([np.cos(a), -np.sin(a)]).astype(np.float64) / np.sqrt(512.0)
    return {"consts": c, "consts1": c1, "dftl": dl.astype(np.float32)}


PARAMS = [("c", 8), ("c_ctx", 8), ("b_ada", 48), ("ssd_conv_w", 24), ("ssd_conv_b", 8), ("ssd_norm_w", 4),
          ("pool_scale", 2), ("ln1_g", 8), ("ln1_b", 8), ("ffn_conv_w", 396), ("ffn_conv_b", 44), ("ln2_g", 8),
          ("ln2_b", 8), ("g_mix_2", 16), ("g_cq_2", 4), ("conv_w_2", 64), ("conv_b_2", 16), ("g_mh_2", 8),
          ("g_mlp_2", 16), ("g_ple_2", 16), ("b_ple_gate_2", 16)]
ROWS = [("ssd_dt_bias", 16), ("ssd_a_log", 16), ("ssd_d", 8), ("g_qn_2", 128), ("g_kn_2", 128), ("g_ik_2", 128)]


def offsets(table):
    at, n = {}, 0
    for name, w in table:
        at[name] = n
        n += w
    return at, n


LAST4 = [4, 5, 6, 7, 0, 1, 2, 3]
OWN = object()


class Sem:

    def __init__(self, h):
        self.h, self.n = h, 0

    def add(self, k):
        self.n += k
        return (self, self.n)


class Eng:

    def __init__(self, sem, chain):
        self.sem, self.chain, self.q, self.seen = sem, chain, [], {}

    def wait(self, *toks):
        for t in toks:
            if t is None or t is OWN:
                continue
            if isinstance(t, list):
                self.wait(*t)
                continue
            s, v = t
            if self.seen.get(id(s), 0) < v:
                self.seen[id(s)] = v
                self.q.append(("w", s.h, v))

    def do(self, fn, *toks, inc=True):
        self.wait(*toks)
        if self.chain and self.sem.n and OWN not in toks:
            self.wait((self.sem, self.sem.n))
        if inc:
            self.q.append(("i", fn, self.sem.h, 1))
            return self.sem.add(1)
        self.q.append(("i", fn, None, 0))
        return None

    def dma(self, sem, fn, *toks):
        self.wait(*toks)
        self.q.append(("i", fn, sem.h, 16))
        return sem.add(16)

    def play(self, eng):
        for it in self.q:
            if it[0] == "w":
                eng.wait_ge(it[1], it[2])
            else:
                ins = it[1](eng)
                if it[2] is not None:
                    ins.then_inc(it[2], it[3])


class Bank:
    def __init__(self, ap):
        self.ap, self.toks, self.idle, self.age = ap, [], True, 0

    def free(self, *toks):
        Bank.now += 1
        self.toks, self.idle, self.age = list(toks), True, Bank.now


Bank.now = 0


def in_step(units, more=lambda: False):
    live = []
    while units or live or more():
        for u in list(live):
            if next(u, "end") == "end":
                live.remove(u)
        if units:
            u = units.pop(0)()
            next(u, None)
            live.append(u)
        yield


def build(nc, A, out):
    cat, cn = const_layout()
    pat, pn = offsets(PARAMS)
    rat, rn = offsets(ROWS)
    NPT = (pn + 127) // 128

    with ExitStack() as ctx:
        def sb(name, n, dt=F32, p=128):
            return ctx.enter_context(nc.sbuf_tensor(name, [p, n], dt))

        sems = {}

        def sem(name):
            sems[name] = Sem(ctx.enter_context(nc.semaphore(name)))
            return sems[name]

        V = Eng(sem("s_dve"), True)
        S = Eng(sem("s_act"), True)
        G = Eng(sem("s_pool"), True)
        E = Eng(sem("s_pe"), False)
        D = Eng(sem("s_sp"), False)
        s_slot = [sem(f"s_slot{i}") for i in range(NSLOT)]
        s_con, s_wq, s_con1, s_par, s_row, s_x, s_cx, s_fw, s_pw, s_gb, s_pos, s_p, s_out = [
            sem(n) for n in ("s_con", "s_wq", "s_con1", "s_par", "s_row", "s_x", "s_cx", "s_fw", "s_pw", "s_gb", "s_pos", "s_p",
                             "s_out")]

        h_t = sb("h", 4096)
        xh_t = sb("xh", 4096, F32R)
        xl_t = sb("xl", 4096, F32R)
        wh_t = sb("wh", 2 * SLOT, F32R)
        wl_t = sb("wl", 2 * SLOT, F32R)
        mix_t = sb("mix", 4096)
        ring = sb("ring", NSLOT * SLOT)
        con = sb("con", cn)
        par = sb("par", pn)
        rb = sb("rb", rn)
        mod = sb("mod", 96)
        fw = sb("fw", 128)
        pw = sb("pw", 128)
        gb = sb("gb", 8)
        posi = sb("posi", 4, I32)
        rope = sb("rope", 64)
        eps = sb("eps", 2)
        csil_t = sb("csil", 16)
        scope = [ctx.enter_context(ExitStack()), ctx.enter_context(ExitStack())]
        small = sb("small", 1024)
        arena_n = [0, 0, None]

        def region(name, n, dt=F32, lvl=0):
            return scope[lvl].enter_context(nc.sbuf_tensor(name, [128, n], dt))

        def close(lvl):
            for i in range(1, lvl - 1, -1):
                scope[i].close()
                scope[i] = ctx.enter_context(ExitStack())

        def use(t, n, at=0):
            arena_n[0], arena_n[1], arena_n[2] = at, n, t

        def reset(to=0):
            arena_n[0] = to

        def tmp(n):
            a = arena_n[0]
            arena_n[0] += n
            assert arena_n[0] <= arena_n[1], arena_n[0]
            return arena_n[2][:, a:a + n]

        h = h_t[:, :].rearrange("p (j t) -> p j t", j=8)
        xh = xh_t[:, :].rearrange("p (j t) -> p j t", j=8)
        xl = xl_t[:, :].rearrange("p (j t) -> p j t", j=8)
        mix = mix_t[:, :].rearrange("p (j t) -> p j t", j=8)

        def cc(name, w=128, p=128):
            return con[0:p, cat[name]:cat[name] + w]

        ident, ule, uge, ones = cc("ident"), cc("ule"), cc("uge"), cc("ones")

        def pc(name, j, w=1):
            return par[:, pat[name] + j:pat[name] + j + w]

        def row(name, o, w):
            return rb[:, rat[name] + o:rat[name] + o + w]

        banks = [Bank(ctx.enter_context(nc.psum_tensor(f"ps{i}", [128, 512], F32))) for i in range(8)]
        turn = [0]

        def bank():
            b = min((x for x in banks if x.idle), key=lambda x: x.age)
            b.idle = False
            return b

        def mm(b, out_ap, lhsT, rhs, start=True, stop=True, waits=(), inc=False):
            if start:
                E.wait(*b.toks)
            return E.do(lambda e: e.matmul(out_ap, lhsT, rhs, start=start, stop=stop), *waits, inc=inc)

        def tr(b, out_ap, src, waits=(), inc=False):
            p = src.shape[0]
            E.wait(*b.toks)
            return E.do(lambda e: e.transpose(out_ap, src, con[0:p, cat["ident"]:cat["ident"] + p]), *waits, inc=inc)

        def act(out_ap, in_ap, func, *toks, bias=0.0, scale=1.0, accum=None):
            if accum is None:
                return S.do(lambda e: e.activation(out_ap, in_ap, func, bias=bias, scale=scale), *toks)
            return S.do(lambda e: e.activation(out_ap, in_ap, func, bias=bias, scale=scale, accum_out=accum), *toks)

        def tt(out_ap, a, b, op, *toks, eng=None):
            return (eng or V).do(lambda e: e.tensor_tensor(out_ap, a, b, op), *toks)

        def ts(out_ap, a, s1, s2, op0, op1, *toks, eng=None):
            if op1 is None:
                return (eng or V).do(lambda e: e.tensor_scalar(out_ap, a, s1, None, op0), *toks)
            return (eng or V).do(lambda e: e.tensor_scalar(out_ap, a, s1, s2, op0, op1), *toks)

        def stt(out_ap, a, s, b, op0, op1, *toks):
            return V.do(lambda e: e.scalar_tensor_tensor(out=out_ap, in0=a, scalar=s, in1=b, op0=op0, op1=op1), *toks)

        def ttr(out_ap, a, b, scale, acc, op0, op1, *toks):
            return V.do(lambda e: e.tensor_tensor_reduce(out=out_ap, in0=a, in1=b, scale=scale, scalar=-3.0e38, op0=op0,
                                                         op1=op1, accum_out=acc), *toks)

        def recip(out_ap, a, *toks):
            return V.do(lambda e: e.reciprocal(out_ap, a), *toks)

        def reduce(out_ap, a, op, *toks):
            return V.do(lambda e: e.tensor_reduce(out_ap, a, X, op), *toks)

        def fill(out_ap, v, *toks):
            return V.do(lambda e: e.memset(out_ap, v), *toks)

        def scan(out_ap, one, a, op):
            return V.do(lambda e: e.tensor_tensor_scan(out_ap, one, a, 0.0, ALU.mult, op))

        def top8(m8, a, *toks):
            return V.do(lambda e: e.max(m8, a), *toks)

        def drop8(out_ap, m8, a, *toks):
            return V.do(lambda e: e.match_replace(out_ap, m8, a, GONE), *toks)

        def cp(out_ap, a, *toks, eng=None):
            if eng is S:
                return act(out_ap, a, ACT.Copy, *toks)
            return (eng or V).do(lambda e: e.tensor_copy(out_ap, a), *toks)

        def fence():
            now = [(e.sem, e.sem.n) for e in (V, S, G, E) if e.sem.n]
            for e in (V, S, G, E):
                e.wait(*now)
            return now

        class Load:
            pass

        loads = []
        order = []
        head = [0, 0, 0, 0]

        def plan(src, kt, w, split=True, halves=(0, 1)):
            s = Load()
            s.src, s.kt, s.w, s.split, s.users, s.toks, s.tok = src, kt, w, split, (2 if split and w > 128 else 1), [], None
            loads.append(s)
            if split:
                s.at = head[2] % 2
                head[2] += 1
                s.part = {}
                for hf in halves[:s.users]:
                    order.append((s, hf))
            return s

        split_free = [[[], []], [[], []]]

        def pump():
            while head[0] < len(loads):
                i = head[0]
                if i >= NSLOT and loads[i - NSLOT].users:
                    return
                s = loads[i]
                prev = loads[i - NSLOT].toks if i >= NSLOT else []
                o = i % NSLOT * SLOT
                s.ap = ring[:, o:o + s.kt * s.w].rearrange("p (k n) -> p k n", k=s.kt)
                v = s.src.rearrange("(k p) n -> p k n", p=128)
                s.tok = D.dma(s_slot[i % NSLOT], lambda e, s=s, v=v: e.dma_start(s.ap, v), *prev)
                head[0] += 1

        lo_eng = [None]
        x_read = [None]

        def split_next():
            s, hf = order[head[1]]
            if s.tok is None:
                return False
            head[1] += 1
            a, w = 128 * hf, min(128, s.w - 128 * hf)
            wide = 256 if s.w > 128 else s.w
            o = s.at * SLOT
            hi = wh_t[:, o:o + s.kt * wide].rearrange("p (k n) -> p k n", k=s.kt)
            lo = wl_t[:, o:o + s.kt * wide].rearrange("p (k n) -> p k n", k=s.kt)
            both = split_free[s.at]
            fr = both[hf] if s.w > 128 else both[0] + both[1]
            t1 = act(hi[:, :, a:a + w], s.ap[:, :, a:a + w], ACT.Copy, s.tok, *fr)
            t2 = tt(lo[:, :, a:a + w], s.ap[:, :, a:a + w], hi[:, :, a:a + w].bitcast(F32), ALU.subtract, t1, s.tok,
                    *fr, eng=lo_eng[0])
            both[hf] = None
            if s.w <= 128:
                both[1] = None
            s.hi, s.lo = hi, lo
            s.part[hf] = [t1, t2]
            s.toks += [t1, t2]
            s.users -= 1
            pump()
            return True

        def need(s, hf, ahead=3):
            pump()
            while hf not in s.part:
                assert split_next()
            for _ in range(ahead):
                if head[1] >= len(order):
                    break
                n, nh = order[head[1]]
                fr = split_free[n.at]
                if n.tok is None or fr[nh] is None or (n.w <= 128 and fr[1] is None):
                    break
                split_next()
            return s.part[hf]

        def freed(s, hf, tok):
            split_free[s.at][hf] = [tok]
            if s.w <= 128:
                split_free[s.at][1] = [tok]

        def raw(s):
            pump()
            assert s.tok is not None
            return s

        def done(s, tok):
            s.toks.append(tok)
            s.users -= 1
            pump()

        def mm3(b, out_ap, a, x, start, stop, waits=(), inc=False):
            mm(b, out_ap, a[0], x[0], start=start, stop=False, waits=waits)
            mm(b, out_ap, a[0], x[1], start=False, stop=False)
            return mm(b, out_ap, a[1], x[0], start=False, stop=stop, inc=inc)

        t_con = D.dma(s_con, lambda e: e.dma_start(con[:, :], A["consts"]))
        N1 = 16240
        arena = region("arena", N1)
        use(arena, N1)
        csil = csil_t[:, :].rearrange("p (k w) -> p k w", w=2)
        arow = [tmp(512), tmp(512)]
        con1 = tmp(1280)
        t_con1 = S.dma(s_con1, lambda e: e.dma_start(con1, A["consts1"]))
        lo = arena_n[0]
        stage = tmp(NPT * 128)
        w_in, w_up, w_dn = A["w_in"][0], A["ffn_w_up"][0], A["ffn_w_down"][0]
        GR = (8, 8, 6)

        def cols_of(W, o, n, w=256):
            return [plan(W[:, o + i * w:o + i * w + w], 8, w) for i in range(n)]

        def plan_ada(n):
            return [plan(A["w_ada"][0, :, i * 256:i * 256 + 256], 8, 256, split=False) for i in n]

        L_ada = plan_ada(range(8))
        L_xbc = cols_of(w_in, 512, 4)
        L_dt = plan(w_in[:, 1536:1552], 8, 16)
        L_fp = cols_of(w_in, 1552, 2)
        L_z = cols_of(w_in, 0, 1)
        L_dft = [plan(A["dftl"][i], 4, 512, split=False) for i in range(2)]
        L_ada += plan_ada(range(8, 10))
        L_z += cols_of(w_in, 256, 1)
        L_ada += plan_ada(range(10, 20))
        L_wout = cols_of(A["w_out"][0], 0, 1)
        L_ada += plan_ada(range(20, 22))
        L_wout += cols_of(A["w_out"][0], 256, 2)
        L_ada += plan_ada(range(22, 24))
        L_wout += cols_of(A["w_out"][0], 768, 1)

        def plan_up(g):
            out_ = []
            for jp in range(GR[g] // 2):
                o = (sum(GR[:g]) // 2 + jp) * 256
                n0 = len(order)
                sg = plan(w_up[:, FF1 + o:FF1 + o + 256], 8, 256)
                sv = plan(w_up[:, o:o + 256], 8, 256)
                order[n0:] = [(sg, 0), (sv, 0), (sg, 1), (sv, 1)]
                out_.append((sg, sv))
            return out_

        def plan_down(W, k0, kt):
            return [plan(W[k0 * 128:(k0 + kt) * 128, i * 256:i * 256 + 256], kt, 256) for i in range(4)]

        L_up, L_dn = [None] * 3, [None] * 3
        for kind, g in (("u", 0), ("u", 1), ("d", 0), ("u", 2), ("d", 1), ("d", 2)):
            if kind == "u":
                L_up[g] = plan_up(g)
            else:
                L_dn[g] = plan_down(w_dn, sum(GR[:g]), GR[g])
        L2 = []
        for l in range(2):
            n = Load()
            w2 = A["w_in_2"][l]
            n.tok_ = cols_of(w2, 0, 3)
            n.mqk = cols_of(w2, 584, 4)
            n.mv = cols_of(w2, 1608, 1)
            n.gate = plan(w2[:, 2632:2640], 8, 8)
            n.mv += cols_of(w2, 1864, 1)
            n.mo = cols_of(w2, 2120, 2)
            n.wout = cols_of(A["w_out_2"][l], 0, 4)
            n.up, n.dn = [None] * 4, [None] * 4
            for kind, g in (("u", 0), ("u", 1), ("d", 0), ("u", 2), ("d", 1), ("u", 3), ("d", 2), ("d", 3)):
                if kind == "u":
                    n.up[g] = cols_of(A["w_ff1_2"][l], g * 1024, 4)
                else:
                    n.dn[g] = plan_down(A["w_ff2_2"][l], 8 * g, 8)
            n.ple = plan(A["w_ple_2"][l], 2, 1024, split=False)
            n.pg = cols_of(A["w_ple_gate_2"][l], 0, 4)
            L2.append(n)

        r = 0
        for name, w in PARAMS:
            src = A[name].rearrange(A["_flat"][name]) if A["_flat"][name] else A[name]
            src = src.rearrange("(r f) -> r f", f=128)
            a = 0
            while a < w:
                n = min(w - a, 128 - r % 128)
                t, q = r // 128, r % 128
                dst, sr = stage[q:q + n, t * 128:t * 128 + 128], src[a:a + n, :]
                t_par = D.dma(s_par, lambda e, dst=dst, sr=sr: e.dma_start(dst, sr))
                a += n
                r += n
        rowp = tmp(512)
        for name, w in ROWS:
            src = A[name].rearrange(A["_flat"][name]) if A["_flat"][name] else A[name]
            src = src.rearrange("(a f) -> a f", a=1)
            dst = rowp[0:1, rat[name]:rat[name] + w]
            t_row = S.dma(s_row, lambda e, dst=dst, src=src: e.dma_start(dst, src))
        xs_t = mix_t[:, :].rearrange("p (c d) -> p c d", c=4)
        cs_t = tmp(2048).rearrange("p (c d) -> p c d", c=2)
        t_x = S.dma(s_x, lambda e: e.dma_start(xs_t, A["x"].rearrange("a (c p) d -> p (a c) d", p=128)))
        t_cx = S.dma(s_cx, lambda e: e.dma_start(cs_t, A["ctx"].rearrange("a (c p) d -> p (a c) d", p=128)))
        fw3 = fw[:, :].rearrange("p (i d) -> p i d", i=2)
        pw3 = pw[:, :].rearrange("p (i d) -> p i d", i=2)
        t_fw = S.dma(s_fw, lambda e: e.dma_start(fw3, A["fnet_w"].rearrange("a (i g) c d -> (g c) (a i) d", i=2)))
        t_pw = S.dma(s_pw, lambda e: e.dma_start(pw3, A["pool_w"].rearrange("a (i g) c d -> (g c) (a i) d", i=2)))
        for n, name in enumerate(("i_bias_2", "f_bias_2")):
            src = A[name].rearrange("l h -> h l")
            dst = gb[0:4, 2 * n:2 * n + 2]
            t_gb = S.dma(s_gb, lambda e, dst=dst, src=src: e.dma_start(dst, src, allow_slow_non_contiguous=True))
        t_pos = S.dma(s_pos, lambda e: e.dma_start(
            posi[:, :], A["positions_2"].rearrange("a (c p) -> p (a c)", p=128), allow_slow_non_contiguous=True))

        fill(eps[:, 0:1], EPS)
        t_eps = fill(eps[:, 1:2], 1.0)
        S.wait(t_eps)
        E.wait(t_con)
        V.wait(t_con)
        G.wait(t_con)

        for i in range(NPT):
            n = min(128, pn - i * 128)
            b = bank()
            t = tr(b, b.ap[:, 0:n], stage[0:n, i * 128:i * 128 + 128], waits=(t_par,), inc=True)
            t_parT = cp(par[:, i * 128:i * 128 + n], b.ap[:, 0:n], t)
            b.free(t_parT)
        S.wait(t_parT)
        b = bank()
        t = mm(b, b.ap[:, 0:rn], ones[0:1, :], rowp[0:1, 0:rn], waits=(t_row,), inc=True)
        t_rb = cp(rb[:, :], b.ap[:, 0:rn], t)
        b.free(t_rb)

        act(csil[:, :, 0], pc("c", 0, 8), ACT.Silu)
        t_cs = act(csil[:, :, 1], pc("c_ctx", 0, 8), ACT.Silu)

        mod3 = mod[:, :].rearrange("p (j w) -> p j w", w=2)
        ada_n = [0]
        arow_free = [[], []]

        def ada_unit():
            i = ada_n[0]
            ada_n[0] += 1
            b = bank()
            for half in range(2):
                s = raw(L_ada[2 * i + half])
                for k in range(8):
                    t = mm(b, b.ap[0:2, half * 256:half * 256 + 256], csil[:, k, :], s.ap[:, k, :],
                           start=(k == 0), stop=(k == 7), waits=(s.tok, t_cs), inc=(k == 7))
                done(s, t)
                if half == 0:
                    yield
            ar = arow[i % 2]
            t = cp(ar[0:2, :], b.ap[0:2, :], t, *arow_free[i % 2], OWN, eng=S)
            b.free(t)
            yield
            b = bank()
            for q in range(4):
                t2 = tr(b, b.ap[:, 2 * q:2 * q + 2], ar[0:2, q * 128:q * 128 + 128], waits=(t,), inc=(q == 3))
            arow_free[i % 2] = [t2]
            t = tt(mod3[:, 4 * i:4 * i + 4, :], b.ap[:, 0:8].rearrange("p (j w) -> p j w", w=2),
                   pc("b_ada", 4 * i, 4).unsqueeze(2).to_broadcast([128, 4, 2]), ALU.add, t2)
            b.free(t)
            if i // 2 in (1, 4):
                t = ts(mod3[:, 4 * i:4 * i + 4, :], mod3[:, 4 * i:4 * i + 4, :], 1.0, None, ALU.add, None)
            t_modn[0] = t

        t_modn = [None]

        def ada_block():
            for _ in ada_unit():
                pass
            return t_modn[0]

        flip = [0]

        def evac(out_ap, in_ap, *toks):
            flip[0] ^= 1
            return cp(out_ap, in_ap, *toks, eng=S if flip[0] else V)

        t_h = []
        ada_block()
        for j in range(8):
            b = bank()
            for c in range(4):
                t = tr(b, b.ap[:, c * 128:c * 128 + 128], xs_t[:, c, j * 128:j * 128 + 128], waits=(t_x,), inc=(c == 3))
            t = evac(h[:, j, :], b.ap[:, :], t)
            b.free(t)
            t_h.append(t)
        hc = tmp(2048).rearrange("p (j t) -> p j t", j=8)
        xc_ctx = tmp(2048).rearrange("p (j t) -> p j t", j=8)
        t_hc = []
        for jj in range(4):
            b = bank()
            for q in range(4):
                j, c = 2 * jj + q // 2, q % 2
                t = tr(b, b.ap[:, q * 128:q * 128 + 128], cs_t[:, c, j * 128:j * 128 + 128], waits=(t_cx,),
                       inc=(q == 3))
            t = evac(hc[:, 2 * jj:2 * jj + 2, :], b.ap[:, :].rearrange("p (j t) -> p j t", j=2), t)
            b.free(t)
            t_hc += [t, t]

        def norm_stats(src, toks, sq, n, rs, center=None, count=1024, between=None, sq_first=False):
            xt = list(toks)
            if center is not None:
                b = bank()
                for j in range(8):
                    t = mm(b, b.ap[:, 0:n], cc("mean"), src[:, j, :], start=(j == 0), stop=(j == 7),
                           waits=(toks[j],), inc=(j == 7))
                for j in range(8):
                    xt[j] = tt(center[:, j, :], src[:, j, :], b.ap[:, 0:n], ALU.subtract, t, toks[j], OWN)
                b.free(xt[7])
                src = center
                if between is not None:
                    between()
            b = bank()
            used = [None] * len(sq)
            first = [(S.sem, S.sem.n), (V.sem, V.sem.n)] if sq_first else []
            for j in range(8):
                q = sq[j % len(sq)]
                t = act(q[:, 0:n], src[:, j, :], ACT.Square, xt[j], used[j % len(sq)], *first, OWN)
                t = mm(b, b.ap[:, 0:n], ones, q[:, 0:n], start=(j == 0), stop=(j == 7), waits=(t,), inc=True)
                used[j % len(sq)] = t
            t = act(rs[:, 0:n], b.ap[:, 0:n], ACT.Sqrt, t, bias=eps[:, 0:1], scale=1.0 / count)
            b.free(t)
            return recip(rs[:, 0:n], rs[:, 0:n], t)

        def apply_norm(src, dst, rs, n, g, bias=None, each=None):
            out_t = []
            t0 = (V.sem, V.sem.n)
            for j in range(8):
                t = stt(dst[:, j, :], src[:, j, :], g(j), rs[:, 0:n], ALU.mult, ALU.mult, t0, OWN)
                if bias is not None:
                    t = act(dst[:, j, :], dst[:, j, :], ACT.Identity, t, OWN, bias=bias(j))
                out_t.append(t)
                if each is not None and j:
                    each(j - 1, out_t[j - 1])
            if each is not None:
                each(7, t)
            return out_t

        sq = [tmp(512) for _ in range(4)]
        rs = tmp(512)
        rs2 = tmp(256)
        def modulate(src, hi, lo, rs, n, g, bias):
            out_t = []
            S.wait(x_read[0])
            t0 = (V.sem, V.sem.n)
            late = []
            for j in range(9):
                if j < 8:
                    t = stt(src[:, j, :], src[:, j, :], g(j), rs[:, 0:n], ALU.mult, ALU.mult, t0, OWN)
                    t = act(hi[:, j, :], src[:, j, :], ACT.Identity, t, OWN, bias=bias(j))
                    late.append(t)
                if j:
                    i, t = j - 1, late[j - 1]
                    out_t.append([t, stt(lo[:, i, :], src[:, i, :], bias(i), hi[:, i, :].bitcast(F32), ALU.add,
                                         ALU.subtract, t, OWN)])
            return out_t

        def split_x(src, g, toks, ks=range(8), out_=None):
            out_t = [None] * 8
            S.wait(x_read[0])
            for j in ks:
                if g is None:
                    hi, lo_ = (o[:, j, :] for o in (out_ or (xh, xl)))
                    t = act(hi, src[j], ACT.Copy, toks[j], OWN)
                    t2 = tt(lo_, src[j], hi.bitcast(F32), ALU.subtract, t, toks[j], OWN)
                else:
                    t = act(xh[:, j, :], src[:, j, :], ACT.Copy, toks[j], OWN, scale=g(j))
                    t2 = stt(xl[:, j, :], src[:, j, :], g(j), xh[:, j, :].bitcast(F32), ALU.mult, ALU.subtract, t,
                             toks[j], OWN)
                out_t[j] = [t, t2]
            return out_t

        norm_stats(h, t_h, sq, T, rs, center=mix, between=ada_block)
        ada_block()
        norm_stats(hc, t_hc, sq, TC, rs2, center=xc_ctx)
        t_mod = ada_block()
        S.wait(t_mod)
        ctxr = region("ctxr", 4096, F32R, lvl=1)
        ch = ctxr[:, 0:2048].rearrange("p (j t) -> p j t", j=8)
        cl = ctxr[:, 2048:4096].rearrange("p (j t) -> p j t", j=8)
        t_xn = modulate(mix, xh, xl, rs, T, lambda j: mod3[:, 8 + j, 0:1], lambda j: mod3[:, j, 0:1])
        t_xc = modulate(xc_ctx, ch, cl, rs2, TC, lambda j: mod3[:, 8 + j, 1:2], lambda j: mod3[:, j, 1:2])

        posf = tmp(4)
        ang = tmp(32)
        kk = tmp(32)
        rr = tmp(32)
        cosT, sinT = rope[:, 0:32], rope[:, 32:64]
        cp(posf, posi[:, :], t_pos)
        tt(ang.rearrange("p (c f) -> p c f", c=4), posf.unsqueeze(2).to_broadcast([128, 4, 8]),
           cc("freq", 8).unsqueeze(1).to_broadcast([128, 4, 8]), ALU.mult)
        for dst, shift, add in ((sinT, 0.0, 0.0), (cosT, 0.25, float(np.pi / 2))):
            ts(kk, ang, 1.0 / TWO_PI, shift, ALU.mult, ALU.add)
            ts(kk, kk, MAGIC, None, ALU.add, None)
            ts(kk, kk, MAGIC, None, ALU.subtract, None)
            stt(rr, kk, -C1, ang, ALU.mult, ALU.add)
            stt(rr, kk, -C2, rr, ALU.mult, ALU.add)
            stt(rr, kk, -C3, rr, ALU.mult, ALU.add)
            ts(rr, rr, add, 3.1415925, ALU.add, ALU.min)
            t = ts(rr, rr, -3.1415925, None, ALU.max, None)
            t = act(dst, rr, ACT.Sin, t)
            V.wait(t)
        f = fence()

        def product(s, hf, x2, n, toks, m=128, k0=0, kt=8, o=0, extra=(), ks=None):
            t_w = need(s, hf)
            b = bank()
            a = 128 * hf + o
            ks = list(ks or range(kt))
            for k in ks:
                w = ([t_w] if k == ks[0] else []) + ([toks[k0 + k]] if toks else []) + list(extra)
                t = mm3(b, b.ap[0:m, 0:n], (s.hi[:, k, a:a + m], s.lo[:, k, a:a + m]),
                        (x2[0][:, k, :], x2[1][:, k, :]), start=(k == ks[0]), stop=(k == ks[-1]), waits=w,
                        inc=(k == ks[-1]))
            if x2[0] is xh:
                x_read[0] = t
            return b, t

        def product_t(s, c, toks=None):
            t_w = [need(s, 0, 0), need(s, 1)]
            b = bank()
            for k in range(8):
                t = mm3(b, b.ap[:, 0:256], (xh[:, k, c * 128:c * 128 + 128], xl[:, k, c * 128:c * 128 + 128]),
                        (s.hi[:, k, :], s.lo[:, k, :]), start=(k == 0), stop=(k == 7),
                        waits=(t_w if k == 0 else []) + ([toks[k]] if toks else []), inc=(k == 7))
            x_read[0] = t
            return b, t

        reset(lo)
        Xt = tmp(2048 + 1024).rearrange("p (q n) -> p q n", q=6)
        Bt = tmp(1024 + 512).rearrange("p (q n) -> p q n", q=6)
        Z = tmp(2048).rearrange("p (q n) -> p q n", q=4)
        dtr, dta, dtb, wst, dt = [small[:, i * 96:i * 96 + 96] for i in range(5)]
        ex = small[:, 480:960]
        aneg = small[:, 960:976]
        BT = tmp(1024).rearrange("p (g t) -> p g t", g=2)
        CT = tmp(1024).rearrange("p (g t) -> p g t", g=2)
        acc = [tmp(512) for _ in range(4)]
        acc_free = [[] for _ in range(4)]
        nacc = [0]
        after_conv = arena_n[0]

        def xbc_unit(j, which):
            def unit():
                s = L_xbc[j // 2]
                x2, n, tk = ((xh, xl), T, t_xn) if which == 0 else ((ch, cl), TC, t_xc)
                b, t = product(s, j % 2, x2, n, tk)
                if which == 1 or j >= 6:
                    freed(s, j % 2, t)
                i = nacc[0] % 4
                nacc[0] += 1
                a, u = acc[i], b.ap
                t = act(a[:, 0:n], u[:, 0:n], ACT.Identity, t, *acc_free[i], OWN, bias=pc("ssd_conv_b", j),
                        scale=pc("ssd_conv_w", 8 + j))
                yield
                t = stt(a[:, 1:n], u[:, 0:n - 1], pc("ssd_conv_w", j), a[:, 1:n], ALU.mult, ALU.add, t, OWN)
                t = stt(a[:, 0:n - 1], u[:, 1:n], pc("ssd_conv_w", 16 + j), a[:, 0:n - 1], ALU.mult, ALU.add, t, OWN)
                b.free(t)
                yield
                if j >= 4 and which == 0:
                    dst = CT[:, j - 6, :] if j >= 6 else BT[:, j - 4, :]
                    t = act(dst, a, ACT.Silu, t, OWN)
                    acc_free[i] = [t]
                    if j >= 6:
                        return
                    a = dst
                else:
                    t = act(a[:, 0:n], a[:, 0:n], ACT.Silu, t, OWN)
                yield
                b = bank()
                for c in range(n // 128):
                    t2 = tr(b, b.ap[:, c * 128:c * 128 + 128], a[:, c * 128:c * 128 + 128], waits=(t,),
                            inc=(c == n // 128 - 1))
                if not (j >= 4 and which == 0):
                    acc_free[i] = [t2]
                qs = 2 if which == 0 else 0
                dst = Xt[:, qs:qs + n // 128, j * 128:j * 128 + 128] if j < 4 else \
                    Bt[:, qs:qs + n // 128, (j - 4) * 128:(j - 4) * 128 + 128]
                t = evac(dst, b.ap[:, 0:n].rearrange("p (c f) -> p c f", f=128), t2, OWN)
                b.free(t)
            return unit

        for _ in in_step([xbc_unit(j, which) for j in range(8) for which in ((0, 1) if j < 6 else (0,))]):
            pass
        dtw = [acc[i] for i in (0, 1)]
        for i, (x2, n) in enumerate((((ch, cl), TC), ((xh, xl), T))):
            b, t = product(L_dt, 0, x2, n, None, m=16)
            t_dw = cp(dtw[i][0:16, 0:n], b.ap[0:16, 0:n], t, *acc_free[i])
            b.free(t_dw)
            if i == 0:
                t_ctx_read = t
        freed(L_dt, 0, t)

        def softplus(dst, raw, e1, e2, sign):
            t = ts(e1, raw, -1.0, None, ALU.mult, None)
            tt(e1, e1, raw, ALU.min)
            ts(dst, raw, sign, 0.0, ALU.mult, ALU.max)
            t = act(e1, e1, ACT.Exp, (V.sem, V.sem.n))
            yield
            ts(e2, e1, 1.0, None, ALU.add, None, t)
            t = act(e2, e2, ACT.Ln, (V.sem, V.sem.n))
            yield
            tt(dst, dst, e2, ALU.add, t)
            ts(e2, e1, 1.0, None, ALU.add, None)
            ts(raw, e2, 1.0, None, ALU.subtract, None)
            tt(e1, e1, raw, ALU.subtract)
            recip(e2, e2)
            tt(e1, e1, e2, ALU.mult)
            tt(dst, dst, e1, ALU.add)

        dt3 = dt.rearrange("p (q w) -> p q w", q=6)
        ex4 = ex.rearrange("p (i q w) -> p i q w", i=5, q=6)
        w3 = wst.rearrange("p (q w) -> p q w", q=6)
        t_in = {}

        def dt_path():
            b = bank()
            for q in range(6):
                src, c = (dtw[0], q) if q < 2 else (dtw[1], q - 2)
                t = tr(b, b.ap[:, q * 16:q * 16 + 16], src[0:16, c * 128:c * 128 + 128], waits=(t_dw,), inc=(q == 5))
            acc_free[0] = acc_free[1] = [t]
            t = tt(dtr.rearrange("p (q w) -> p q w", q=6), b.ap[:, 0:96].rearrange("p (q w) -> p q w", q=6),
                   row("ssd_dt_bias", 0, 16).unsqueeze(1).to_broadcast([128, 6, 16]), ALU.add, t)
            b.free(t)
            yield from softplus(dt, dtr, dta, dtb, 1.0)
            t = act(aneg, row("ssd_a_log", 0, 16), ACT.Exp, t_rb)
            yield
            ts(aneg, aneg, -1.0, None, ALU.mult, None, t)
            t_in["a"] = t = tt(dta.rearrange("p (q w) -> p q w", q=6), dt3,
                               aneg.unsqueeze(1).to_broadcast([128, 6, 16]), ALU.mult)
            yield
            b = bank()
            for i, m in enumerate((ule, uge, cc("ugt"), cc("ult"), ones)):
                t = mm(b, b.ap[:, i * 96:i * 96 + 96], m, dta, waits=(t_in["a"],), inc=(i == 4))
            t_ex = act(ex, b.ap[:, 0:480], ACT.Exp, t)
            b.free(t_ex)
            yield
            tt(w3[:, :, 0:8], dt3[:, :, 0:8], ex4[:, 2, :, 0:8], ALU.mult, t_ex)
            tt(w3[:, :, 8:16], dt3[:, :, 8:16], ex4[:, 3, :, 8:16], ALU.mult)

        def z_unit(sl, c):
            def unit():
                s = L_z[sl]
                b, t = product_t(s, c)
                if c == 3:
                    freed(s, 0, t)
                    freed(s, 1, t)
                t_in["z"] = act(Z[:, c, sl * 256:sl * 256 + 256], b.ap[:, 0:256], ACT.Silu, t, OWN)
                b.free(t_in["z"])
                yield
            return unit

        fA = tmp(2048).rearrange("p (c i s f) -> p c i s f", c=4, i=2, s=2)
        fi = [tmp(512), tmp(512)]
        PW = 544
        close(1)
        arena2 = region("arena2", 4096, lvl=1)
        use(arena2, 4096)
        V.wait(t_ctx_read)
        pb = [tmp(2 * PW).rearrange("p (i t) -> p i t", i=2) for _ in range(3)]
        fill(pb[0][:, :, 0:16], 0.0)
        fill(pb[0][:, :, 528:544], 0.0)

        def fp_unit(n):
            def unit():
                s = L_fp[n // 2]
                b, t = product(s, n % 2, (xh, xl), T, None)
                freed(s, n % 2, t)
                if n < 2:
                    t = t_in[("f", n)] = act(fi[n], b.ap[:, :], ACT.Copy, t, OWN)
                else:
                    t = t_in[("p", n - 2)] = cp(pb[0][:, n - 2, 16:528], b.ap[:, :], t)
                b.free(t)
                yield
            return unit

        po = [mix[:, 6, :], mix[:, 7, :]]
        spec = [mix[:, 4, :], mix[:, 5, :]]

        def pool_path():
            while ("p", 1) not in t_in:
                yield
            P0, P1, P2 = pb
            V.wait(t_con1)
            iv = con1[:, 256:1280].rearrange("p (i t) -> p i t", i=2)
            tt(P1[:, :, 1:544], P0[:, :, 0:543], P0[:, :, 1:544], ALU.add)
            tt(P2[:, :, 2:543], P1[:, :, 1:542], P1[:, :, 3:544], ALU.add)
            yield
            tt(po[0][0:64, :], P1[0:64, 0, 16:528], iv[0:64, 0, :], ALU.mult)
            tt(po[0][64:128, :], P2[64:128, 0, 16:528], iv[64:128, 0, :], ALU.mult)
            tt(P1[:, 1, 4:541], P2[:, 1, 2:539], P2[:, 1, 6:543], ALU.add)
            tt(po[1][0:64, :], P1[0:64, 1, 16:528], iv[0:64, 1, :], ALU.mult)
            yield
            tt(P2[:, 1, 16:528], P1[:, 1, 12:524], P1[:, 1, 20:532], ALU.add)
            tt(po[1][64:128, :], P2[64:128, 1, 16:528], iv[64:128, 1, :], ALU.mult)
            tt(po[0], po[0], P0[:, 0, 16:528], ALU.subtract)
            t_in["po"] = tt(po[1], po[1], P0[:, 1, 16:528], ALU.subtract)

        def together(*live):
            while live:
                live = [g_ for g_ in live if next(g_, "end") != "end"]
                yield

        def feat_unit(c):
            def unit():
                b = bank()
                for i in range(2):
                    t = mm(b, b.ap[:, i * 256:i * 256 + 256], fi[i][:, c * 128:c * 128 + 128], con1[:, 0:256],
                           waits=(t_in[("f", 0)], t_in[("f", 1)], t_con1), inc=(i == 1))
                t_in[("A", c)] = act(fA[:, c].rearrange("p i s f -> p (i s f)"), b.ap[:, :], ACT.Copy, t, OWN)
                b.free(t_in[("A", c)])
                yield
            return unit

        def token_unit():
            bs = [bank(), bank()]
            for cs_ in range(2):
                s = raw(L_dft[cs_])
                for i in range(2):
                    for c in range(4):
                        t = mm(bs[i], bs[i].ap[:, :], fA[:, c, i, cs_, :], s.ap[:, c, :], start=(cs_ == 0 and c == 0),
                               stop=(cs_ == 1 and c == 3), waits=(s.tok, t_in[("A", c)]), inc=(c == 3))
                    if cs_ == 1:
                        t_in[("s", i)] = act(spec[i], bs[i].ap[:, :], ACT.Copy, t, OWN)
                        bs[i].free(t_in[("s", i)])
                done(s, t)
                yield

        def groups_unit(src, w, t_w, base, keys):
            def unit():
                for i in range(2):
                    b = bank()
                    for g in range(2):
                        t = mm(b, b.ap[g * 64:g * 64 + 64, :], w[g * 64:g * 64 + 64, i, :],
                               src[i][g * 64:g * 64 + 64, :], waits=(t_w, t_in[keys[i]]), inc=(g == 1))
                    if base == 4:
                        t = act(mix[:, 4 + i, :], b.ap[:, :], ACT.Copy, t, OWN)
                    else:
                        t = act(mix[:, 6 + i, :], b.ap[:, :], ACT.Copy, t, OWN, scale=pc("pool_scale", i))
                    b.free(t)
                    t_in[("m", base + i)] = t
                    yield
            return unit

        reset(0)
        Sf = tmp(2048).rearrange("p (q n) -> p q n", q=4)
        Sb = tmp(2048).rearrange("p (q n) -> p q n", q=4)
        Xs, Stmp = [acc[0], acc[1]], [acc[2], acc[3]]

        def v8(ap):
            return ap.rearrange("p (h d) -> p h d", h=8)

        def bc8(ap):
            return ap.unsqueeze(2).to_broadcast([128, 8, 64])

        t_st = {}

        def scan_path(d):
            order_, where = (((0, 1, 2, 3, 4), (0, 1, 2, 3)), ((1, 0, 5, 4, 3), (3, 2, 1, 0)))[d]
            St, cur = (Sf, Sb)[d], None
            x_free = [t for a_ in acc_free for t in a_]
            for n, q in enumerate(order_):
                t = tt(v8(Xs[d]), v8(Xt[:, q, :]), bc8(w3[:, q, d * 8:d * 8 + 8]), ALU.mult, *x_free, OWN)
                b = bank()
                for g in range(2):
                    t = mm(b, b.ap[:, g * 256:g * 256 + 256], Bt[:, q, g * 128:g * 128 + 128],
                           Xs[d][:, g * 256:g * 256 + 256], waits=(t,), inc=(g == 1))
                x_free = [t]
                if n:
                    dst = St[:, where[n - 1], :]
                    t_c = tt(v8(dst), v8(cur), bc8(ex4[:, 4, q, d * 8:d * 8 + 8]), ALU.mult, t_c, OWN)
                yield
                if n:
                    t_c = t_st[(d, where[n - 1])] = tt(dst, dst, b.ap[:, :], ALU.add, t, t_c, OWN)
                    cur = dst
                else:
                    t_c = cp(Stmp[d], b.ap[:, :], t, OWN)
                    cur = Stmp[d]
                b.free(t_c)
                yield

        use(arena, N1, after_conv)
        dmb, Ex, dmf = tmp(1024), tmp(1024), tmp(1024)
        Rf, Rb = Xt[:, 0:2, :].rearrange("p q n -> p (q n)"), Bt[:, 0:4, :].rearrange("p q n -> p (q n)")
        ssq = small[:, 984:1000]

        def v3(ap):
            return ap.rearrange("p (h l) -> p h l", h=8)

        def masks(m):
            return m.unsqueeze(1).to_broadcast([128, 8, 128])

        def cols(ap):
            return ap.unsqueeze(2).to_broadcast([128, 8, 128])

        R_free = [[]]
        M_free = [[]]
        t_mixc = []
        a3 = dta.rearrange("p (q w) -> p q w", q=6)

        def chunk_unit(c):
            def unit():
                q = c + 2
                tg1 = tt(v3(Rf), cols(a3[:, q, 0:8]), masks(ule), ALU.mult, *R_free[0], eng=G)
                tg2 = tt(v3(Rb), cols(a3[:, q, 8:16]), masks(uge), ALU.mult, eng=G)
                yield
                bs = []
                for half in range(2):
                    b = bank()
                    mm(b, b.ap[:, :], cc("ugt"), Rf[:, half * 512:half * 512 + 512], start=True, stop=False,
                       waits=(tg2,))
                    t = mm(b, b.ap[:, :], cc("ult"), Rb[:, half * 512:half * 512 + 512], start=False, stop=True,
                           inc=True)
                    bs.append((b, t))
                R_free[0] = [t]
                bg = bank()
                for g in range(2):
                    t_g = mm(bg, bg.ap[:, g * 128:g * 128 + 128], BT[:, g, c * 128:c * 128 + 128],
                             CT[:, g, c * 128:c * 128 + 128], inc=(g == 1))
                yield
                for half in range(2):
                    b, t = bs[half]
                    t_E = act(Ex[:, half * 512:half * 512 + 512], b.ap[:, :], ACT.Exp, t, *M_free[0], OWN)
                    b.free(t_E)
                tt(v3(dmf), cols(dt3[:, q, 0:8]), masks(ule), ALU.mult, *M_free[0])
                tt(v3(dmb), cols(dt3[:, q, 8:16]), masks(uge), ALU.mult)
                tt(dmf, dmf, dmb, ALU.add)
                yield
                tt(dmf, dmf, Ex, ALU.mult, t_E)
                for g in range(2):
                    t_M = tt(v3(dmf)[:, 4 * g:4 * g + 4, :], v3(dmf)[:, 4 * g:4 * g + 4, :],
                             bg.ap[:, g * 128:g * 128 + 128].unsqueeze(1).to_broadcast([128, 4, 128]), ALU.mult, t_g)
                bg.free(t_M)
                y = acc[c % 2]
                y1 = acc[3]
                tt(v8(y), v8(Xt[:, q, :]), bc8(row("ssd_d", 0, 8)), ALU.mult, t_rb)
                yield
                bf, bb = bank(), bank()
                for bx, St, d in ((bf, Sf, 0), (bb, Sb, 1)):
                    for g in range(2):
                        t_off = mm(bx, bx.ap[:, g * 256:g * 256 + 256], CT[:, g, c * 128:c * 128 + 128],
                                   St[:, c, g * 256:g * 256 + 256], inc=(g == 1))
                bd = bank()
                for hh in range(8):
                    t_d = mm(bd, bd.ap[:, hh * 64:hh * 64 + 64], dmf[:, hh * 128:hh * 128 + 128],
                             Xt[:, q, hh * 64:hh * 64 + 64], waits=(t_M,), inc=(hh == 7))
                M_free[0] = [t_d]
                yield
                tt(y, y, bd.ap[:, :], ALU.add, t_d)
                bd.free((V.sem, V.sem.n))
                tt(v8(y1), v8(bf.ap[:, :]), bc8(ex4[:, 0, q, 0:8]), ALU.mult, t_off)
                bf.free((V.sem, V.sem.n))
                tt(y, y, y1, ALU.add)
                tt(v8(y1), v8(bb.ap[:, :]), bc8(ex4[:, 1, q, 8:16]), ALU.mult)
                bb.free((V.sem, V.sem.n))
                tt(y, y, y1, ALU.add)
                t = tt(Z[:, c, :], y, Z[:, c, :], ALU.mult, t_in["z"])
                y = Z[:, c, :]
                for g in range(2):
                    act(acc[2][:, g * 256:g * 256 + 256], y[:, g * 256:g * 256 + 256], ACT.Square, t,
                        accum=ssq[:, 2 * c + g:2 * c + g + 1])
                r2 = ssq[:, 8 + 2 * c:10 + 2 * c]
                t = act(r2, ssq[:, 2 * c:2 * c + 2], ACT.Sqrt, bias=eps[:, 0:1], scale=1.0 / 256)
                yield
                recip(r2, r2, t)
                t = tt(y.rearrange("p (g n) -> p g n", g=2), y.rearrange("p (g n) -> p g n", g=2),
                       r2.unsqueeze(2).to_broadcast([128, 2, 256]), ALU.mult)
                yield
                b = bank()
                for j in range(4):
                    t2 = tr(b, b.ap[:, j * 128:j * 128 + 128], y[:, j * 128:j * 128 + 128], waits=(t,), inc=(j == 3))
                t = tt(mix[:, 0:4, c * 128:c * 128 + 128], b.ap[:, :].rearrange("p (j t) -> p j t", j=4),
                       pc("ssd_norm_w", 0, 4).unsqueeze(2).to_broadcast([128, 4, 128]), ALU.mult, t2)
                b.free(t)
                t_mixc.append(t)
            return unit

        def nothing():
            yield

        t_xn = [None] * 8

        def split_unit(j):
            def unit():
                t = act(xh[:, j, :], mix[:, j, :], ACT.Copy, t_in.get(("m", j)), *t_mixc, x_read[0], OWN)
                yield
                t_xn[j] = [t, tt(xl[:, j, :], mix[:, j, :], xh[:, j, :].bitcast(F32), ALU.subtract, t, OWN)]
            return unit

        def ssd_path():
            yield from dt_path()
            yield from pool_path()
            yield from together(scan_path(0), scan_path(1))
            while ("m", 5) not in t_in:
                yield
            for e_ in (V, G, S):
                e_.wait((E.sem, E.sem.n))
            yield from in_step([u for c in range(4) for u in (chunk_unit(c), nothing)])

        for _ in together(ssd_path(), in_step(
                [fp_unit(n) for n in (2, 3, 0, 1)] + [feat_unit(c) for c in range(4)]
                + [z_unit(0, c) for c in range(4)] + [token_unit, nothing, ada_unit]
                + [groups_unit(po, pw3, t_pw, 6, ["po", "po"]), groups_unit(spec, fw3, t_fw, 4, [("s", 0), ("s", 1)])]
                + [z_unit(1, c) for c in range(4)] + [ada_unit, nothing, split_unit(4), ada_unit, nothing,
                                                      split_unit(5), ada_unit, nothing, split_unit(6), ada_unit,
                                                      nothing, split_unit(7), ada_unit])):
            pass
        for _ in in_step([split_unit(j) for j in range(4)]):
            pass
        S.wait(t_modn[0])

        def project(L, x2, toks, evac_fn, kt=8, k0=0, ks=None):
            for j in range(8):
                s = L[j // 2]
                b, t = product(s, j % 2, x2, T, toks, k0=k0, kt=kt, ks=ks)
                freed(s, j % 2, t)
                evac_fn(j, b, t)

        toks = [None] * 8

        def scale_h(toks):
            return [S.do(lambda e, j=j: e.activation(h[:, j, :], h[:, j, :], ACT.Copy, scale=ALPHA), toks[j])
                    for j in range(8)]

        def residual(gcol):
            def fn(j, b, t):
                toks[j] = stt(h[:, j, :], b.ap[:, :], mod3[:, gcol + j, 0:1], h[:, j, :], ALU.mult, ALU.add, t,
                              toks[j])
                b.free(toks[j])
            return fn

        close(0)
        acts = region("acts", 16384, F32R)
        U = [[acts[:, (2 * u + v) * 4096:(2 * u + v + 1) * 4096].rearrange("p (j t) -> p j t", j=8)
              for v in range(2)] for u in range(2)]
        arena = region("arena_f", 2560)
        use(arena, 2560)
        sq = [tmp(512) for _ in range(2)]
        rs = tmp(512)
        arow[:] = [tmp(512), tmp(512)]
        acc = [mix[:, i, :] for i in range(8)]
        toks[:] = scale_h(t_h)
        add_out = residual(16)

        def out_fn(j, b, t):
            add_out(j, b, t)
            if j in (1, 5):
                ada_block()

        project(L_wout, (xh, xl), t_xn, out_fn, ks=LAST4)

        class Stream:

            def __init__(self, gname, l, sq, rs, into=None, free=None, squares=None):
                self.squares = squares
                self.into, self.free = into or (xh, xl), free
                self.g, self.l, self.sq, self.rs = gname, l, sq, rs
                self.used, self.late, self.bank, self.x = [None] * len(sq), [], bank(), [None] * 8

            def feed(self, j):
                i = j % len(self.sq)
                self.stat()
                if self.squares is G:
                    t = tt(self.sq[i], h[:, j, :], h[:, j, :], ALU.mult, toks[j], self.used[i], OWN, eng=G)
                else:
                    t = act(self.sq[i], h[:, j, :], ACT.Square, toks[j], self.used[i], OWN)
                self.late.append((j, i, t))
                hi, lo_ = (o[:, j, :] for o in self.into)
                t = act(hi, h[:, j, :], ACT.Copy, toks[j], self.free or x_read[0], OWN,
                        scale=pc(self.g, 8 * self.l + j))
                self.x[j] = [t, stt(lo_, h[:, j, :], pc(self.g, 8 * self.l + j), hi.bitcast(F32), ALU.mult,
                                    ALU.subtract, t, toks[j], OWN)]

            def stat(self):
                while self.late:
                    j, i, t = self.late.pop()
                    self.used[i] = mm(self.bank, self.bank.ap[:, :], ones, self.sq[i], start=(j == 0), stop=(j == 7),
                                      waits=(t,), inc=True)

            def end(self):
                self.stat()
                t = act(self.rs, self.bank.ap[:, :], ACT.Sqrt, self.used[7 % len(self.sq)], OWN, bias=eps[:, 0:1],
                        scale=1.0 / 1024)
                self.bank.free(t)
                return recip(self.rs, self.rs, t, OWN)

        def feeding(fn, st):
            def both(j, b, t):
                fn(j, b, t)
                st.feed(j)
            return both

        def post_norm(g, bb_, each=None):
            norm_stats(h, toks, sq, T, rs, center=mix)
            return apply_norm(mix, h, rs, T, lambda j: pc(g, j), lambda j: pc(bb_, j), each)

        t_h = post_norm("ln1_g", "ln1_b")
        norm_stats(h, t_h, sq, T, rs, center=mix)
        t_xn = modulate(mix, xh, xl, rs, T, lambda j: mod3[:, 32 + j, 0:1], lambda j: mod3[:, 24 + j, 0:1])
        toks[:] = scale_h([(V.sem, V.sem.n)] * 8)

        acc_free = [[(V.sem, V.sem.n)] for _ in range(8)]
        U_free = [[], []]
        U_tok = [[None] * 8, [None] * 8]
        na = [0]

        def grid(ap, dr, dc, src):
            v = ap.rearrange("p (r c) -> p r c", r=8)
            r0, r1 = max(0, -dr), min(8, 8 - dr)
            c0, c1 = max(0, -dc), min(64, 64 - dc)
            if src:
                return v[:, r0 + dr:r1 + dr, c0 + dc:c1 + dc]
            return v[:, r0:r1, c0:c1]

        def store_u(u, jl, src, *tk):
            t1 = act(U[u][0][:, jl, :], src, ACT.Copy, *tk, *U_free[u])
            t2 = tt(U[u][1][:, jl, :], src, U[u][0][:, jl, :].bitcast(F32), ALU.subtract, t1, *tk, *U_free[u], eng=G)
            U_tok[u][jl] = [t1, t2]
            return t2

        def up_tile(g, jl):
            j = sum(GR[:g]) + jl
            pair = L_up[g][jl // 2]
            got = []
            for s, col in ((pair[0], 22 + j), (pair[1], j)):
                b, t = product(s, jl % 2, (xh, xl), T, t_xn)
                freed(s, jl % 2, t)
                i = na[0] % 8
                na[0] += 1
                a = acc[i]
                t = act(a, b.ap[:, :], ACT.Identity, t, *acc_free[i], OWN, bias=pc("ffn_conv_b", col),
                        scale=pc("ffn_conv_w", 4 * 44 + col))
                got.append([i, a, t, b, col])
            for dr in (-1, 0, 1):
                for dc in (-1, 0, 1):
                    if dr == 0 and dc == 0:
                        continue
                    tap = (dr + 1) * 3 + dc + 1
                    for q in got:
                        o = grid(q[1], dr, dc, False)
                        q[2] = stt(o, grid(q[3].ap[:, :], dr, dc, True), pc("ffn_conv_w", tap * 44 + q[4]), o,
                                   ALU.mult, ALU.add, q[2], OWN)
            for q in got:
                q[3].free(q[2])
            return g, jl, got

        def up_end(g, jl, got):
            (ig, ga, tg, _, _), (iv_, va, tv, _, _) = got
            tg = act(ga, ga, ACT.Gelu_apprx_tanh, tg, OWN)
            t = tt(va, ga, va, ALU.mult, tg, tv, eng=G)
            acc_free[ig] = [t]
            t = store_u(g % 2, jl, va, t)
            acc_free[iv_] = [t]

        def up(g):
            late = None
            for jl in range(GR[g]):
                now = up_tile(g, jl)
                if late is not None:
                    up_end(*late)
                late = now
            up_end(*late)

        def down(L, g, kt, fn):
            project(L, U[g % 2], U_tok[g % 2], fn, kt=kt)
            U_free[g % 2] = [(E.sem, E.sem.n)]

        lo_eng[0] = G
        up(0)
        up(1)
        down(L_dn[0], 0, 8, residual(40))
        up(2)
        down(L_dn[1], 1, 8, residual(40))
        down(L_dn[2], 2, 6, residual(40))
        lo_eng[0] = None
        st = Stream("g_mix_2", 0, sq, small[:, 0:512], squares=G)

        def each(j, t):
            toks[j] = t
            st.feed(j)

        t_h = post_norm("ln2_g", "ln2_b", each)

        def rms(gname, l, t_h):
            return split_x(h, lambda j: pc(gname, 8 * l + j), t_h)

        def add_h(j, b, t):
            toks[j] = tt(h[:, j, :], h[:, j, :], b.ap[:, :], ALU.add, t, toks[j])
            b.free(toks[j])

        for l in range(2):
            Ln = L2[l]
            close(0)
            AM = 20600
            arena = region(f"arena_m{l}", AM)
            use(arena, AM)
            sq = [tmp(512) for _ in range(4)]
            rs = tmp(512)
            st8 = tmp(128)
            rsT = st8[:, 112:116]
            t_xn = st.x
            t_rs = st.end()
            early = [product_t(Ln.tok_[0], c, t_xn) for c in range(2)]
            rs_src = small[:, 0:512]
            cp(rs, rs_src, t_rs)
            b = bank()
            for c in range(4):
                t = tr(b, b.ap[:, c:c + 1], rs_src[0:1, c * 128:c * 128 + 128], waits=(t_rs,), inc=(c == 3))
            t_rsT = cp(rsT, b.ap[:, 0:4], t)
            b.free(t_rsT)
            S.wait(t_rsT)
            qt = tmp(2048).rearrange("p (c n) -> p c n", c=4)
            it = tmp(2048).rearrange("p (c n) -> p c n", c=4)
            ct = tmp(1024).rearrange("p (c n) -> p c n", c=4)
            ctT = tmp(1024).rearrange("p (k t) -> p k t", k=2)
            kt_t = tmp(1024)
            kt = kt_t.rearrange("p (c n) -> p c n", c=4)
            ikt = tmp(512).rearrange("p (c n) -> p c n", c=4)
            iw = tmp(32).rearrange("p (c n) -> p c n", c=4)
            vt = tmp(512).rearrange("p (c n) -> p c n", c=4)
            ro_t = tmp(1024)
            ro = [ro_t[:, i * 256:i * 256 + 256] for i in range(4)]
            mq = tmp(2048).rearrange("p (j t) -> p j t", j=4)
            mk = tmp(2048).rearrange("p (j t) -> p j t", j=4)
            mv_t, mo_t = tmp(2048), tmp(2048)
            mv = mv_t.rearrange("p (c n) -> p c n", c=4)
            mo = mo_t.rearrange("p (j t) -> p j t", j=4)
            fr, ir = sq[1], sq[2]
            spare = [small[:, 0:512], small[:, 512:1024]]
            ksrc = kt.rearrange("p c (v r d) -> p c v r d", v=2, r=2)
            rsI = st8[:, 116:120]
            t_rsI = ts(rsI, rsT, float(8 ** -0.5 * 64 ** -0.5), None, ALU.mult, None)
            S.wait(t_rsI)
            wq = mo_t.rearrange("p (s k n) -> p s k n", s=2, k=2)
            behind = [(e_.sem, e_.sem.n) for e_ in (V, G, E)]
            t_wq = [S.dma(s_wq, lambda e, src=src, dst=dst: e.dma_start(dst, src), *behind) for src, dst in (
                (A["w_iq_up_2"][l].rearrange("(k p) n -> p k n", p=128), wq[:, 0]),
                (A["w_q_up_2"][l].rearrange("(k p) n -> p k n", p=128), wq[:, 1]))]
            t_vt = []
            for n, s in enumerate(Ln.tok_):
                for c in range(4):
                    b, t = early[c] if n == 0 and c < 2 else product_t(s, c)
                    if c == 3:
                        freed(s, 0, t)
                        freed(s, 1, t)
                    rc = rsT[:, c:c + 1]
                    if n == 0:
                        t_ct = act(ct[:, c, :], b.ap[:, 0:256], ACT.Copy, t, OWN, scale=rc)
                        b.free(t_ct)
                    elif n == 1:
                        act(ksrc[:, c, :, 0, :], b.ap[:, 0:128].rearrange("p (v d) -> p v d", v=2), ACT.Copy, t,
                            OWN, scale=rc)
                        t_kt = act(vt[:, c, :], b.ap[:, 128:256], ACT.Copy, t, OWN, scale=rc)
                        b.free(t_kt)
                    else:
                        act(ikt[:, c, 0:64], b.ap[:, 0:64], ACT.Copy, t, OWN, scale=rc)
                        t_ik = act(iw[:, c, :], b.ap[:, 64:72], ACT.Copy, t, OWN, scale=rsI[:, c:c + 1])
                        b.free(t_ik)

            cfree = [None] * 4
            t_mk = [None] * 8
            t_mv = [None] * 4
            t_mo = [None] * 4
            scratch_read = [None, None]

            def mqk_unit(j):
                def unit():
                    s = Ln.mqk[j // 2]
                    b, t = product(s, j % 2, (xh, xl), T, None)
                    freed(s, j % 2, t)
                    i, i2 = (2 * j) % 4, (2 * j + 1) % 4
                    a, u = sq[i], sq[i2]
                    t = tt(u, b.ap[:, :], rs, ALU.mult, t, cfree[i2], OWN)
                    b.free(t)
                    yield
                    t = act(a, u, ACT.Identity, t, cfree[i], OWN, bias=pc("conv_b_2", 8 * l + j),
                            scale=pc("conv_w_2", 32 * l + 24 + j))
                    for sh in (3, 2, 1):
                        t = stt(a[:, sh:512], u[:, 0:512 - sh], pc("conv_w_2", 32 * l + (3 - sh) * 8 + j),
                                a[:, sh:512], ALU.mult, ALU.add, t, OWN)
                    cfree[i2] = t
                    yield
                    dst = mq[:, j, :] if j < 4 else mk[:, j - 4, :]
                    t_mk[j] = cfree[i] = act(dst, a, ACT.Silu, t, OWN)
                return unit

            def mv_unit(n, c):
                def unit():
                    s = Ln.mv[n]
                    b, t = product_t(s, c)
                    if c == 3:
                        freed(s, 0, t)
                        freed(s, 1, t)
                    t_mv[c] = act(mv[:, c, n * 256:n * 256 + 256], b.ap[:, 0:256], ACT.Copy, t, scratch_read[0], OWN,
                                  scale=rsT[:, c:c + 1])
                    b.free(t_mv[c])
                    got["mvs"] = n == 1 and c == 3
                    yield
                return unit

            def mo_unit(j):
                def unit():
                    s = Ln.mo[j // 2]
                    b, t = product(s, j % 2, (xh, xl), T, None)
                    freed(s, j % 2, t)
                    t = tt(mo[:, j, :], b.ap[:, :], rs, ALU.mult, t, scratch_read[1], OWN)
                    b.free(t)
                    yield
                    t_mo[j] = act(mo[:, j, :], mo[:, j, :], ACT.Sigmoid, t, OWN)
                return unit

            gate_t = [None, None]

            def gate_unit():
                for i, (o, dst, bcol) in enumerate(((0, ir, l), (4, fr, 2 + l))):
                    b, t = product(Ln.gate, 0, (xh, xl), T, None, m=4, o=o)
                    t2 = tt(dst[0:4, :], b.ap[0:4, :], rs[0:4, :], ALU.mult, t, *cfree, OWN)
                    b.free(t2)
                    gate_t[i] = ts(dst[0:4, :], dst[0:4, :], gb[0:4, bcol:bcol + 1], None, ALU.add, None, t_gb, t2,
                                   OWN)
                freed(Ln.gate, 0, t)
                got["gate"] = True
                yield

            i_flat = it.rearrange("p c n -> p (c n)")
            q_flat = qt.rearrange("p c n -> p (c n)")
            qT, iT = mix[:, 4:8, :], mix[:, 0:4, :]
            kT = [ct.rearrange("p c n -> p (c n)")[:, 0:512], ct.rearrange("p c n -> p (c n)")[:, 512:1024]]
            ikT = ctT[:, 0, :]
            k3 = ksrc[:, :, :, 0, :]
            ik3 = ikt[:, :, 0:64]
            got = {}
            qf = qt.rearrange("p c (n d) -> p (c n) d", n=8)

            def rope_on(src, nh, *tk):
                co = cosT.rearrange("p (c f) -> p c f", c=4).unsqueeze(2).to_broadcast([128, 4, nh, 8])
                si = sinT.rearrange("p (c f) -> p c f", c=4).unsqueeze(2).to_broadcast([128, 4, nh, 8])
                x1, x2 = src[:, :, :, 0:8], src[:, :, :, 8:16]
                r4 = [r_[:, 0:32 * nh].rearrange("p (c n f) -> p c n f", c=4, n=nh) for r_ in ro]
                t0 = [(V.sem, V.sem.n)] + list(tk)
                tt(r4[0], x1, co, ALU.mult, *t0, OWN)
                tt(r4[1], x2, si, ALU.mult, *t0, OWN)
                t2 = tt(r4[2], x2, co, ALU.mult, *t0, OWN)
                t4 = tt(r4[3], x1, si, ALU.mult, *t0, OWN)
                tt(x1, r4[0], r4[1], ALU.subtract, t4, OWN)
                return tt(x2, r4[2], r4[3], ALU.add, t4, OWN)

            def turned(src, j, dst, *tk):
                b = bank()
                for c in range(4):
                    t = tr(b, b.ap[:, c * 128:c * 128 + 128], src[:, c, j * 128:j * 128 + 128], waits=tk, inc=(c == 3))
                t = act(dst, b.ap[:, :], ACT.Copy, t, OWN)
                b.free(t)
                return t

            score = {1: i_flat[:, 1536:1792], 2: ctT[:, 1, 0:384], 3: ikt.rearrange("p c n -> p (c n)")}
            work = i_flat[:, 0:512]
            rl = [i_flat[:, 512:1024], i_flat[:, 1024:1536]]
            m8 = st8[:, 48:56]
            pens = {0: cc("pen")}
            t_pens = {0: None}

            att_list, path_done, index_read = [], [False], {}

            def queries():
                tt(qf, qf, st8[:, 0:32].unsqueeze(2).to_broadcast([128, 32, 64]), ALU.mult)
                tt(qf, qf, row("g_qn_2", 64 * l, 64).unsqueeze(1).to_broadcast([128, 32, 64]), ALU.mult)
                yield
                t = rope_on(qt.rearrange("p c (n d) -> p c n d", n=8), 8)
                for j in range(4):
                    turned(qt, j, qT[:, j, :], t)
                yield
                tt(k3, k3, st8[:, 32:40].rearrange("p (c v) -> p c v", c=4).unsqueeze(3).to_broadcast([128, 4, 2, 64]),
                   ALU.mult)
                tt(k3, k3, row("g_kn_2", 64 * l, 64).unsqueeze(1).unsqueeze(1).to_broadcast([128, 4, 2, 64]),
                   ALU.mult)
                rope_on(k3, 2)
                t = cp(ksrc[:, :, :, 1, :], k3)
                turned(kt, 0, kT[0], t)
                got["k"] = turned(kt, 1, kT[1], t)
                yield

            def main_path():
                sv = mv_t[:, 0:1024].rearrange("p (c n) -> p c n", c=4)
                t = act(sv, ct, ACT.Square, t_ct, OWN)
                t = reduce(st8[:, 0:4], sv, ALU.add, t)
                t = act(st8[:, 0:4], st8[:, 0:4], ACT.Sqrt, t, OWN, bias=eps[:, 0:1], scale=1.0 / 256)
                recip(st8[:, 0:4], st8[:, 0:4], t)
                t = tt(ct, ct, st8[:, 0:4].unsqueeze(2).to_broadcast([128, 4, 256]), ALU.mult)
                yield
                for k in range(2):
                    b = bank()
                    for c in range(4):
                        t2 = tr(b, b.ap[:, c * 128:c * 128 + 128], ct[:, c, k * 128:k * 128 + 128], waits=(t,),
                                inc=(c == 3))
                    t3 = ts(ctT[:, k, :], b.ap[:, :], pc("g_cq_2", 2 * l + k), None, ALU.mult, None, t2)
                    b.free(t3)
                t_c = t3
                yield
                for w, dst in ((0, it), (1, qt)):
                    for c in range(4):
                        b = bank()
                        for k in range(2):
                            t = mm(b, b.ap[:, :], ctT[:, k, c * 128:c * 128 + 128], wq[:, w, k, :], start=(k == 0),
                                   stop=(k == 1), waits=(*t_wq, t_c), inc=(k == 1))
                        t_e = act(dst[:, c, :], b.ap[:, :], ACT.Copy, t, OWN)
                        b.free(t_e)
                    got[w] = t_e
                    yield
                mo3 = mo_t.rearrange("p (n d) -> p n d", n=32)
                t = act(mo3, qf, ACT.Square, t, got[1], OWN)
                t1 = act(sv[:, :, 0:128].rearrange("p c (v d) -> p c v d", v=2), k3, ACT.Square, t_kt, OWN)
                t2 = act(sv[:, :, 128:192], ik3, ACT.Square, t_ik, OWN)
                reduce(st8[:, 0:32], mo3, ALU.add, t, OWN)
                scratch_read[1] = (V.sem, V.sem.n)
                reduce(st8[:, 32:40].rearrange("p (c v) -> p c v", c=4),
                       sv[:, :, 0:128].rearrange("p c (v d) -> p c v d", v=2), ALU.add, t1, OWN)
                t = reduce(st8[:, 40:44], sv[:, :, 128:192], ALU.add, t2, OWN)
                scratch_read[0] = t
                act(st8[:, 0:44], st8[:, 0:44], ACT.Sqrt, t, OWN, bias=eps[:, 0:1], scale=1.0 / 64)
                i4 = it.rearrange("p c (n d) -> p c n d", n=8)
                t_i = rope_on(i4, 8, got[0])
                yield
                recip(st8[:, 0:44], st8[:, 0:44], (S.sem, S.sem.n))
                tt(ik3, ik3, st8[:, 40:44].unsqueeze(2).to_broadcast([128, 4, 64]), ALU.mult)
                tt(ik3, ik3, row("g_ik_2", 64 * l, 64).unsqueeze(1).to_broadcast([128, 4, 64]), ALU.mult)
                rope_on(ik3.unsqueeze(2), 1)
                t_k = cp(ikt[:, :, 64:128], ik3)
                yield
                t_I = turned(ikt, 0, ikT, t_k)
                for j in range(4):
                    t_I = turned(it, j, iT[:, j, :], t_i)
                yield
                rl_free = [t_I, t_I]
                n = 0
                for c in (3, 2, 1):
                    W = 128 * (c + 1)
                    sc = score[c]

                    def index_mm(hh):
                        o = 64 * (hh % 2)
                        b = bank()
                        t = mm(b, b.ap[:, 0:W], iT[o:o + 64, hh // 2, c * 128:c * 128 + 128], ikT[o:o + 64, 0:W],
                               waits=(t_I,), inc=True)
                        return b, t

                    for h0 in range(0, 8, 2):
                        pair = [index_mm(h0), index_mm(h0 + 1)]
                        for hh in (h0, h0 + 1):
                            b, t = pair[hh - h0]
                            i = n % 2
                            n += 1
                            t = act(rl[i][:, 0:W], b.ap[:, 0:W], ACT.Relu, t, rl_free[i], OWN)
                            b.free(t)
                            if hh == 0:
                                t = ts(sc[:, 0:W], rl[i][:, 0:W], iw[:, c, 0:1], None, ALU.mult, None, t, t_I, OWN)
                            else:
                                t = stt(sc[:, 0:W], rl[i][:, 0:W], iw[:, c, hh:hh + 1], sc[:, 0:W], ALU.mult,
                                        ALU.add, t, ts_, OWN)
                            ts_ = t
                            rl_free[i] = t
                        yield
                    index_read[c] = (E.sem, E.sem.n)
                    t = tt(sc[:, W - 128:W], sc[:, W - 128:W], cc("neg"), ALU.add, ts_, OWN)
                    for r_ in range(16):
                        src = sc if r_ == 0 else work
                        t = top8(m8, src[:, 0:W], t, OWN)
                        yield
                        t = drop8(work[:, 0:W], m8, src[:, 0:W], t, OWN)
                        yield
                    t = tt(sc[:, 0:W], work[:, 0:W], sc[:, 0:W], ALU.is_equal, t, OWN)
                    t_pens[c] = ts(sc[:, 0:W], sc[:, 0:W], PEN, None, ALU.mult, None, t, OWN)
                    pens[c] = sc
                    if c == 3:
                        yield from queries()
                        att_list.extend([att_unit(0, hh) for hh in range(8)] + [att_end(0)])
                    att_list.extend([att_unit(c, hh) for hh in range(8)] + [att_end(c)])
                    yield
                path_done[0] = True

            def rows():
                yield from softplus(lg, f4, e4, e2r, -1.0)
                ts(lg, lg, -1.0, None, ALU.mult, None)
                fill(one, 1.0)
                scan(f4, one, lg, ALU.add)
                yield
                tt(i4r, i4r, f4, ALU.subtract)
                scan(mrow, one, i4r, ALU.max)
                t = tt(thr, f4, mrow, ALU.add)
                got["rows"] = act(thr, thr, ACT.Exp, t, scale=-1.0)
                yield
                b = bank()
                for c in range(4):
                    t2 = tr(b, b.ap[:, c * 4:c * 4 + 4], i4r[:, c * 128:c * 128 + 128], waits=(t,), inc=(c == 3))
                t2 = cp(aT, b.ap[:, 0:16], t2)
                b.free(t2)
                got["aT"] = t2
                yield

            lg, e2r = spare[0][0:4, :], spare[1][0:4, :]
            f4, i4r, e4, one = fr[0:4, :], ir[0:4, :], sq[3][0:4, :], sq[0][0:4, :]
            mrow, thr = e4, e2r
            aT = st8[:, 64:80]

            sm = [q_flat[:, k * 512:k * 512 + 512] for k in range(4)]
            PT, dg, bcs = [kt_t[:, 0:512], kt_t[:, 512:1024]], ro_t[:, 0:512], ro_t[:, 512:1024]
            sm_free, PT_free, misc_free = [None] * 4, [None] * 2, [None, None]
            bo = {}
            t_pv = {}
            t_exp = {}

            def att_unit(c, hh):
                def unit():
                    W = 128 * (c + 1)
                    n = 8 * c + hh
                    i, p = n % 4, n % 2
                    mx = st8[:, 80 + 8 * (c % 2) + hh:81 + 8 * (c % 2) + hh]
                    rsum = st8[:, 96 + 8 * (c % 2) + hh:97 + 8 * (c % 2) + hh]
                    o = 64 * (hh % 2)
                    b = bank()
                    t = mm(b, b.ap[:, 0:W], qT[o:o + 64, hh // 2, c * 128:c * 128 + 128], kT[hh // 4][o:o + 64, 0:W],
                           waits=(got["k"],), inc=True)
                    yield
                    t = ttr(sm[i][:, 0:W], b.ap[:, 0:W], pens[c][:, 0:W], 0.125, mx, ALU.add, ALU.max, t, sm_free[i],
                            t_pens[c], got["k"], OWN)
                    b.free(t)
                    t = ts(mx, mx, -1.0, None, ALU.mult, None, t, OWN)
                    yield
                    t = act(sm[i][:, 0:W], sm[i][:, 0:W], ACT.Exp, t, misc_free[0], OWN, bias=mx, accum=rsum)
                    t_exp[(c, hh)] = t
                    yield
                    b = bank()
                    for kb in range(c + 1):
                        t2 = tr(b, b.ap[:, kb * 128:kb * 128 + 128], sm[i][:, kb * 128:kb * 128 + 128], waits=(t,),
                                inc=(kb == c))
                    sm_free[i] = t2
                    t = act(PT[p][:, 0:W], b.ap[:, 0:W], ACT.Copy, t2, PT_free[p], OWN)
                    b.free(t)
                    yield
                    if hh == 0:
                        bo[c] = bank()
                    d = bo[c].ap[o:o + 64, (hh // 2) * 128:(hh // 2) * 128 + 128]
                    for kb in range(c + 1):
                        t2 = mm(bo[c], d, vt[:, kb, (hh // 4) * 64:(hh // 4) * 64 + 64],
                                PT[p][:, kb * 128:kb * 128 + 128], start=(kb == 0), stop=(kb == c), waits=(t,),
                                inc=(kb == c))
                    PT_free[p] = t2
                    t_pv[c] = t2
                return unit

            def att_end(c):
                def unit():
                    yield
                    yield
                    yield
                    rsum = st8[:, 96 + 8 * (c % 2):104 + 8 * (c % 2)]
                    t_r = recip(rsum, rsum, t_exp[(c, 7)], OWN)
                    for g in range(2):
                        b = bank()
                        t = tt(dg.rearrange("p (n q) -> p n q", n=4), ident.unsqueeze(1).to_broadcast([128, 4, 128]),
                               rsum[:, g:8:2].unsqueeze(2).to_broadcast([128, 4, 128]), ALU.mult, t_r, misc_free[1],
                               OWN)
                        t = mm(b, b.ap[:, :], ones, dg, waits=(t,), inc=True)
                        misc_free[1] = t
                        o = 64 * g
                        t = act(bcs[o:o + 64, :], b.ap[o:o + 64, :], ACT.Copy, t, got.get(("m", g)), OWN)
                        b.free(t)
                        t = tt(mix[o:o + 64, 0:4, c * 128:c * 128 + 128],
                               bo[c].ap[o:o + 64, :].rearrange("p (j q) -> p j q", j=4),
                               bcs[o:o + 64, :].rearrange("p (j q) -> p j q", j=4), ALU.mult, t, t_pv[c],
                               index_read.get(c), OWN)
                        got[("m", g)] = t
                    misc_free[0] = t
                    bo[c].free(t)
                return unit

            dm, Mb = [sq[1], sq[2], spare[0]], sq[0]
            dm_free, Mb_free = [None] * 3, [None]
            acc2 = {}

            def head_row(r_, hh):
                return ident[0:4, hh:hh + 1].to_broadcast([4, 128]), r_

            def sel(hh):
                return cc("sel", 16)[:, 4 * hh:4 * hh + 4]

            def ml_unit(hh, j):
                def unit():
                    W = 512 - 128 * j
                    i = (4 * hh + j) % 3
                    d = dm[i][:, 0:W]
                    if j == 0:
                        bm = bank()
                        t = mm(bm, bm.ap[:, :], *head_row(mrow, hh), waits=(got["rows"],), inc=True)
                        acc2["M"] = act(Mb, bm.ap[:, :], ACT.Copy, t, Mb_free[0], OWN)
                        bm.free(acc2["M"])
                    t = ts(d, Mb[:, 128 * j:512], aT[:, 4 * j + hh:4 * j + hh + 1], 0.0, ALU.subtract, ALU.max,
                           acc2["M"], got["aT"], dm_free[i], OWN, eng=G)
                    Mb_free[0] = t
                    yield
                    t = act(d, d, ACT.Exp, t, OWN, scale=-1.0)
                    bs_ = bank()
                    t_s = mm(bs_, bs_.ap[:, 0:W], mk[:, hh, j * 128:j * 128 + 128], mq[:, hh, 128 * j:512],
                             waits=(t_mk[hh], t_mk[4 + hh]), inc=True)
                    yield
                    t = stt(d, bs_.ap[:, 0:W], float(128 ** -0.5), d, ALU.mult, ALU.mult, t, t_s, OWN)
                    bs_.free(t)
                    t2 = tt(d[:, 0:128], d[:, 0:128], ule, ALU.mult, t, OWN, eng=G)
                    yield
                    if j == 0:
                        acc2[hh] = bank()
                        if hh == 0:
                            acc2["den"] = bank()
                    bn, bden = acc2[hh], acc2["den"]
                    mm(bden, bden.ap[0:4, 128 * j:512], sel(hh), d, start=(hh == 0 and j == 0),
                       stop=(hh == 3 and j == 3), waits=(t, t2))
                    t_n = mm(bn, bn.ap[:, 128 * j:512], mv[:, j, hh * 128:hh * 128 + 128], d, start=(j == 0),
                             stop=(j == 3), waits=(t_mv[j],), inc=True)
                    dm_free[i] = t_n
                    if j < 3:
                        return
                    yield
                    t = act(mq[:, hh, :], bn.ap[:, :], ACT.Square, t_n, OWN)
                    t2 = act(mk[:, hh, :], bn.ap[:, :], ACT.Copy, t_n, OWN, scale=pc("g_mh_2", 4 * l + hh))
                    bn.free(t2)
                    got[("h", hh)] = t
                    got[("o", hh)] = tt(mk[:, hh, :], mk[:, hh, :], mo[:, hh, :], ALU.mult, t2, t_mo[hh], OWN, eng=G)
                return unit

            def ml_end():
                bden = acc2["den"]
                dr, er_ = spare[0][0:4, :], sq[1][0:4, :]
                t_n = got[("h", 3)]
                t = act(dr, bden.ap[0:4, :], ACT.Abs, t_n, *dm_free, OWN)
                bden.free(t)
                t = tt(dr, dr, thr, ALU.max, t, got["rows"], OWN)
                b = bank()
                for hh in range(4):
                    t2 = mm(b, b.ap[0:4, :], sel(hh), mq[:, hh, :], start=(hh == 0), stop=(hh == 3),
                            waits=(got[("h", hh)],), inc=(hh == 3))
                yield
                t = recip(dr, dr, t, OWN)
                yield
                t = tt(er_, b.ap[0:4, :], dr, ALU.mult, t, t2, *dm_free, OWN)
                b.free(t)
                t = tt(er_, er_, dr, ALU.mult, t, OWN)
                t = act(er_, er_, ACT.Sqrt, t, OWN, bias=eps[0:4, 0:1], scale=1.0 / 128)
                yield
                t = recip(er_, er_, t, OWN)
                t_e = tt(er_, er_, dr, ALU.mult, t, OWN)
                yield
                for hh in range(4):
                    b = bank()
                    t = mm(b, b.ap[:, :], *head_row(er_, hh), waits=(t_e,), inc=True)
                    t = tt(mk[:, hh, :], mk[:, hh, :], b.ap[:, :], ALU.mult, t, got[("o", hh)], OWN)
                    b.free(t)
                    got[("mix", hh)] = t
                    yield

            mv_units = [mv_unit(n, c) for n in range(2) for c in range(4)]
            units = [mqk_unit(j) for j in range(8)] + mv_units[0:4] + [gate_unit] + mv_units[4:8] \
                + [mo_unit(j) for j in range(4)]
            path, fill_ = main_path(), in_step(units)
            att = in_step(att_list, lambda: not path_done[0])

            def recurrence():
                while "gate" not in got:
                    yield
                yield from rows()
                while not got["mvs"]:
                    yield
                yield from in_step([ml_unit(hh, j) for hh in range(4) for j in range(4)])
                yield from ml_end()

            mls = recurrence()
            going = {"path": True, "fill": True, "att": True, "mls": True}
            step = 0

            due = {"path": 0.0, "fill": 0.0, "att": 0.0, "mls": 0.0}

            def move(name, gen, n=1.0):
                due[name] += n if going["path"] else 1.0
                while due[name] >= 1.0:
                    due[name] -= 1.0
                    if going[name]:
                        going[name] = next(gen, "end") != "end"

            while any(going.values()):
                step += 1
                move("path", path)
                move("fill", fill_, 0.6)
                move("att", att, 0.35)
                move("mls", mls, 0.25)
            t_last = (V.sem, V.sem.n)
            t_heads = [got[("mix", hh)] for hh in range(4)]
            close(0)
            arena = region(f"arena_f{l}", 1536)
            use(arena, 1536)
            sq = [tmp(512) for _ in range(2)]
            rs = tmp(512)
            acts = [region(f"acts{l}{u}", 8192, F32R, lvl=u) for u in range(2)]
            U = [[acts[u][:, v * 4096:(v + 1) * 4096].rearrange("p (j t) -> p j t", j=8)
                  for v in range(2)] for u in range(2)]
            for e_ in (V, S):
                e_.wait((E.sem, E.sem.n), (G.sem, G.sem.n))
            t_xn = split_x([mix[:, j, :] for j in range(4)] + [mk[:, j, :] for j in range(4)], None,
                           [t_last] * 4 + t_heads, LAST4, out_=U[0])
            uu = [mix[:, i, :] for i in range(4)]
            toks[:] = t_h
            st = Stream("g_mlp_2", l, sq, rs)
            project(Ln.wout, U[0], t_xn, feeding(add_h, st), ks=LAST4)
            t_xn = st.x
            rs_of = [None]
            U_free = [[(E.sem, E.sem.n)], []]
            U_tok = [[None] * 8, [None] * 8]
            ufree = [[(V.sem, V.sem.n), (S.sem, S.sem.n)] for _ in range(4)]
            nu = [0]

            def ff_up(g):
                for jl in range(8):
                    s = Ln.up[g][jl // 2]
                    b, t = product(s, jl % 2, (xh, xl), T, t_xn)
                    freed(s, jl % 2, t)
                    if rs_of[0] is None:
                        rs_of[0] = st.end()
                    i = nu[0] % 4
                    nu[0] += 1
                    t = stt(uu[i], b.ap[:, :], 0.0, rs, ALU.max, ALU.mult, t, rs_of[0], *ufree[i])
                    b.free(t)
                    t1 = act(U[g % 2][0][:, jl, :], uu[i], ACT.Square, t, *U_free[g % 2])
                    t2 = tt(uu[i], uu[i], uu[i], ALU.mult, t1)
                    t2 = tt(U[g % 2][1][:, jl, :], uu[i], U[g % 2][0][:, jl, :].bitcast(F32), ALU.subtract, t2, t1,
                            *U_free[g % 2])
                    U_tok[g % 2][jl] = [t1, t2]
                    ufree[i] = [t2]

            lo_eng[0] = G
            ff_up(0)
            ff_up(1)
            down(Ln.dn[0], 0, 8, add_h)
            ff_up(2)
            down(Ln.dn[1], 1, 8, add_h)
            ff_up(3)
            down(Ln.dn[2], 2, 8, add_h)
            st = Stream("g_ple_2", l, sq, rs, U[0], U_free[0])
            down(Ln.dn[3], 3, 8, feeding(add_h, st))
            lo_eng[0] = None

            t_xn = st.x
            close(1)
            arena = region(f"arena_p{l}", 7168, lvl=1)
            use(arena, 7168)
            f = [(e_.sem, e_.sem.n) for e_ in (V, S, G, E)]
            pst = tmp(1024).rearrange("p (c d) -> p c d", c=4)
            pT = tmp(1024).rearrange("p (k t) -> p k t", k=2)
            pw_ = tmp(4096).rearrange("p (j t) -> p j t", j=8)
            gates = tmp(1024).rearrange("p (j t) -> p j t", j=2)
            t_p = S.dma(s_p, lambda e, l=l, pst=pst: e.dma_start(
                pst, A["p_2"][l].rearrange("a (c p) d -> p (a c) d", p=128)), *f)
            for k in range(2):
                b = bank()
                for c in range(4):
                    t = tr(b, b.ap[:, c * 128:c * 128 + 128], pst[:, c, k * 128:k * 128 + 128], waits=(t_p,),
                           inc=(c == 3))
                t_pT = evac(pT[:, k, :], b.ap[:, :], t)
                b.free(t_pT)
                E.wait(t_pT)
            t_rs = st.end()
            raw(Ln.ple)
            t_pw = []
            for j in range(8):
                b = bank()
                for k in range(2):
                    t = mm(b, b.ap[:, :], Ln.ple.ap[:, k, j * 128:j * 128 + 128], pT[:, k, :], start=(k == 0),
                           stop=(k == 1), waits=(Ln.ple.tok,), inc=(k == 1))
                t2 = evac(pw_[:, j, :], b.ap[:, :], t)
                b.free(t2)
                t_pw.append(t2)
            done(Ln.ple, t)
            gfree = [[], []]

            def gate_fn(j, b, t):
                g = gates[:, j % 2, :]
                t = tt(g, b.ap[:, :], rs, ALU.mult, t, t_rs, *gfree[j % 2])
                b.free(t)
                t = act(g, g, ACT.Sigmoid, t, bias=pc("b_ple_gate_2", 8 * l + j))
                t = tt(g, g, pw_[:, j, :], ALU.mult, t, t_pw[j])
                toks[j] = tt(h[:, j, :], h[:, j, :], g, ALU.add)
                gfree[j % 2] = [toks[j]]

            if l == 0:
                st = Stream("g_mix_2", 1, sq, small[:, 0:512])
                project(Ln.pg, U[0], t_xn, feeding(gate_fn, st))
            else:
                project(Ln.pg, U[0], t_xn, gate_fn)
            t_h = list(toks)

        ot = mix_t[:, :].rearrange("p (c d) -> p c d", c=4)
        for c in range(4):
            for jj in range(2):
                b = bank()
                for q in range(4):
                    j = 4 * jj + q
                    t = tr(b, b.ap[:, q * 128:q * 128 + 128], h[:, j, c * 128:c * 128 + 128], waits=(t_h[j],),
                           inc=(q == 3))
                t = evac(ot[:, c, jj * 512:jj * 512 + 512], b.ap[:, :], t)
                b.free(t)
                D.wait(t)
            t_out = D.dma(s_out, lambda e, c=c: e.dma_start(out[0, c * 128:c * 128 + 128, :], ot[:, c, :]))
        D.wait(t_out)

        block = ctx.enter_context(nc.Block())

        @block.sync
        def _(eng):
            D.play(eng)

        @block.gpsimd
        def _(eng):
            G.play(eng)

        @block.scalar
        def _(eng):
            S.play(eng)

        @block.tensor
        def _(eng):
            E.play(eng)

        @block.vector
        def _(eng):
            V.play(eng)


_INS = ["x", "c", "ctx", "c_ctx", "w_ada", "b_ada", "w_in", "ssd_conv_w", "ssd_conv_b", "ssd_dt_bias", "ssd_a_log",
        "ssd_d", "ssd_norm_w", "fnet_w", "pool_w", "pool_scale", "w_out", "ln1_g", "ln1_b", "ffn_w_up", "ffn_conv_w",
        "ffn_conv_b", "ffn_w_down", "ln2_g", "ln2_b", "p_2", "positions_2", "g_mix_2", "w_in_2", "g_cq_2",
        "w_q_up_2", "w_iq_up_2", "g_qn_2", "g_kn_2", "g_ik_2", "conv_w_2", "conv_b_2", "i_bias_2", "f_bias_2",
        "g_mh_2", "w_out_2", "g_mlp_2", "w_ff1_2", "w_ff2_2", "g_ple_2", "w_ple_gate_2", "b_ple_gate_2", "w_ple_2"]
_FLAT = {1: "", 2: "a b -> (a b)", 3: "a b c -> (a b c)", 4: "a b c d -> (a b c d)"}


def kernel(**inputs):
    import concourse.bacc as _bacc
    from concourse.bass_utils import run_bass_kernel_spmd as _run

    nc = _bacc.Bacc("TRN2", target_bir_lowering=False, num_devices=1)
    arrays, A = {}, {"_flat": {}}
    for name in _INS:
        a = np.ascontiguousarray(inputs[name])
        arrays[f"in_{name}_dram"] = a
        A[name] = nc.dram_tensor(f"in_{name}_dram", a.shape, mybir.dt.from_np(a.dtype), kind="ExternalInput").ap()
        A["_flat"][name] = _FLAT[a.ndim]
    for name, a in const_arrays().items():
        arrays[f"in_{name}_dram"] = a
        A[name] = nc.dram_tensor(f"in_{name}_dram", a.shape, F32, kind="ExternalInput").ap()
    out = nc.dram_tensor("out_0_dram", (1, T, 1024), F32, kind="ExternalOutput").ap()
    build(nc, A, out)
    r = _run(nc, [arrays], core_ids=[0])
    return r.results[0]["out_0_dram"]
```
